# Optimizing a Trainium2 kernel written in Bass

```python
import jax, jax.numpy as jnp
from jax import lax
import numpy as np
import math

D_MODEL = 1024
BATCH = 1
SEQ = 256
DEPTH = 2

POOL_WINDOWS = (2, 4, 8, 16)
POOL_GROUP = 64
POOL_WIDTH = POOL_GROUP * len(POOL_WINDOWS)
ATTN_HEADS = 4
ATTN_HEAD_DIM = 64
ATTN_WIDTH = ATTN_HEADS * ATTN_HEAD_DIM
IDX_HEADS = 8
IDX_DIM = 64
TOPK_MAX = 256
Q_BLOCK = 128
HGRN_HEADS = 4
HGRN_EXPAND = 128
HGRN_HEAD_V = 128
HGRN_KW = HGRN_HEADS * HGRN_EXPAND
HGRN_VW = HGRN_HEADS * HGRN_HEAD_V
HGRN_CHUNK = 64
KEY_MAX = 1.0 - 1e-6
REL_BUCKETS = 32
REL_MAX_DIST = 128
D_FF = 2816
N_SUB = 3
DN_ALPHA = (2 * DEPTH) ** 0.25
DN_BETA = (8 * DEPTH) ** -0.25
LN_EPS = 1e-5
RMS_EPS = 1e-6

MIX_WIDTH = POOL_WIDTH + ATTN_WIDTH + HGRN_VW
MIX_IN_WIDTHS = (POOL_WIDTH, ATTN_WIDTH, ATTN_WIDTH, ATTN_WIDTH, IDX_HEADS * IDX_DIM, IDX_DIM, IDX_HEADS,
                 HGRN_KW, HGRN_KW, HGRN_VW, HGRN_VW, 3 * D_MODEL)
MIX_IN_WIDTH = sum(MIX_IN_WIDTHS)
MIX_SPLITS = tuple(int(s) for s in np.cumsum(MIX_IN_WIDTHS)[:-1])


def layer_norm(x, g, b):
    x32 = x.astype(jnp.float32)
    mu = jnp.mean(x32, axis=-1, keepdims=True)
    var = jnp.mean(jnp.square(x32 - mu), axis=-1, keepdims=True)
    y = (x32 - mu) * lax.rsqrt(var + LN_EPS)
    return (y * g.astype(jnp.float32) + b.astype(jnp.float32)).astype(x.dtype)

def swiglu(h, w_in, w_out):
    gate, up = jnp.split(h @ w_in, 2, axis=-1)
    return (jax.nn.silu(gate) * up) @ w_out

def modulate(h, mod, j):
    return h * (1 + mod[:, j, 1][:, None, :]) + mod[:, j, 0][:, None, :]

def sub_gate(mod, j):
    return 1 + mod[:, j, 2][:, None, :]

def pool_mixer(a, pool_w, pool_scale):
    B, S, _ = a.shape
    a32 = a.astype(jnp.float32)
    P = jnp.pad(jnp.cumsum(a32, axis=1), ((0, 0), (1, 0), (0, 0)))
    pos1 = jnp.arange(1, S + 1)
    means = []
    for g, w in enumerate(POOL_WINDOWS):
        Pg = P[..., g * POOL_GROUP:(g + 1) * POOL_GROUP]
        lead = Pg[:, 1:]
        lag = jnp.concatenate([jnp.zeros_like(Pg[:, :w - 1]), Pg[:, :S + 1 - w]], axis=1)
        cnt = jnp.minimum(pos1, w).astype(jnp.float32)
        means.append((lead - lag) / cnt[None, :, None])
    pooled = jnp.stack(means, axis=2)
    d = (pooled - a32.reshape(B, S, len(POOL_WINDOWS), POOL_GROUP)).astype(a.dtype)
    y = jnp.einsum('bsgc,gcd->bsgd', d, pool_w)
    return y.reshape(B, S, POOL_WIDTH) * pool_scale

def t5_bucket(dist):
    max_exact = REL_BUCKETS // 2
    d32 = jnp.maximum(dist, 1).astype(jnp.float32)
    large = max_exact + (jnp.log(d32 / max_exact) / np.log(REL_MAX_DIST / max_exact)
                         * (REL_BUCKETS - max_exact)).astype(jnp.int32)
    large = jnp.minimum(large, REL_BUCKETS - 1)
    return jnp.where(dist < max_exact, dist, large)

def sparse_attention(q, k, v, q_idx, k_idx, w_idx, rel_bias):
    B, S, H, dh = q.shape
    top_k = min(TOPK_MAX, S // 4)
    n_blocks = S // Q_BLOCK
    scale = dh ** -0.5
    idx_scale = (IDX_DIM ** -0.5) * (IDX_HEADS ** -0.5)
    key_pos = jnp.arange(S)

    def block(i):
        q0 = i * Q_BLOCK
        qb = lax.dynamic_slice_in_dim(q, q0, Q_BLOCK, axis=1)
        qib = lax.dynamic_slice_in_dim(q_idx, q0, Q_BLOCK, axis=1)
        wb = lax.dynamic_slice_in_dim(w_idx, q0, Q_BLOCK, axis=1)
        qpos = q0 + jnp.arange(Q_BLOCK)
        logit_idx = jnp.einsum('bqhd,bsd->bqhs', qib, k_idx)
        score = jnp.einsum('bqh,bqhs->bqs', wb, jax.nn.relu(logit_idx)).astype(jnp.float32) * idx_scale
        causal = key_pos[None, :] <= qpos[:, None]
        score = jnp.where(causal[None], score, -jnp.inf)
        _, sel = lax.top_k(score, top_k)
        k_sel = jax.vmap(lambda kk, ii: kk[ii])(k, sel)
        v_sel = jax.vmap(lambda vv, ii: vv[ii])(v, sel)
        logits = jnp.einsum('bqhd,bqkhd->bhqk', qb, k_sel).astype(jnp.float32) * scale
        dist = qpos[None, :, None] - sel
        bias = rel_bias[t5_bucket(jnp.maximum(dist, 0))].astype(jnp.float32)
        logits = logits + jnp.transpose(bias, (0, 3, 1, 2))
        logits = jnp.where((dist >= 0)[:, None], logits, -jnp.inf)
        p = jax.nn.softmax(logits, axis=-1).astype(v.dtype)
        return jnp.einsum('bhqk,bqkhd->bqhd', p, v_sel)

    out = lax.map(block, jnp.arange(n_blocks))
    return jnp.transpose(out, (1, 0, 2, 3, 4)).reshape(B, S, H * dh)

def hgrn2(q, f_logit, i_val, g_out, lb, norm_g):
    B, S, _ = q.shape
    C = HGRN_CHUNK
    NC = S // C
    z = f_logit.astype(jnp.float32)
    lb = lb.astype(jnp.float32)
    key = (1 - lb) * jax.nn.sigmoid(-z)
    log_f = jnp.log1p(-jnp.minimum(key, KEY_MAX))
    qf = jax.nn.silu(q.astype(jnp.float32))

    def to_chunks(t, d):
        return jnp.transpose(t.reshape(B, NC, C, HGRN_HEADS, d), (1, 0, 3, 2, 4))

    qc = to_chunks(qf, HGRN_EXPAND)
    kc = to_chunks(key, HGRN_EXPAND)
    gc = to_chunks(log_f, HGRN_EXPAND)
    vc = to_chunks(i_val.astype(jnp.float32), HGRN_HEAD_V)
    tri = jnp.tril(jnp.ones((C, C), dtype=bool))

    def step(state, inp):
        qq, kk, vv, gg = inp
        A = jnp.cumsum(gg, axis=2)
        o_inter = jnp.einsum('bhtd,bhdv->bhtv', qq * jnp.exp(A), state)
        diff = A[:, :, :, None, :] - A[:, :, None, :, :]
        decay = jnp.exp(jnp.where(tri[None, None, :, :, None], diff, -jnp.inf))
        scores = jnp.einsum('bhtd,bhsd,bhtsd->bhts', qq, kk, decay)
        o_intra = jnp.einsum('bhts,bhsv->bhtv', scores, vv)
        k_dec = kk * jnp.exp(A[:, :, -1:, :] - A)
        new_state = jnp.exp(A[:, :, -1, :])[..., None] * state + jnp.einsum('bhsd,bhsv->bhdv', k_dec, vv)
        return new_state, o_inter + o_intra

    s0 = jnp.zeros((B, HGRN_HEADS, HGRN_EXPAND, HGRN_HEAD_V), jnp.float32)
    _, o = lax.scan(step, s0, (qc, kc, vc, gc))
    o = jnp.transpose(o, (1, 0, 3, 2, 4)).reshape(B, S, HGRN_HEADS, HGRN_HEAD_V)
    o = o * lax.rsqrt(jnp.mean(jnp.square(o), axis=-1, keepdims=True) + RMS_EPS)
    o = o.reshape(B, S, HGRN_VW).astype(q.dtype)
    return o * norm_g * jax.nn.silu(g_out)

def token_mixer(h, w_in, pool_w, pool_scale, rel_bias, lb, norm_g, w_branch, w_out):
    B, S, _ = h.shape
    proj = h @ w_in
    (a, q, k, v, qi, ki, wi, hq, hf, hi, hg, gates) = jnp.split(proj, MIX_SPLITS, axis=-1)
    y_a = pool_mixer(a, pool_w, pool_scale)
    y_b = sparse_attention(q.reshape(B, S, ATTN_HEADS, ATTN_HEAD_DIM),
                           k.reshape(B, S, ATTN_HEADS, ATTN_HEAD_DIM),
                           v.reshape(B, S, ATTN_HEADS, ATTN_HEAD_DIM),
                           qi.reshape(B, S, IDX_HEADS, IDX_DIM), ki, wi, rel_bias)
    y_c = hgrn2(hq, hf, hi, hg, lb, norm_g)
    g = jax.nn.sigmoid(gates.reshape(B, S, 3, D_MODEL))
    merged = (g[:, :, 0] * (y_a @ w_branch[:POOL_WIDTH])
              + g[:, :, 1] * (y_b @ w_branch[POOL_WIDTH:POOL_WIDTH + ATTN_WIDTH])
              + g[:, :, 2] * (y_c @ w_branch[POOL_WIDTH + ATTN_WIDTH:]))
    return merged @ w_out

def first_inputs(seed: int = 0) -> dict:
    key = jax.random.key(seed)
    ks = jax.random.split(key, 16)
    f32 = jnp.float32

    def n(k, shape):
        return jax.random.normal(k, shape, f32)

    x = n(ks[0], (BATCH, SEQ, D_MODEL))
    c = n(ks[1], (BATCH, D_MODEL))
    w_ada = n(ks[2], (DEPTH, D_MODEL, N_SUB * 3 * D_MODEL)) * (0.3 * D_MODEL ** -0.5)
    b_ada = 0.01 * n(ks[3], (DEPTH, N_SUB * 3 * D_MODEL))
    ln_g = 1.0 + 0.02 * n(ks[4], (DEPTH, N_SUB, D_MODEL))
    ln_b = 0.02 * n(ks[5], (DEPTH, N_SUB, D_MODEL))
    ffn_w_in = n(ks[6], (DEPTH, 2, D_MODEL, 2 * D_FF)) * D_MODEL ** -0.5
    ffn_w_out = n(ks[7], (DEPTH, 2, D_FF, D_MODEL)) * (DN_BETA * D_FF ** -0.5)
    mix_w_in = n(ks[8], (DEPTH, D_MODEL, MIX_IN_WIDTH)) * D_MODEL ** -0.5
    pool_w = n(ks[9], (DEPTH, len(POOL_WINDOWS), POOL_GROUP, POOL_GROUP)) * POOL_GROUP ** -0.5
    pool_scale = 1.0 + 0.02 * n(ks[10], (DEPTH, POOL_WIDTH))
    rel_bias = 0.5 * n(ks[11], (REL_BUCKETS, ATTN_HEADS))
    hgrn_lb = 1.0 + 0.1 * n(ks[12], (DEPTH, HGRN_KW))
    hgrn_norm_g = 1.0 + 0.02 * n(ks[13], (DEPTH, HGRN_VW))
    row_scale = jnp.concatenate([jnp.full((POOL_WIDTH,), POOL_WIDTH ** -0.5, f32),
                                 jnp.full((ATTN_WIDTH,), ATTN_WIDTH ** -0.5, f32),
                                 jnp.full((HGRN_VW,), HGRN_VW ** -0.5, f32)])
    w_branch = n(ks[14], (DEPTH, MIX_WIDTH, D_MODEL)) * row_scale[None, :, None]
    w_out = n(ks[15], (DEPTH, D_MODEL, D_MODEL)) * (DN_BETA * D_MODEL ** -0.5)
    return {'x': x, 'c': c, 'w_ada': w_ada, 'b_ada': b_ada, 'ln_g': ln_g, 'ln_b': ln_b,
            'ffn_w_in': ffn_w_in, 'ffn_w_out': ffn_w_out, 'mix_w_in': mix_w_in,
            'pool_w': pool_w, 'pool_scale': pool_scale, 'rel_bias': rel_bias,
            'hgrn_lb': hgrn_lb, 'hgrn_norm_g': hgrn_norm_g, 'w_branch': w_branch, 'w_out': w_out}

def first_block(x, c, w_ada, b_ada, ln_g, ln_b, ffn_w_in, ffn_w_out, mix_w_in, pool_w, pool_scale,
              rel_bias, hgrn_lb, hgrn_norm_g, w_branch, w_out):
    B = x.shape[0]
    lb_sm = jax.nn.softmax(hgrn_lb.astype(jnp.float32), axis=0)
    lbs = jnp.cumsum(lb_sm, axis=0) - lb_sm[0:1]
    cond = jax.nn.silu(c)
    for l in range(DEPTH):
        mod = (cond @ w_ada[l] + b_ada[l]).reshape(B, N_SUB, 3, D_MODEL)
        y = swiglu(modulate(x, mod, 0), ffn_w_in[l, 0], ffn_w_out[l, 0])
        x = layer_norm(DN_ALPHA * x + 0.5 * sub_gate(mod, 0) * y, ln_g[l, 0], ln_b[l, 0])
        y = token_mixer(modulate(x, mod, 1), mix_w_in[l], pool_w[l], pool_scale[l], rel_bias,
                        lbs[l], hgrn_norm_g[l], w_branch[l], w_out[l])
        x = layer_norm(DN_ALPHA * x + sub_gate(mod, 1) * y, ln_g[l, 1], ln_b[l, 1])
        y = swiglu(modulate(x, mod, 2), ffn_w_in[l, 1], ffn_w_out[l, 1])
        x = layer_norm(DN_ALPHA * x + 0.5 * sub_gate(mod, 2) * y, ln_g[l, 2], ln_b[l, 2])
    return x


N_MIXERS = 2
N_A = (DEPTH + 1) // 2
N_B = DEPTH // 2
FFN_RES = 0.5
EPS = 1e-6

MLA_HEADS = 16
Q_LORA = 384
KV_LORA = 256
QK_NOPE = 64
QK_ROPE = 32
V_HEAD = 64
ROPE_THETA = 10000.0

DIL_GROUPS = ((128, 1), (512, 4), (2048, 16))
N_GROUPS = 3
DIL_HEADS = 16
DIL_HEAD_DIM = 64
DIL_BLOCK = 128
DIL_WIDTH = DIL_HEADS * DIL_HEAD_DIM

N_BUCKETS = 32
MAX_DISTANCE = 2048


def rmsnorm(x, g):
    xf = x.astype(jnp.float32)
    y = xf * lax.rsqrt(jnp.mean(xf * xf, axis=-1, keepdims=True) + EPS)
    return (y * g.astype(jnp.float32)).astype(x.dtype)

def swiglu_2(h, w_gate, w_up, w_down):
    return (jax.nn.silu(h @ w_gate) * (h @ w_up)) @ w_down

def rope(x, pos):
    half = x.shape[-1] // 2
    freqs = ROPE_THETA ** (-jnp.arange(half, dtype=jnp.float32) / half)
    ang = pos[:, None] * freqs[None, :]
    cos = jnp.cos(ang)[None, :, None, :]
    sin = jnp.sin(ang)[None, :, None, :]
    x1 = x[..., :half].astype(jnp.float32)
    x2 = x[..., half:].astype(jnp.float32)
    return jnp.concatenate([x1 * cos - x2 * sin, x1 * sin + x2 * cos], axis=-1).astype(x.dtype)

def causal_block_attention(q, k, v, scale):
    B, S, H, dq = q.shape
    nb = S // Q_BLOCK
    qb = q.reshape(B, nb, Q_BLOCK, H, dq).transpose(1, 0, 3, 2, 4)
    kt = k.transpose(0, 2, 1, 3)
    vt = v.transpose(0, 2, 1, 3)
    kpos = jnp.arange(S)

    def one_block(args):
        qi, n = args
        s = jnp.einsum('bhqd,bhkd->bhqk', qi, kt).astype(jnp.float32) * scale
        qpos = n * Q_BLOCK + jnp.arange(Q_BLOCK)
        s = jnp.where(kpos[None, :] <= qpos[:, None], s, -jnp.inf)
        p = jax.nn.softmax(s, axis=-1).astype(vt.dtype)
        return jnp.einsum('bhqk,bhkd->bhqd', p, vt)

    out = lax.map(one_block, (qb, jnp.arange(nb)))
    return out.transpose(1, 0, 3, 2, 4).reshape(B, S, H, v.shape[-1])

def mla(h, w_in, q_norm, w_q_up, kv_norm, w_kv_up, w_o):
    B, S, _ = h.shape
    lat = h @ w_in
    cq = lat[..., :Q_LORA]
    ckv = lat[..., Q_LORA:Q_LORA + KV_LORA]
    k_rope = lat[..., Q_LORA + KV_LORA:][:, :, None, :]
    q = (rmsnorm(cq, q_norm) @ w_q_up).reshape(B, S, MLA_HEADS, QK_NOPE + QK_ROPE)
    kv = (rmsnorm(ckv, kv_norm) @ w_kv_up).reshape(B, S, MLA_HEADS, QK_NOPE + V_HEAD)
    pos = jnp.arange(S, dtype=jnp.float32)
    q = jnp.concatenate([q[..., :QK_NOPE], rope(q[..., QK_NOPE:], pos)], axis=-1)
    k_rope = jnp.broadcast_to(rope(k_rope, pos), (B, S, MLA_HEADS, QK_ROPE))
    k = jnp.concatenate([kv[..., :QK_NOPE], k_rope.astype(kv.dtype)], axis=-1)
    v = kv[..., QK_NOPE:]
    o = causal_block_attention(q, k, v, (QK_NOPE + QK_ROPE) ** -0.5)
    return o.reshape(B, S, MLA_HEADS * V_HEAD) @ w_o

def t5_bucket_2(dist):
    max_exact = N_BUCKETS // 2
    d = jnp.maximum(dist, 1).astype(jnp.float32)
    large = max_exact + (jnp.log(d / max_exact) / math.log(MAX_DISTANCE / max_exact)
                         * (N_BUCKETS - max_exact)).astype(jnp.int32)
    large = jnp.minimum(large, N_BUCKETS - 1)
    return jnp.where(dist < max_exact, dist, large)

def strided_window_attention(q, k, v, dilation, span, bias_table):
    B, S, H, E = q.shape
    L = S // dilation
    nb = -(-L // DIL_BLOCK)
    Lp = nb * DIL_BLOCK
    qs = q.reshape(B, L, dilation, H, E)
    qb = jnp.pad(qs, ((0, 0), (0, Lp - L), (0, 0), (0, 0), (0, 0))).reshape(B, nb, DIL_BLOCK, dilation, H, E)

    def windows(t):
        tp = jnp.pad(t.reshape(B, L, dilation, H, E),
                     ((0, 0), (DIL_BLOCK, Lp - L), (0, 0), (0, 0), (0, 0)))
        tp = tp.reshape(B, nb + 1, DIL_BLOCK, dilation, H, E)
        return jnp.concatenate([tp[:, :-1], tp[:, 1:]], axis=2)

    kw, vw = windows(k), windows(v)
    s = jnp.einsum('bnqrhe,bnkrhe->bnrhqk', qb, kw).astype(jnp.float32) * (E ** -0.5)
    iq = jnp.arange(DIL_BLOCK)[:, None]
    ik = jnp.arange(2 * DIL_BLOCK)[None, :]
    rel = DIL_BLOCK + iq - ik
    in_window = (rel >= 0) & (rel <= span)
    bucket = t5_bucket_2(jnp.maximum(rel, 0) * dilation)
    bias = jnp.transpose(bias_table[bucket], (2, 0, 1)).astype(jnp.float32)
    key_m = (jnp.arange(nb)[:, None] - 1) * DIL_BLOCK + jnp.arange(2 * DIL_BLOCK)[None, :]
    valid = in_window[None] & (key_m >= 0)[:, None, :]
    logits = jnp.where(valid[None, :, None, None], s + bias, -jnp.inf)
    lse = jax.nn.logsumexp(logits, axis=-1)
    p = jnp.exp(logits - lse[..., None]).astype(v.dtype)
    o = jnp.einsum('bnrhqk,bnkrhe->bnqrhe', p, vw)
    o = o.reshape(B, Lp, dilation, H, E)[:, :L].reshape(B, S, H, E)
    lse = jnp.transpose(lse, (0, 1, 4, 2, 3)).reshape(B, Lp, dilation, H)[:, :L].reshape(B, S, H)
    return o, lse

def dilated_attention(h, w_in, w_o, rel_bias):
    B, S, _ = h.shape
    proj = (h @ w_in).reshape(B, S, N_GROUPS, 3, DIL_HEADS, DIL_HEAD_DIM)
    outs, lses = [], []
    for g, (window, dilation) in enumerate(DIL_GROUPS):
        o, lse = strided_window_attention(
            proj[:, :, g, 0], proj[:, :, g, 1], proj[:, :, g, 2],
            dilation, window // dilation, rel_bias[:, g * DIL_HEADS:(g + 1) * DIL_HEADS])
        outs.append(o)
        lses.append(lse)
    alpha = jax.nn.softmax(jnp.stack(lses, axis=0), axis=0)
    o = jnp.sum(alpha[..., None] * jnp.stack(outs, axis=0).astype(jnp.float32), axis=0)
    return o.astype(h.dtype).reshape(B, S, DIL_WIDTH) @ w_o

def sandwich(x, fn, pre_g, post_g, shift, scale, gate, res_w):
    hn = rmsnorm(x, pre_g) * (1 + scale[:, None, :]) + shift[:, None, :]
    y = rmsnorm(fn(hn), post_g)
    return x + res_w * gate[:, None, :] * y

def second_inputs(seed: int = 0) -> dict:
    key = jax.random.key(seed)
    ks = jax.random.split(key, 20)
    D = D_MODEL
    nrm = lambda k, shape, fan: jax.random.normal(k, shape, jnp.float32) * fan ** -0.5
    return {
        "x": jax.random.normal(ks[0], (BATCH, SEQ, D), jnp.float32),
        "c": jax.random.normal(ks[1], (BATCH, D), jnp.float32),
        "norm_pre": 1.0 + 0.05 * jax.random.normal(ks[2], (DEPTH, N_SUB, D), jnp.float32),
        "norm_post": 1.0 + 0.05 * jax.random.normal(ks[3], (DEPTH, N_SUB, D), jnp.float32),
        "w_mod": nrm(ks[4], (DEPTH, D, N_SUB * 3 * D), D) * 0.5,
        "b_mod": 0.02 * jax.random.normal(ks[5], (DEPTH, N_SUB * 3 * D), jnp.float32),
        "ffn_w_gate": nrm(ks[6], (DEPTH, 2, D, D_FF), D),
        "ffn_w_up": nrm(ks[7], (DEPTH, 2, D, D_FF), D),
        "ffn_w_down": nrm(ks[8], (DEPTH, 2, D_FF, D), D_FF),
        "mla_w_in": nrm(ks[9], (N_A, D, Q_LORA + KV_LORA + QK_ROPE), D),
        "mla_q_norm": 1.0 + 0.05 * jax.random.normal(ks[10], (N_A, Q_LORA), jnp.float32),
        "mla_w_q_up": nrm(ks[11], (N_A, Q_LORA, MLA_HEADS * (QK_NOPE + QK_ROPE)), Q_LORA),
        "mla_kv_norm": 1.0 + 0.05 * jax.random.normal(ks[12], (N_A, KV_LORA), jnp.float32),
        "mla_w_kv_up": nrm(ks[13], (N_A, KV_LORA, MLA_HEADS * (QK_NOPE + V_HEAD)), KV_LORA),
        "mla_w_o": nrm(ks[14], (N_A, MLA_HEADS * V_HEAD, D), MLA_HEADS * V_HEAD),
        "dil_w_in": nrm(ks[15], (N_B, D, N_GROUPS * 3 * DIL_WIDTH), D),
        "dil_w_o": nrm(ks[16], (N_B, DIL_WIDTH, D), DIL_WIDTH),
        "rel_bias": 0.5 * jax.random.normal(ks[17], (N_BUCKETS, N_GROUPS * DIL_HEADS), jnp.float32),
    }

def second_block(x, c, norm_pre, norm_post, w_mod, b_mod, ffn_w_gate, ffn_w_up, ffn_w_down,
              mla_w_in, mla_q_norm, mla_w_q_up, mla_kv_norm, mla_w_kv_up, mla_w_o,
              dil_w_in, dil_w_o, rel_bias):
    B = x.shape[0]
    for i in range(DEPTH):
        mod = (jax.nn.silu(c) @ w_mod[i] + b_mod[i]).reshape(B, N_SUB, 3, D_MODEL)

        def ffn_first(h, i=i):
            return swiglu_2(h, ffn_w_gate[i, 0], ffn_w_up[i, 0], ffn_w_down[i, 0])

        def ffn_second(h, i=i):
            return swiglu_2(h, ffn_w_gate[i, 1], ffn_w_up[i, 1], ffn_w_down[i, 1])

        if i % N_MIXERS == 0:
            a = i // N_MIXERS
            def mixer(h, a=a):
                return mla(h, mla_w_in[a], mla_q_norm[a], mla_w_q_up[a],
                           mla_kv_norm[a], mla_w_kv_up[a], mla_w_o[a])
        else:
            b = i // N_MIXERS
            def mixer(h, b=b):
                return dilated_attention(h, dil_w_in[b], dil_w_o[b], rel_bias)

        x = sandwich(x, ffn_first, norm_pre[i, 0], norm_post[i, 0],
                     mod[:, 0, 0], mod[:, 0, 1], mod[:, 0, 2], FFN_RES)
        x = sandwich(x, mixer, norm_pre[i, 1], norm_post[i, 1],
                     mod[:, 1, 0], mod[:, 1, 1], mod[:, 1, 2], 1.0)
        x = sandwich(x, ffn_second, norm_pre[i, 2], norm_post[i, 2],
                     mod[:, 2, 0], mod[:, 2, 1], mod[:, 2, 2], FFN_RES)
    return x


def setup_inputs(seed=0):
    out = dict(first_inputs(seed))
    for name, value in second_inputs(seed + 1).items():
        if name != "x":
            out[name + "_2"] = value
    return out


def reference(
    x, c, w_ada, b_ada, ln_g, ln_b, ffn_w_in, ffn_w_out, mix_w_in, pool_w, pool_scale, rel_bias,
    hgrn_lb, hgrn_norm_g, w_branch, w_out, c_2, norm_pre_2, norm_post_2, w_mod_2, b_mod_2,
    ffn_w_gate_2, ffn_w_up_2, ffn_w_down_2, mla_w_in_2, mla_q_norm_2, mla_w_q_up_2,
    mla_kv_norm_2, mla_w_kv_up_2, mla_w_o_2, dil_w_in_2, dil_w_o_2, rel_bias_2,
):
    x = first_block(
        x, c, w_ada, b_ada, ln_g, ln_b, ffn_w_in, ffn_w_out, mix_w_in, pool_w, pool_scale,
        rel_bias, hgrn_lb, hgrn_norm_g, w_branch, w_out,
    )
    return second_block(
        x, c_2, norm_pre_2, norm_post_2, w_mod_2, b_mod_2, ffn_w_gate_2, ffn_w_up_2,
        ffn_w_down_2, mla_w_in_2, mla_q_norm_2, mla_w_q_up_2, mla_kv_norm_2, mla_w_kv_up_2,
        mla_w_o_2, dil_w_in_2, dil_w_o_2, rel_bias_2,
    )


_drawn_inputs = setup_inputs


def setup_inputs(seed=0):
    import zlib

    import numpy as np

    out = dict(_drawn_inputs(seed))
    spreads = {}
    factors = {'b_ada': 4.607,
     'pool_scale': 8.0,
     'hgrn_lb': 8.0,
     'hgrn_norm_g': 8.0,
     'mla_q_norm_2': 8.0,
     'mla_kv_norm_2': 3.155}
    for name, (base, spread) in spreads.items():
        noise = np.random.default_rng([zlib.crc32(name.encode()), seed]).standard_normal(out[name].shape)
        drawn = base * np.exp(spread * noise) if base else spread * noise
        out[name] = __import__('jax').numpy.asarray(drawn.astype(out[name].dtype))
    for name, factor in factors.items():
        out[name] = (out[name] * factor).astype(out[name].dtype)
    return out
```

```python
from contextlib import ExitStack

import numpy as np

import concourse.bass as bass
from concourse import mybir

F32 = mybir.dt.float32
ALU = mybir.AluOpType
ACT = mybir.ActivationFunctionType
AXX = mybir.AxisListType.X

P = 128
S = 256
ST = S // P
D = 1024
DC = D // P
DEPTH = 2
N_SUB = 3
F = 2816
FT = F // P
HALF = 512
ALPHA = (2 * DEPTH) ** 0.25
LN_EPS = 1e-5
RMS_EPS = 1e-6
MASKED = -1e30

SLOTS = 4
SLOT = 4096
FULL = 80
MOD_UNITS = 6
IN_COLS = 256
IN_UNITS = F // IN_COLS
OUT_KC = (4, 3, 3, 3, 3, 3, 3)
FFN_ROUNDS = (MOD_UNITS + IN_UNITS + len(OUT_KC)) // SLOTS

POOL_GROUPS = 4
POOL_WIDTH = 256
POOL_WINDOWS = (2, 4, 8, 16)
AH = 4
IDX_H = 8
TOP_K = min(256, S // 4)
IDX_SCALE = 64 ** -0.5 * IDX_H ** -0.5
PICKED = -3e38
HH = 4
KEY_MAX = 1.0 - 1e-6
CHUNK = 64
NCH = S // CHUNK
SUB = 8
NSB = CHUNK // SUB
HC = HH * NCH
MIX_UNIT_COLS = (0, 512, 1024, 1536, 1608, 3144, 2632, 2120) + tuple(3656 + HALF * u for u in range(6))
MIX_ROUNDS = (MOD_UNITS + len(MIX_UNIT_COLS) + 4) // SLOTS

MH = 16
NOPE, ROPE, VH = 64, 32, 64
Q_LORA, KV_LORA = 384, 256
MLA_ROUNDS = (MOD_UNITS + 2 + 3 + 1 + 4) // SLOTS
DG = 3
DILATION = (1, 4, 16)
DSPAN = 128
DH = 16
OCT = 8
DIL_ROUNDS = (MOD_UNITS + 2 * 9 + 4) // SLOTS
TAB = 384
TABLES = AH + DG * DH

CONST = {}
CONST_COLS = 0
for _name, _cols in (("ident", P), ("ones", P), ("sel4", 4), ("selb", MOD_UNITS * P), ("causal", P),
                     ("reset64", S), ("reset8", S), ("invcnt", ST * S), ("swap", P), ("cos", S), ("sin", S)):
    if _name == "invcnt":
        KEPT_COLS = CONST_COLS
    CONST[_name] = (CONST_COLS, CONST_COLS + _cols)
    CONST_COLS += _cols


def buckets(dist, max_dist):
    d = np.maximum(dist, 1).astype(np.float32)
    large = 16 + (np.log(d / np.float32(16)) / np.float32(np.log(max_dist / 16)) * np.float32(16)).astype(np.int32)
    return np.where(dist < 16, dist, np.minimum(large, 31))


def constants():
    c = np.zeros((P, CONST_COLS), np.float32)

    def part(name, *shape):
        lo, hi = CONST[name]
        v = c[:, lo:hi]
        return v.reshape(P, *shape) if shape else v

    part("ident")[:] = np.eye(P)
    part("ones")[:] = 1.0
    for r in range(4):
        part("sel4")[32 * r, r] = 1.0
    selb = part("selb", MOD_UNITS, P)
    for r in range(4):
        selb[r, r, 0] = 1.0
    for r in range(4, 6):
        selb[r, r, :] = 1.0
    part("causal")[:] = np.where(np.arange(P)[None, :] <= np.arange(P)[:, None], 0.0, MASKED)
    part("reset64")[:] = (np.arange(S) % CHUNK != 0)
    part("reset8")[:] = (np.arange(S) % SUB != 0)
    inv = part("invcnt", ST, S)
    for g, w in enumerate(POOL_WINDOWS):
        inv[64 * (g % 2):64 * (g % 2) + 64, g // 2] = 1.0 / np.minimum(np.arange(1, S + 1), w)
    swap = part("swap")
    for h in range(4):
        for i in range(16):
            swap[32 * h + 16 + i, 32 * h + i] = -1.0
            swap[32 * h + i, 32 * h + 16 + i] = 1.0
    freqs = np.float32(10000.0) ** (-np.arange(16, dtype=np.float32) / np.float32(16))
    ang = np.arange(S, dtype=np.float32)[None, :] * freqs[:, None]
    part("cos")[:] = np.tile(np.cos(ang), (8, 1))
    part("sin")[:] = np.tile(np.sin(ang), (8, 1))
    return c


def picks():
    e = np.zeros((33, 1 + DG, TAB), np.float32)
    dist = S - 1 - np.arange(TAB)
    for g in range(1 + DG):
        dil = 1 if g == 0 else DILATION[g - 1]
        seen = dist >= 0
        if g:
            seen &= (dist % dil == 0) & (dist // dil <= DSPAN)
        b = buckets(np.maximum(dist, 0), 128 if g == 0 else 2048)
        e[np.where(seen, b, 32), g, np.arange(TAB)] = 1.0
    return e


class Links:

    def __init__(self, eng, sem):
        self.eng, self.sem, self.base, self.n = eng, sem, 0, 0

    def inc(self, ins):
        ins.then_inc(self.sem, 1)
        self.n += 1

    def wait(self):
        self.eng.wait_ge(self.sem, self.base + self.n)

    def link(self, ins):
        self.inc(ins)
        self.wait()

    def loop(self, count, name):
        return _LinkLoop(self, count, name)


class _LinkLoop:
    def __init__(self, links, count, name):
        self.links, self.count, self.name, self.per = links, count, name, LINKS[name]

    def __enter__(self):
        k = self.links
        self.kept = (k.base, k.n)
        self.fori = k.eng.Fori(0, self.count)
        i = self.fori.__enter__()
        k.base = k.base + k.n + i * self.per
        k.n = 0
        return i

    def __exit__(self, *error):
        k = self.links
        assert error[0] or k.n == self.per, f"the loop {self.name} makes {k.n} links a round, not {self.per}"
        out = self.fori.__exit__(*error)
        k.base, k.n = self.kept[0], self.kept[1] + self.count * self.per
        return out


ARENA = 21504
START_DMAS = 15
LINKS = {"dve1": 132}


def build(nc, a, out, stop=None):
    ctx = ExitStack()
    with ctx:
        def sb(name, shape):
            return ctx.enter_context(nc.sbuf_tensor(name, shape, F32))

        def sem(name):
            return ctx.enter_context(nc.semaphore(name))

        ring = [sb(f"ring{s}", [P, SLOT]) for s in range(SLOTS)]
        const = sb("const", [P, KEPT_COLS])
        x = sb("x", [P, ST, D])
        z = sb("z", [P, ST, D])
        hT = sb("hT", [P, DC, S])
        gate = sb("gate", [P, D])
        post_g = sb("post_g", [P, D])
        post_b = sb("post_b", [P, D])
        mod_rows = sb("mod_rows", [P, HALF])
        mod_cols = sb("mod_cols", [P, 2, DC])
        bias_rows = sb("bias_rows", [P, HALF])
        c_cols = sb("c_cols", [P, 2, DC])
        cond = sb("cond", [P, 2, DC])
        cond_row = sb("cond_row", [P, 2, DC, 32])
        cond_all = sb("cond_all", [P, DC, P])
        stat = sb("stat", [P, ST, 2, 6])
        mv = sb("mv", [P, ST, 2])
        rstd = sb("rstd", [P, ST])
        nmr = sb("nmr", [P, ST])
        sq = sb("sq", [P, ST, 2])
        pre_cols = sb("pre_cols", [P, DEPTH * N_SUB, DC])
        table1 = sb("table1", [P, AH, S])
        pool_bd = sb("pool_bd", [P, 2, P])
        layer_cols = sb("layer_cols", [P, 6])
        lb_cols = sb("lb_cols", [P, DEPTH, HH])
        oml = sb("oml", [P, DEPTH, HH])
        oml_l = sb("oml_l", [P, HH])
        lb_tmp = sb("lb_tmp", [P, 3, HH])
        eal = sb("eal", [P, HC])
        small = sb("small", [P, 64])
        mla_cols = sb("mla_cols", [P, 5])
        arena = sb("arena", [P, ARENA])

        def view(at, *shape, parts=P):
            n = int(np.prod(shape))
            assert at + n <= ARENA
            v = arena[0:parts, at:at + n]
            if len(shape) == 2:
                v = v.rearrange("p (a b) -> p a b", a=shape[0])
            if len(shape) == 3:
                v = v.rearrange("p (a b c) -> p a b c", a=shape[0], b=shape[1])
            return v

        act_t = view(0, FT, S)
        silu = view(FT * S, 2, S)
        pick = view(0, 1 + DG, TAB, parts=33)
        rb1 = view(1536, AH, parts=33)
        rb2 = view(1600, DG * DH, parts=33)
        tab = view(8192, 1 + DG, TAB, parts=DH)
        gates = view(0, 3 * DC, S)
        K0 = 3 * DC * S
        W = HH * S
        hq, sg, key, ff, aa, _, vt, ob = (view(K0 + n * W, HH, S) for n in range(8))
        vrows = view(K0 + 5 * W, ST, HH * P)
        y = z[:, :, :].rearrange("p t (c s) -> p (t c) s", s=S)
        T0 = K0 + 8 * W
        qT, kT = view(T0, 2, S), view(T0 + 512, 2, S)
        v_rows = view(T0 + 1024, ST, AH * 64)
        qiT = view(T0 + 1536, 4, S)
        kiT = view(T0 + 2560, S)
        wi = view(T0 + 2816, ST, IDX_H)
        aT = view(T0 + 2832, 2, S)
        T1 = T0 + 3344
        addm = view(T1, ST, S)
        score, work = view(T1 + 512, S), view(T1 + 768, S)
        relu = view(T1 + 1024, 2, S)
        lg = view(T1 + 1536, 2, S)
        pT = view(T1 + 2048, 2, ST * S)
        sums = [view(K0 + 7 * W, 2, S), view(K0 + 7 * W + 512, 2, S)]
        qb, gb0, gb1, tm0, tm1 = (view(T0 + n * W, HH, S) for n in range(5))
        qa, qd, kr0, kr1, kdec = (view(T0 + n * W, HH, S) for n in range(5))
        kd_rows = view(T0 + 4 * W, ST, HH * P)
        states = view(T0 + 5 * W, NCH - 1, HH, P)
        scoreT = aa
        refs = view(T0 + 4 * W, HC, NSB + 1)
        decay = ff

        cq, ck, kr = view(0, 3, S), view(768, 2, S), view(1280, S)
        lat_sq = view(1536, 5, S)
        inv_diag = view(2816, 2, S)
        rot = view(3328, S)
        mla_const = view(3584, P + 2 * S)
        swap, cos_t, sin_t = mla_const[:, 0:P], mla_const[:, P:P + S], mla_const[:, P + S:]
        mask2 = view(4224, S)
        qn, qr = view(4480, MH // 2, S), view(6528, MH // 4, S)
        kn = view(7552, MH // 2, S)
        v_mla = view(9600, ST, MH * VH)
        lg_m, pT_m = view(11648, 2, S), view(12160, 2, ST * S)
        oT = view(15360, DC, S)
        dq, dk = view(0, DG, OCT // 2, S), view(3072, DG, OCT // 2, S)
        dv = view(6144, DG, ST, OCT * 64)
        tabs = view(9216, 2, DG, S)
        lg_d = view(10752, 2, DG * S)
        pT_d = view(12288, 2, DG * ST * S)

        def cst(name, parts=P):
            lo, hi = CONST[name]
            return const[0:parts, lo:hi]

        ident, ones, sel4, causal = cst("ident"), cst("ones"), cst("sel4"), cst("causal")
        selb = cst("selb").rearrange("r (u m) -> r u m", u=MOD_UNITS)
        invcnt = aa[:, 0:2, :]
        carrier = sb("carrier", [P, 1])
        neg_half = sb("neg_half", [P, 8])
        ms = sb("ms", [P, 8])
        rs = sb("rs", [P, 8])

        bank = [ctx.enter_context(nc.psum_tensor(f"bank{b}", [P, HALF], F32)) for b in range(8)]

        bias_tab = nc.dram_tensor("bias_tab", (TABLES, P, TAB), F32, kind="Internal").ap()

        def table_src(row, n):
            return bass.AP(bias_tab.tensor, row * (P * TAB) + P - 1, [[TAB - 1, P], [P * TAB, n], [1, S]])

        ring_full = [sem(f"ring_full{s}") for s in range(SLOTS)]
        units_done = sem("units_done")
        const_in, x_in, start_in = sem("const_in"), sem("x_in"), sem("start_in")
        start_dve, start_act, start_pe = sem("start_dve"), sem("start_act"), sem("start_pe")
        lb_arg, lb_exp = sem("lb_arg"), sem("lb_exp")
        zeroed = sem("zeroed")
        tab_out, table_in = sem("tab_out"), sem("table_in")
        layer_in = sem("layer_in")
        bias_in, bias_used = sem("bias_in"), sem("bias_used")
        mod_rows_out = sem("mod_rows_out")
        mod_cols_done = sem("mod_cols_done")
        mod_cols_out = sem("mod_cols_out")
        gate_out = sem("gate_out")
        post_in = sem("post_in")
        post_used = sem("post_used")
        rows_ready = sem("rows_ready")
        y_read = sem("y_read")
        turned = sem("turned")
        h_act, h_dve = sem("h_act"), sem("h_dve")
        in_done = sem("in_done")
        silu_done = sem("silu_done")
        tile_done = sem("tile_done")
        var_done, inv_done = sem("var_done"), sem("inv_done")
        nmr_done, norm_done = sem("nmr_done"), sem("norm_done")
        sq_done = sem("sq_done")
        out_done = sem("out_done")
        dve_link, act_link, pool_link = sem("dve_link"), sem("act_link"), sem("pool_link")
        px_done, px_out = sem("px_done"), sem("px_out")
        pool_d, pool_done = sem("pool_d"), sem("pool_done")
        ya_out = sem("ya_out")
        ix_done, ix_relu, ix_used = sem("ix_done"), sem("ix_relu"), sem("ix_used")
        at_s, at_read, at_ready, at_exp = sem("at_s"), sem("at_read"), sem("at_ready"), sem("at_exp")
        at_p, at_t, at_pt, at_o, at_out = sem("at_p"), sem("at_t"), sem("at_pt"), sem("at_o"), sem("at_out")
        h_f, h_ln, h_scan, h_ea = sem("h_f"), sem("h_ln"), sem("h_scan"), sem("h_ea")
        vt_done, vt_out = sem("vt_done"), sem("vt_out")
        band_g, band_mm, band_read = sem("band_g"), sem("band_mm"), sem("band_read")
        kr_arg, kr_exp, kr_ready, kr_used = sem("kr_arg"), sem("kr_exp"), sem("kr_ready"), sem("kr_used")
        kd_done, kd_out = sem("kd_done"), sem("kd_out")
        sc_out, ds_done, st_ready, ho_done = sem("sc_out"), sem("ds_done"), sem("st_ready"), sem("ho_done")
        ho_sum, ho_sq, ho_ss = sem("ho_sum"), sem("ho_sq"), sem("ho_ss")
        ho_ms, ho_inv, ho_diag, ho_rep, yc_out = sem("ho_ms"), sem("ho_inv"), sem("ho_diag"), sem("ho_rep"), sem("yc_out")
        gates_out, br_done, merged = sem("gates_out"), sem("br_done"), sem("merged")

        normed = sem("normed")
        gate2_out = sem("gate2_out")
        ml_done, ml_out = sem("ml_done"), sem("ml_out")
        ml_sq, ml_ss, ml_ms, ml_inv = sem("ml_sq"), sem("ml_ss"), sem("ml_ms"), sem("ml_inv")
        ml_diag, ml_rep, ml_norm = sem("ml_diag"), sem("ml_rep"), sem("ml_norm")
        ml_const, rot_done, rot_out = sem("ml_const"), sem("rot_done"), sem("rot_out")
        mt_s, mt_read, mt_ready, mt_exp = sem("mt_s"), sem("mt_read"), sem("mt_ready"), sem("mt_exp")
        mt_p, mt_t, mt_pt, mt_o, mt_out = sem("mt_p"), sem("mt_t"), sem("mt_pt"), sem("mt_o"), sem("mt_out")
        dx_done, dx_out = sem("dx_done"), sem("dx_out")
        tabs_in = [sem("tabs_in0"), sem("tabs_in1")]
        tabs_used = sem("tabs_used")
        dt_s, dt_read, dt_ready, dt_exp = sem("dt_s"), sem("dt_read"), sem("dt_ready"), sem("dt_exp")
        dt_p, dt_t, dt_pt, dt_o, dt_out = sem("dt_p"), sem("dt_t"), sem("dt_pt"), sem("dt_o"), sem("dt_out")

        block = ctx.enter_context(nc.Block())
        layers = DEPTH if stop is None or stop > N_SUB else 1
        subs = range(N_SUB if stop is None else min(stop, N_SUB))

        START1 = (0, FFN_ROUNDS, FFN_ROUNDS + MIX_ROUNDS)
        LAYER1 = 2 * FFN_ROUNDS + MIX_ROUNDS

        START2 = [DEPTH * LAYER1]
        for rounds in (FFN_ROUNDS, MLA_ROUNDS, FFN_ROUNDS, FFN_ROUNDS, DIL_ROUNDS):
            START2.append(START2[-1] + rounds)
        M2 = DEPTH * N_SUB
        subs2 = range(DEPTH * N_SUB if stop is None else max(0, stop - M2))

        def freed(round_, unit):
            return SLOTS + SLOTS * round_ + unit + 1

        TILES = []
        for u, kinds in enumerate((["c"] * 4, ["c", "c", "r256", "r256"], ["c"] * 4, ["c", "r8", "r8"], ["c"] * 4,
                                   ["c"] * 4, ["r512", "r512"], ["c"] * 4) + (["c"] * 4,) * 6):
            for k, kind in enumerate(kinds):
                rows = kind[0] == "r"
                n = int(kind[1:]) if rows else P
                c0 = (0 if n == HALF else (256 if n == 256 else P)) if rows else k * P
                TILES.append((MOD_UNITS + u, rows, c0, n, k - (2 if n == 256 else 1 if n == 8 else 0) if rows else 0,
                              k == len(kinds) - 1))
        MID = sum(not t[5] for t in TILES)
        NT = len(TILES)
        MID_AT = [sum(not t[5] for t in TILES[:i + 1]) for i in range(NT)]

        def kcn(w):
            return w.rearrange("(kc p) n -> p kc n", p=P)

        def cols(slot, kc, n):
            return ring[slot][:, 0:kc * n].rearrange("p (kc n) -> p kc n", kc=kc)

        def sub1(l, j):
            return l * N_SUB + j

        @block.sync
        def _(sp):
            def load(round_, slot, *moves):
                sp.wait_ge(units_done, SLOTS * round_ + slot + 1)
                for i, (dst, src) in enumerate(moves):
                    sp.dma_start(dst, src).then_inc(ring_full[slot], FULL - 16 * (len(moves) - 1) if i == 0 else 16)

            def load_mod(round_, w, j):
                for u in range(MOD_UNITS):
                    at = (j * MOD_UNITS + u) * HALF
                    load(round_ + u // SLOTS, u % SLOTS, (cols(u % SLOTS, DC, HALF), kcn(w)[:, :, at:at + HALF]))

            def load_ffn(round_, w_gate, w_up, w_out):
                def unit(u, i=0):
                    r, s = divmod(MOD_UNITS + u, SLOTS)
                    at = (i * SLOTS + u) * IN_COLS
                    v = ring[s][:, :].rearrange("p (two kc n) -> p two kc n", two=2, kc=DC)
                    load(round_ + i + r, s,
                         (v[:, 0], kcn(w_gate)[:, :, bass.ds(at, IN_COLS)]),
                         (v[:, 1], kcn(w_up)[:, :, bass.ds(at, IN_COLS)]))

                with sp.Fori(0, IN_UNITS // SLOTS) as i:
                    for u in range(SLOTS):
                        unit(u, i)
                for u in range(IN_UNITS // SLOTS * SLOTS, IN_UNITS):
                    unit(u)
                kc = 0
                for u, n in enumerate(OUT_KC):
                    r, s = divmod(MOD_UNITS + IN_UNITS + u, SLOTS)
                    load(round_ + r, s, (cols(s, n, D), kcn(w_out)[:, kc:kc + n, :]))
                    kc += n

            def load_mix(round_, w, w_branch, w_out):
                for u, at in enumerate(MIX_UNIT_COLS):
                    r, s = divmod(MOD_UNITS + u, SLOTS)
                    if u == 3:
                        v = cols(s, DC, P + IDX_H)
                        load(round_ + r, s, (v[:, :, 0:64], kcn(w)[:, :, at:at + 64]),
                             (v[:, :, 64:P + IDX_H], kcn(w)[:, :, at:at + 64 + IDX_H]))
                    else:
                        load(round_ + r, s, (cols(s, DC, HALF), kcn(w)[:, :, at:at + HALF]))
                for h in range(2):
                    load(round_ + 5, h, (cols(h, DC, HALF), kcn(w_branch)[:, :, h * HALF:(h + 1) * HALF]))
                for h in range(2):
                    load(round_ + 5, 2 + h, (cols(2 + h, 4, D), kcn(w_out)[:, 4 * h:4 * h + 4, :]))

            sp.wait_ge(zeroed, 1)
            with sp.Fori(0, layers) as l:
                for j in subs:
                    r = l * LAYER1 + START1[j]
                    load_mod(r, a["w_ada"][l], j)
                    if j == 1:
                        load_mix(r, a["mix_w_in"][l], a["w_branch"][l], a["w_out"][l])
                    else:
                        w_in = a["ffn_w_in"][l, j // 2]
                        load_ffn(r, w_in[:, 0:F], w_in[:, F:2 * F], a["ffn_w_out"][l, j // 2])
            for n in subs2:
                i, j = divmod(n, N_SUB)
                r = START2[n]
                load_mod(r, a["w_mod_2"][i], j)
                if j != 1:
                    load_ffn(r, a["ffn_w_gate_2"][i, j // 2], a["ffn_w_up_2"][i, j // 2], a["ffn_w_down_2"][i, j // 2])
                elif i == 0:
                    w = kcn(a["mla_w_in_2"][0])
                    load(r + 1, 2, (cols(2, DC, Q_LORA), w[:, :, 0:Q_LORA]))
                    v = cols(3, DC, KV_LORA + P)
                    load(r + 1, 3, (v[:, :, 0:KV_LORA], w[:, :, Q_LORA:Q_LORA + KV_LORA]),
                         *((v[:, :, KV_LORA + 32 * g:KV_LORA + 32 * (g + 1)], w[:, :, Q_LORA + KV_LORA:]) for g in range(4)))
                    for q in range(3):
                        w = a["mla_w_q_up_2"][0][q * P:(q + 1) * P].rearrange("p (h e) -> p h e", h=MH)
                        load(r + 2, q, (ring[q][:, 0:MH * NOPE].rearrange("p (h e) -> p h e", h=MH), w[:, :, 0:NOPE]),
                             (ring[q][:, MH * NOPE:MH * (NOPE + ROPE)].rearrange("p (h e) -> p h e", h=MH), w[:, :, NOPE:]))
                    moves = []
                    for kc in range(2):
                        w = a["mla_w_kv_up_2"][0][kc * P:(kc + 1) * P].rearrange("p (h two e) -> p two h e", h=MH, two=2)
                        for g in range(2):
                            moves.append((cols(3, 4, MH * NOPE)[:, 2 * kc + g, :].rearrange("p (h e) -> p h e", h=MH), w[:, g]))
                    load(r + 2, 3, *moves)
                    for q in range(4):
                        load(r + 3, q, (cols(q, 2, D), kcn(a["mla_w_o_2"][0])[:, 2 * q:2 * q + 2, :]))
                else:
                    for u in range(2 * 3 * DG):
                        rr, s = divmod(MOD_UNITS + u, SLOTS)
                        o, gt = divmod(u, 3 * DG)
                        at = gt * D + o * OCT * 64
                        load(r + rr, s, (cols(s, DC, HALF), kcn(a["dil_w_in_2"][0])[:, :, at:at + HALF]))
                    for q in range(4):
                        load(r + 6, q, (cols(q, 2, D), kcn(a["dil_w_o_2"][0])[:, 2 * q:2 * q + 2, :]))
            sp.wait_ge(rows_ready, ST * (layers * len(subs) + len(subs2) + 1))
            sp.dma_start(out[0].rearrange("(t p) d -> p t d", p=P), x[:, :, :]).then_inc(out_done, 16)
            sp.wait_ge(out_done, 16)

        @block.tensor
        def _(pe):
            mm = nc.tensor.matmul

            def arrived(round_, unit):
                r, s = divmod(unit, SLOTS)
                pe.wait_ge(ring_full[s], (round_ + r + 1) * FULL)
                return s

            def mod_pe(round_, m, blk):
                pe.wait_ge(bias_in, 16 * (m + 1))
                for u in range(MOD_UNITS):
                    w = cols(arrived(round_, u), DC, HALF)
                    if u < 4:
                        o, lhs = bank[0][32 * u:32 * u + 32, :], cond_row[:, blk]
                    else:
                        o, lhs = bank[u - 2][:, :], cond_all
                    mm(o, selb[:, u, 0:32 if u < 4 else P], bias_rows[:, :], start=True, stop=False).then_inc(bias_used, 1)
                    for kc in range(DC):
                        ins = mm(o, lhs[:, kc, :], w[:, kc, :], start=False, stop=kc == DC - 1)
                    ins.then_inc(units_done, 1)
                pe.wait_ge(mod_rows_out, m + 1)
                for c in range(4):
                    ins = mm(bank[1][:, 4 * c:4 * c + 4], mod_rows[:, c * P:(c + 1) * P], sel4, start=True, stop=True)
                ins.then_inc(mod_cols_done, 1)

            def turn_pe(m, src, ready, base):
                for t in range(ST):
                    pe.wait_ge(ready, base + t + 1)
                    if t == 0:
                        pe.wait_ge(y_read, 4 * (m + 1))
                    for c in range(DC):
                        ins = nc.tensor.transpose(bank[4 + c // 2][:, (c % 2) * S + t * P:(c % 2) * S + (t + 1) * P],
                                                  src[:, t, c * P:(c + 1) * P], ident)
                        if t == ST - 1 and c % 2:
                            ins.then_inc(turned, 1)

            def ffn_pe(round_, m, f):
                def unit(u, i=0):
                    s = arrived(round_ + i, MOD_UNITS + u)
                    if u == 0:
                        pe.wait_ge(h_act, 2 * m + 2)
                        pe.wait_ge(h_dve, 2 * m + 2)
                    w = ring[s][:, :].rearrange("p (two kc n) -> p two kc n", two=2, kc=DC)
                    for q in range(2):
                        t = 2 * u + q
                        pe.wait_ge(tile_done, FT * f + 2 * SLOTS * i + t + 1)
                        for g in range(2):
                            for kc in range(DC):
                                ins = mm(bank[t % 4][:, g * S:(g + 1) * S], w[:, g, kc, q * P:(q + 1) * P], hT[:, kc, :],
                                         start=kc == 0, stop=kc == DC - 1)
                        ins.then_inc(in_done if q == 0 else units_done, 1)

                with pe.Fori(0, IN_UNITS // SLOTS) as i:
                    for u in range(SLOTS):
                        unit(u, i)
                for u in range(IN_UNITS // SLOTS * SLOTS, IN_UNITS):
                    unit(u)
                k0 = 0
                for u, n in enumerate(OUT_KC):
                    w = cols(arrived(round_, MOD_UNITS + IN_UNITS + u), n, D)
                    pe.wait_ge(tile_done, 4 + FT * f + k0 + n)
                    for kc in range(n):
                        for t in range(ST):
                            for h in range(2):
                                ins = mm(bank[4 + 2 * t + h][:, :], act_t[:, k0 + kc, t * P:(t + 1) * P],
                                         w[:, kc, h * HALF:(h + 1) * HALF], start=k0 + kc == 0, stop=k0 + kc == FT - 1)
                    ins.then_inc(units_done, 1)
                    k0 += n

            def mix_pe(round_, m, l):
                pe.wait_ge(h_act, 2 * m + 2)
                pe.wait_ge(h_dve, 2 * m + 2)
                last_unit = None
                for i, (u, rows, c0, n, tt, last) in enumerate(TILES):
                    if u != last_unit:
                        width = P + IDX_H if u == MOD_UNITS + 3 else HALF
                        w = cols(arrived(round_, u), DC, width)
                        last_unit = u
                    if i >= 4:
                        pe.wait_ge(px_out, NT * l + i - 3)
                    for kc in range(DC):
                        if rows:
                            ins = mm(bank[i % 4][:, 0:n], hT[:, kc, tt * P:(tt + 1) * P], w[:, kc, c0:c0 + n],
                                     start=kc == 0, stop=kc == DC - 1)
                        else:
                            ins = mm(bank[i % 4][:, 0:S], w[:, kc, c0:c0 + P], hT[:, kc, :],
                                     start=kc == 0, stop=kc == DC - 1)
                    ins.then_inc(units_done if last else px_done, 1)
                pe.wait_ge(px_out, NT * (l + 1))
                pe.wait_ge(layer_in, 16 * 7 * (l + 1))
                pe.wait_ge(pool_d, l + 1)
                for t in range(2):
                    ins = mm(bank[4][:, t * S:(t + 1) * S], pool_bd[:, t, :], aT[:, t, :], start=True, stop=True)
                ins.then_inc(pool_done, 1)
                for n in range(ST * IDX_H):
                    qt, h = divmod(n, IDX_H)
                    ns, b = (qt + 1) * P, 64 * (h % 2)
                    if n >= 4:
                        pe.wait_ge(ix_relu, 16 * l + n - 3)
                    mm(bank[n % 4][:, 0:ns], qiT[b:b + 64, h // 2, qt * P:(qt + 1) * P], kiT[b:b + 64, 0:ns],
                       start=True, stop=True).then_inc(ix_done, 1)

                def scores(c):
                    h, qt = divmod(c, ST)
                    ns, b = (qt + 1) * P, 64 * (h % 2)
                    if c >= 2:
                        pe.wait_ge(at_read, 8 * l + c - 1)
                    elif c == 0:
                        pe.wait_ge(ya_out, l + 1)
                    mm(bank[4 + c % 2][:, 0:ns], qT[b:b + 64, h // 2, qt * P:(qt + 1) * P], kT[b:b + 64, h // 2, 0:ns],
                       start=True, stop=True).then_inc(at_s, 1)

                scores(0)
                for c in range(AH * ST):
                    h, qt = divmod(c, ST)
                    b = 64 * (h % 2)
                    if c + 1 < AH * ST:
                        scores(c + 1)
                    pe.wait_ge(at_p, 8 * l + c + 1)
                    if c >= 2:
                        pe.wait_ge(at_pt, 8 * l + c - 1)
                    for k in range(qt + 1):
                        ins = nc.tensor.transpose(bank[6 + c % 2][:, k * P:(k + 1) * P], lg[:, c % 2, k * P:(k + 1) * P], ident)
                    ins.then_inc(at_t, 1)
                    if qt == 1:
                        pe.wait_ge(at_pt, 8 * l + c + 1)
                        if h == 0:
                            pe.wait_ge(ix_relu, 16 * (l + 1))
                        pt = pT[:, h % 2, :].rearrange("p (k q) -> p k q", k=ST)
                        o = bank[h // 2][b:b + 64, :]
                        mm(o[:, 0:S], v_rows[:, 0, h * 64:(h + 1) * 64], pt[:, 0, :], start=True, stop=False)
                        mm(o[:, P:S], v_rows[:, 1, h * 64:(h + 1) * 64], pt[:, 1, P:S], start=False, stop=True).then_inc(at_o, 1)

                pe.wait_ge(at_pt, 8 * (l + 1))
                pe.wait_ge(at_read, 8 * (l + 1))
                for h in range(HH):
                    for t in range(ST):
                        ins = nc.tensor.transpose(bank[4 + h // 2][:, (h % 2) * S + t * P:(h % 2) * S + (t + 1) * P],
                                                  vrows[:, t, h * P:(h + 1) * P], ident)
                ins.then_inc(vt_done, 1)
                for dt in range(SUB):
                    g = (gb0, gb1)[dt % 2]
                    pe.wait_ge(band_g, SUB * l + dt + 1)
                    if dt >= 2:
                        pe.wait_ge(band_read, 2 * (SUB * l + dt - 1))
                    elif dt == 0:
                        pe.wait_ge(at_out, AH * (l + 1))
                    nblk, w = 2 * S // SUB, SUB - dt
                    for q in range(2):
                        gv = g[:, 2 * q:2 * q + 2, :].rearrange("p h (b s) -> p (h b) s", s=SUB)[:, :, dt:SUB]
                        ov = bank[2 * (dt % 2) + q][:, 0:nblk * w].rearrange("p (b s) -> p b s", s=w)
                        mm(ov, ones, gv, start=True, stop=True).then_inc(band_mm, 1)
                pe.wait_ge(vt_out, l + 1)
                pe.wait_ge(band_read, 2 * SUB * (l + 1))
                for i in range(1, NSB):
                    kr = (kr0, kr1)[i % 2]
                    pe.wait_ge(kr_ready, NSB * l + i)
                    for hc in range(HC):
                        h, c = divmod(hc, NCH)
                        b = CHUNK * (c % 2)
                        at = (h * 2 + c // 2) * CHUNK + SUB * i
                        ins = mm(bank[4][b:b + CHUNK, at:at + SUB], kr[:, h, c * CHUNK:(c + 1) * CHUNK],
                                 qd[:, h, c * CHUNK + SUB * i:c * CHUNK + SUB * (i + 1)], start=True, stop=True)
                    ins.then_inc(kr_used, 1)
                pe.wait_ge(kr_ready, NSB * (l + 1))
                for t in range(ST):
                    for h in range(HH):
                        ins = nc.tensor.transpose(bank[2 + t][:, h * P:(h + 1) * P], kr0[:, h, t * P:(t + 1) * P], ident)
                ins.then_inc(kd_done, 1)
                pe.wait_ge(kd_out, l + 1)
                for c in range(NCH - 1):
                    b = CHUNK * (c % 2)
                    for h in range(HH):
                        ins = mm(bank[(5, 0, 1)[c]][:, h * P:(h + 1) * P], kd_rows[b:b + CHUNK, c // 2, h * P:(h + 1) * P],
                                 vrows[b:b + CHUNK, c // 2, h * P:(h + 1) * P], start=True, stop=True)
                    ins.then_inc(ds_done, 1)
                pe.wait_ge(sc_out, l + 1)
                for t in range(ST):
                    for h in range(HH):
                        o = bank[6 + h // 2][:, (h % 2) * S:(h % 2) * S + S]
                        mm(o[:, t * P:(t + 1) * P], vrows[:, t, h * P:(h + 1) * P], scoreT[:, h, t * P:(t + 1) * P],
                           start=True, stop=False)
                        for c in ((1,), (2, 3))[t]:
                            if h == 0:
                                pe.wait_ge(st_ready, (NCH - 1) * l + c)
                            ins = mm(o[:, c * CHUNK:(c + 1) * CHUNK], states[:, c - 1, h, :], qa[:, h, c * CHUNK:(c + 1) * CHUNK],
                                     start=False, stop=c != 2)
                ins.then_inc(ho_done, 1)
                pe.wait_ge(ho_sq, l + 1)
                for h in range(HH):
                    for t in range(ST):
                        ins = mm(bank[2][:, h * ST + t:h * ST + t + 1], tm0[:, h, t * P:(t + 1) * P], ones[:, 0:1],
                                 start=True, stop=True)
                ins.then_inc(ho_ss, 1)
                pe.wait_ge(ho_diag, l + 1)
                for q in range(2):
                    ins = mm(bank[q][:, :], ones, tm1[:, 2 * q:2 * q + 2, :], start=True, stop=True)
                ins.then_inc(ho_rep, 1)
                pe.wait_ge(yc_out, l + 1)
                pe.wait_ge(at_out, AH * (l + 1))
                for u in range(2):
                    w = cols(arrived(round_, 20 + u), DC, HALF)
                    for q in range(4):
                        t = 4 * u + q
                        if t >= 2:
                            pe.wait_ge(merged, DC * l + t - 1)
                        for g, (k0, k1) in enumerate(((0, 2), (2, 4), (4, 8))):
                            o = bank[2 * (t % 2) + g // 2][:, (g % 2) * S:(g % 2) * S + S]
                            for kc in range(k0, k1):
                                ins = mm(o, w[:, kc, q * P:(q + 1) * P], y[:, kc, :], start=kc == k0, stop=kc == k1 - 1)
                        ins.then_inc(units_done if q == 3 else br_done, 1)
                out_pe(round_, 22, hT, lambda k: pe.wait_ge(merged, DC * l + k))

            def out_pe(round_, unit0, src, ready, kcs=4):
                for u in range(DC // kcs):
                    w = cols(arrived(round_, unit0 + u), kcs, D)
                    ready(kcs * (u + 1))
                    for kc in range(kcs):
                        for t in range(ST):
                            for h in range(2):
                                ins = mm(bank[4 + 2 * t + h][:, :], src[:, kcs * u + kc, t * P:(t + 1) * P],
                                         w[:, kc, h * HALF:(h + 1) * HALF], start=u + kc == 0, stop=kcs * u + kc == DC - 1)
                    ins.then_inc(units_done, 1)

            def mla_pe(round_, m):
                pe.wait_ge(h_act, 2 * m + 2)
                pe.wait_ge(h_dve, 2 * m + 2)
                w6, w7 = cols(arrived(round_, 6), DC, Q_LORA), cols(arrived(round_, 7), DC, KV_LORA + P)
                for t in range(6):
                    if t >= 4:
                        pe.wait_ge(ml_out, t - 3)
                    for kc in range(DC):
                        if t < 3:
                            lhs = w6[:, kc, t * P:(t + 1) * P]
                        else:
                            lhs = w7[:, kc, (t - 3) * P:(t - 2) * P]
                        ins = mm(bank[t % 4][:, 0:S], lhs, hT[:, kc, :], start=kc == 0, stop=kc == DC - 1)
                    ins.then_inc(units_done if t in (2, 5) else ml_done, 1)
                pe.wait_ge(ml_sq, 1)
                for g, (c0, c1) in enumerate(((0, 3), (3, 5))):
                    for t in range(ST):
                        for c in range(c0, c1):
                            ins = mm(bank[4][:, 2 * g + t:2 * g + t + 1], lat_sq[:, c, t * P:(t + 1) * P], ones[:, 0:1],
                                     start=c == c0, stop=c == c1 - 1)
                ins.then_inc(ml_ss, 1)
                pe.wait_ge(ml_diag, 1)
                mm(bank[5][:, :], ones, inv_diag, start=True, stop=True).then_inc(ml_rep, 1)
                pe.wait_ge(ml_norm, 1)
                wq = [ring[arrived(round_, 8 + q)] for q in range(3)]
                wkv = cols(arrived(round_, 11), 4, MH * NOPE)
                for t in range(24):
                    pe.wait_ge(ml_out, t + 3)
                    n = 3 if t < 12 else 2
                    for kc in range(n):
                        o = bank[(6 + t) % 4][:, 0:S]
                        if t < 12:
                            lhs, rhs = wq[kc][:, t * P:(t + 1) * P], cq[:, kc, :]
                        elif t < 20:
                            lhs, rhs = wkv[:, 2 * kc, (t - 12) * P:(t - 11) * P], ck[:, kc, :]
                        else:
                            tt, g = divmod(t - 20, 2)
                            o = bank[(6 + t) % 4][:, :]
                            lhs, rhs = ck[:, kc, tt * P:(tt + 1) * P], wkv[:, 2 * kc + 1, g * HALF:(g + 1) * HALF]
                        ins = mm(o, lhs, rhs, start=kc == 0, stop=kc == n - 1)
                    if t == 11:
                        ins.then_inc(units_done, 3)
                    elif t == 23:
                        ins.then_inc(units_done, 1)
                    else:
                        ins.then_inc(ml_done, 1)
                pe.wait_ge(ml_const, 16)
                pe.wait_ge(ml_out, 30)
                for t in range(5):
                    if t >= 4:
                        pe.wait_ge(rot_out, t - 3)
                    mm(bank[t % 4][:, 0:S], swap, kr if t == 4 else qr[:, t, :], start=True, stop=True).then_inc(rot_done, 1)
                pe.wait_ge(rot_out, 5)

                def scores(c):
                    h, qt = divmod(c, ST)
                    ns = (qt + 1) * P
                    if c >= 2:
                        pe.wait_ge(mt_read, c - 1)
                    b = 64 * (h % 2)
                    mm(bank[4 + c % 2][:, 0:ns], qn[b:b + 64, h // 2, qt * P:(qt + 1) * P], kn[b:b + 64, h // 2, 0:ns],
                       start=True, stop=False)
                    b = 32 * (h % 4)
                    mm(bank[4 + c % 2][:, 0:ns], qr[b:b + 32, h // 4, qt * P:(qt + 1) * P], kr[b:b + 32, 0:ns],
                       start=False, stop=True).then_inc(mt_s, 1)

                scores(0)
                for c in range(MH * ST):
                    h, qt = divmod(c, ST)
                    b = 64 * (h % 2)
                    if c + 1 < MH * ST:
                        scores(c + 1)
                    pe.wait_ge(mt_p, c + 1)
                    if c >= 2:
                        pe.wait_ge(mt_pt, c - 1)
                    for kk in range(qt + 1):
                        ins = nc.tensor.transpose(bank[6 + c % 2][:, kk * P:(kk + 1) * P], lg_m[:, c % 2, kk * P:(kk + 1) * P], ident)
                    ins.then_inc(mt_t, 1)
                    if qt == 1:
                        pe.wait_ge(mt_pt, c + 1)
                        if h >= 4:
                            pe.wait_ge(mt_out, h - 3)
                        pt = pT_m[:, h % 2, :].rearrange("p (k q) -> p k q", k=ST)
                        o = bank[(h // 2) % 2][b:b + 64, :]
                        mm(o[:, 0:S], v_mla[:, 0, h * 64:(h + 1) * 64], pt[:, 0, :], start=True, stop=False)
                        mm(o[:, P:S], v_mla[:, 1, h * 64:(h + 1) * 64], pt[:, 1, P:S], start=False, stop=True).then_inc(mt_o, 1)
                pe.wait_ge(mt_pt, MH * ST)
                out_pe(round_, 12, oT, lambda kc: pe.wait_ge(mt_out, 2 * kc), 2)

            def dil_pe(round_, m):
                pe.wait_ge(h_act, 2 * m + 2)
                pe.wait_ge(h_dve, 2 * m + 2)
                for o in range(2):
                    t = 0
                    for u in range(3 * DG):
                        w = cols(arrived(round_, MOD_UNITS + 9 * o + u), DC, HALF)
                        tiles = 2 if u % 3 == 2 else 4
                        for q in range(tiles):
                            if 30 * o + t >= 4:
                                pe.wait_ge(dx_out, 30 * o + t - 3)
                            for kc in range(DC):
                                if tiles == 2:
                                    ins = mm(bank[t % 4][:, :], hT[:, kc, q * P:(q + 1) * P], w[:, kc, :],
                                             start=kc == 0, stop=kc == DC - 1)
                                else:
                                    ins = mm(bank[t % 4][:, 0:S], w[:, kc, q * P:(q + 1) * P], hT[:, kc, :],
                                             start=kc == 0, stop=kc == DC - 1)
                            ins.then_inc(units_done if q == tiles - 1 else dx_done, 1)
                            t += 1
                    pe.wait_ge(dx_out, 30 * (o + 1))
                    C = OCT * ST

                    def scores(c):
                        h, qt = divmod(c, ST)
                        ns, b = (qt + 1) * P, 64 * (h % 2)
                        if C * o + c >= 2:
                            pe.wait_ge(dt_read, C * o + c - 1)
                        for g in range(DG):
                            at = g * ns
                            ins = mm(bank[4 + 2 * (c % 2) + at // HALF][:, at % HALF:at % HALF + ns],
                                     dq[b:b + 64, g, h // 2, qt * P:(qt + 1) * P], dk[b:b + 64, g, h // 2, 0:ns],
                                     start=True, stop=True)
                        ins.then_inc(dt_s, 1)

                    scores(0)
                    for c in range(C):
                        h, qt = divmod(c, ST)
                        b = 64 * (h % 2)
                        if c + 1 < C:
                            scores(c + 1)
                        pe.wait_ge(dt_p, C * o + c + 1)
                        if C * o + c >= 1:
                            pe.wait_ge(dt_pt, C * o + c)
                        for kk in range(DG * (qt + 1)):
                            ins = nc.tensor.transpose(bank[2 + kk // 4][:, kk % 4 * P:(kk % 4 + 1) * P],
                                                      lg_d[:, c % 2, kk * P:(kk + 1) * P], ident)
                        ins.then_inc(dt_t, 1)
                        if qt == 1:
                            pe.wait_ge(dt_pt, C * o + c + 1)
                            if OCT * o + h >= 4:
                                pe.wait_ge(dt_out, OCT * o + h - 3)
                            pt = pT_d[:, h % 2, :].rearrange("p (g k q) -> p g k q", g=DG, k=ST)
                            ob_ = bank[(h // 2) % 2][b:b + 64, :]
                            for g in range(DG):
                                mm(ob_[:, 0:S], dv[:, g, 0, h * 64:(h + 1) * 64], pt[:, g, 0, :], start=g == 0, stop=False)
                                ins = mm(ob_[:, P:S], dv[:, g, 1, h * 64:(h + 1) * 64], pt[:, g, 1, P:S], start=False, stop=g == DG - 1)
                            ins.then_inc(dt_o, 1)
                    pe.wait_ge(dt_pt, C * (o + 1))
                    pe.wait_ge(dt_out, OCT * (o + 1))
                out_pe(round_, 24, oT, lambda kc: None, 2)

            pe.wait_ge(const_in, 16)
            pe.wait_ge(start_in, 16 * START_DMAS)
            pe.wait_ge(zeroed, 1)
            mm(bank[0][0:AH, 0:TAB], rb1, pick[:, 0, :], start=True, stop=True)
            for g in range(DG):
                ins = mm(bank[1 + g][0:DH, 0:TAB], rb2[:, g * DH:(g + 1) * DH], pick[:, 1 + g, :], start=True, stop=True)
            ins.then_inc(start_pe, 1)
            pe.wait_ge(start_dve, 1)
            pe.wait_ge(start_act, 2)
            with pe.Fori(0, layers) as l:
                for j in subs:
                    r, m = l * LAYER1 + START1[j], sub1(l, j)
                    mod_pe(r, m, 0)
                    turn_pe(m, x, rows_ready, ST * m)
                    if j == 1:
                        mix_pe(r, m, l)
                    else:
                        ffn_pe(r, m, 2 * l + j // 2)
            for n in subs2:
                i, j = divmod(n, N_SUB)
                r, m = START2[n], M2 + n
                if n == 0:
                    pe.wait_ge(start_dve, 2)
                mod_pe(r, m, 1)
                turn_pe(m, z, normed, ST * n)
                if j != 1:
                    ffn_pe(r, m, 2 * DEPTH + 2 * i + j // 2)
                elif i == 0:
                    mla_pe(r, m)
                else:
                    dil_pe(r, m)

        @block.scalar
        def _(act):
            on = nc.scalar.activation
            IDENT, COPY = ACT.Identity, ACT.Copy
            links = Links(act, act_link)

            def mod_act(round_, m, one):
                act.wait_ge(units_done, freed(round_, 3))
                act.wait_ge(mod_cols_done, m + 1)
                on(mod_rows[:, :], bank[0][:, :], COPY).then_inc(mod_rows_out, 1)
                act.wait_ge(units_done, freed(round_, 5))
                act.wait_ge(y_read, 4 * (m + 1))
                for h in range(2):
                    ins = on(gate[:, h * HALF:(h + 1) * HALF], bank[2 + h][:, :], COPY, bias=one)
                ins.then_inc(gate_out, 1)

            def turn_act(m):
                act.wait_ge(mod_cols_out, m + 1)
                for k in (0, 2):
                    act.wait_ge(turned, 4 * m + k + 1)
                    for c in (2 * k, 2 * k + 1):
                        ins = on(hT[:, c, :], bank[4 + k][:, (c % 2) * S:(c % 2) * S + S], IDENT,
                                 bias=mod_cols[:, 0, c:c + 1], scale=mod_cols[:, 1, c:c + 1])
                    ins.then_inc(h_act, 1)

            def post1_act(m):
                for t in range(ST):
                    act.wait_ge(nmr_done, ST * m + t + 1)
                    on(z[:, t, :], z[:, t, :], IDENT, bias=nmr[:, t:t + 1], scale=rstd[:, t:t + 1]).then_inc(norm_done, 1)

            def ffn_act(round_, f):
                def unit(u, i=0):
                    for q in range(2):
                        t = 2 * u + q
                        if q == 0:
                            act.wait_ge(in_done, IN_UNITS * f + SLOTS * i + u + 1)
                        else:
                            act.wait_ge(units_done, freed(round_ + i, MOD_UNITS + u))
                        act.wait_ge(tile_done, 4 + FT * f + 2 * SLOTS * i + t - 1)
                        on(silu[:, t % 2, :], bank[t % 4][:, 0:S], ACT.Silu).then_inc(silu_done, 1)

                with act.Fori(0, IN_UNITS // SLOTS) as i:
                    for u in range(SLOTS):
                        unit(u, i)
                for u in range(IN_UNITS // SLOTS * SLOTS, IN_UNITS):
                    unit(u)

            def mix_act(round_, l):
                act.wait_ge(tab_out, 64)
                dests = ([(aT[:, i, :], COPY, 1.0) for i in range(2)] + [(qT[:, i, :], COPY, 1.0) for i in range(2)]
                         + [(kT[:, i, :], COPY, 1.0) for i in range(2)] + [(v_rows[:, i, :], COPY, 1.0) for i in range(2)]
                         + [(qiT[:, i, :], COPY, 1.0) for i in range(4)] + [(kiT, COPY, 1.0)]
                         + [(wi[:, i, :], COPY, 1.0) for i in range(2)] + [(hq[:, i, :], ACT.Silu, 1.0) for i in range(4)]
                         + [(sg[:, i, :], ACT.Silu, 1.0) for i in range(4)] + [(vrows[:, i, :], COPY, 1.0) for i in range(2)]
                         + [(key[:, i, :], ACT.Sigmoid, -1.0) for i in range(4)]
                         + [(gates[:, i, :], COPY, 1.0) for i in range(24)])
                for i, (u, rows, c0, n, tt, last) in enumerate(TILES):
                    if last:
                        act.wait_ge(units_done, freed(round_, u))
                    else:
                        act.wait_ge(px_done, MID * l + MID_AT[i])
                    dst, func, scale = dests[i]
                    on(dst, bank[i % 4][:, 0:n if rows else S], func, scale=scale).then_inc(px_out, 1)
                act.wait_ge(pool_done, l + 1)
                for t in range(2):
                    ins = on(y[:, t, :], bank[4][:, t * S:(t + 1) * S], COPY, scale=layer_cols[:, t:t + 1])
                ins.then_inc(ya_out, 1)
                for n in range(ST * IDX_H):
                    ns = (n // IDX_H + 1) * P
                    act.wait_ge(ix_done, 16 * l + n + 1)
                    if n >= 2:
                        act.wait_ge(ix_used, 16 * l + n - 1)
                    on(relu[:, n % 2, 0:ns], bank[n % 4][:, 0:ns], ACT.Relu).then_inc(ix_relu, 1)

                def exp(c):
                    ns = (c % ST + 1) * P
                    act.wait_ge(at_ready, 8 * l + c + 1)
                    on(lg[:, c % 2, 0:ns], lg[:, c % 2, 0:ns], ACT.Exp, bias=small[:, 8 + c % 2:9 + c % 2],
                       accum_out=small[:, 16 + c % 2:17 + c % 2]).then_inc(at_exp, 1)

                exp(0)
                for c in range(AH * ST):
                    h, qt = divmod(c, ST)
                    if c + 1 < AH * ST:
                        exp(c + 1)
                    act.wait_ge(at_t, 8 * l + c + 1)
                    pt = pT[:, h % 2, :].rearrange("p (k q) -> p k q", k=ST)
                    if qt == 0 and h >= 2:
                        act.wait_ge(at_o, AH * l + h - 1)
                    on(pt[:, 0:qt + 1, qt * P:(qt + 1) * P],
                       bank[6 + c % 2][:, 0:(qt + 1) * P].rearrange("p (k q) -> p k q", q=P), COPY).then_inc(at_pt, 1)
                    if qt == 1:
                        b = 64 * (h % 2)
                        act.wait_ge(at_o, AH * l + h + 1)
                        on(y[b:b + 64, 2 + h // 2, :], bank[h // 2][b:b + 64, 0:S], COPY).then_inc(at_out, 1)
                act.wait_ge(vt_done, l + 1)
                for h in range(HH):
                    ins = on(vt[:, h, :], bank[4 + h // 2][:, (h % 2) * S:(h % 2) * S + S], COPY)
                ins.then_inc(vt_out, 1)
                act.wait_ge(h_f, l + 1)
                on(aa[:, :, :], ff[:, :, :], ACT.Ln).then_inc(h_ln, 1)
                act.wait_ge(h_scan, l + 1)
                on(qa[:, :, :], decay[:, :, :], ACT.Exp)
                on(eal[:, :], refs[:, :, NSB], ACT.Exp)
                on(qd[:, :, :], qd[:, :, :], ACT.Exp).then_inc(h_ea, 1)
                for i in range(1, NSB + 1):
                    act.wait_ge(kr_arg, NSB * l + i)
                    kr = (kr0, kr1)[i % 2][:, :, :].rearrange("p h (c s) -> p (h c) s", s=CHUNK)[:, :, 0:SUB * i]
                    on(kr, kr, ACT.Exp).then_inc(kr_exp, 1)
                act.wait_ge(kd_done, l + 1)
                for t in range(ST):
                    ins = on(kd_rows[:, t, :], bank[2 + t][:, :], COPY)
                ins.then_inc(kd_out, 1)
                act.wait_ge(kr_used, (NSB - 1) * (l + 1))
                for b in (0, CHUNK):
                    src = bank[4][b:b + CHUNK, :].rearrange("p (h t q) -> p h t q", h=HH, t=ST)
                    dst = scoreT[b:b + CHUNK, :, :].rearrange("p h (t c q) -> p h t c q", t=ST, c=2)[:, :, :, b // CHUNK, :]
                    ins = on(dst[:, :, :, SUB:], src[:, :, :, SUB:], COPY)
                ins.then_inc(sc_out, 1)
                act.wait_ge(ho_sum, l + 1)
                on(tm0[:, :, :], ob[:, :, :], ACT.Square).then_inc(ho_sq, 1)
                on(gates[:, :, :], gates[:, :, :], ACT.Sigmoid).then_inc(gates_out, 1)

            act.wait_ge(start_in, 16 * START_DMAS)
            on(cond[:, :, :], c_cols[:, :, :], ACT.Silu).then_inc(start_act, 1)
            act.wait_ge(lb_arg, 1)
            on(lb_tmp[:, 1:3, :], lb_tmp[:, 1:3, :], ACT.Exp).then_inc(lb_exp, 1)
            act.wait_ge(start_pe, 1)
            on(tab[0:AH, 0, :], bank[0][0:AH, 0:TAB], COPY)
            for g in range(DG):
                ins = on(tab[:, 1 + g, :], bank[1 + g][0:DH, 0:TAB], COPY)
            ins.then_inc(start_act, 1)
            with act.Fori(0, layers) as l:
                for j in subs:
                    r, m = l * LAYER1 + START1[j], sub1(l, j)
                    mod_act(r, m, 1.0)
                    turn_act(m)
                    if j == 1:
                        mix_act(r, l)
                    else:
                        ffn_act(r, 2 * l + j // 2)
                    post1_act(m)

            V1 = ST * M2

            def pre2_act(n):
                for t in range(ST):
                    act.wait_ge(rows_ready, ST * (M2 + n) + t + 1)
                    on(z[:, t, :], x[:, t, :], ACT.Square, accum_out=sq[:, t, 0:1]).then_inc(sq_done, 1)
                for t in range(ST):
                    act.wait_ge(inv_done, V1 + 4 * n + t + 1)
                    act.wait_ge(sq_done, 6 * n + 2)
                    on(z[:, t, :], x[:, t, :], COPY, scale=rstd[:, t:t + 1]).then_inc(normed, 1)

            def post2_act(n, after):
                act.wait_ge(units_done, after)
                for t in range(ST):
                    for h in range(2):
                        on(z[:, t, h * HALF:(h + 1) * HALF], bank[4 + 2 * t + h][:, :], ACT.Square,
                           accum_out=sq[:, t, h:h + 1]).then_inc(sq_done, 1)

            def mla_act(round_):
                dests = ([cq[:, i, :] for i in range(3)] + [ck[:, i, :] for i in range(2)] + [kr]
                         + [qn[:, i, :] for i in range(8)] + [qr[:, i, :] for i in range(4)] + [kn[:, i, :] for i in range(8)]
                         + [v_mla[:, i // 2, (i % 2) * HALF:(i % 2 + 1) * HALF] for i in range(4)])
                mid = 0
                for t, dst in enumerate(dests):
                    if t in (2, 5, 17, 29):
                        act.wait_ge(units_done, freed(round_, {2: 6, 5: 7, 17: 10, 29: 11}[t]))
                    else:
                        mid += 1
                        act.wait_ge(ml_done, mid)
                    on(dst, bank[t % 4][:, 0:HALF if t >= 26 else S], COPY).then_inc(ml_out, 1)
                    if t == 5:
                        act.wait_ge(ml_out, 6)
                        on(lat_sq[:, 0:3, :], cq, ACT.Square)
                        on(lat_sq[:, 3:5, :], ck, ACT.Square).then_inc(ml_sq, 1)

                def exp(c):
                    ns = (c % ST + 1) * P
                    act.wait_ge(mt_ready, c + 1)
                    on(lg_m[:, c % 2, 0:ns], lg_m[:, c % 2, 0:ns], ACT.Exp, bias=small[:, 8 + c % 2:9 + c % 2],
                       accum_out=small[:, 16 + c % 2:17 + c % 2]).then_inc(mt_exp, 1)

                exp(0)
                for c in range(MH * ST):
                    h, qt = divmod(c, ST)
                    if c + 1 < MH * ST:
                        exp(c + 1)
                    act.wait_ge(mt_t, c + 1)
                    pt = pT_m[:, h % 2, :].rearrange("p (k q) -> p k q", k=ST)
                    if qt == 0 and h >= 2:
                        act.wait_ge(mt_o, h - 1)
                    on(pt[:, 0:qt + 1, qt * P:(qt + 1) * P],
                       bank[6 + c % 2][:, 0:(qt + 1) * P].rearrange("p (k q) -> p k q", q=P), COPY).then_inc(mt_pt, 1)
                    if qt == 1:
                        b = 64 * (h % 2)
                        act.wait_ge(mt_o, h + 1)
                        on(oT[b:b + 64, h // 2, :], bank[(h // 2) % 2][b:b + 64, 0:S], COPY).then_inc(mt_out, 1)

            def dil_act(round_):
                mid = 0
                C = OCT * ST
                for o in range(2):
                    t = 0
                    for u in range(3 * DG):
                        g, kind = divmod(u, 3)
                        tiles = 2 if kind == 2 else 4
                        for q in range(tiles):
                            if q == tiles - 1:
                                act.wait_ge(units_done, freed(round_, MOD_UNITS + 9 * o + u))
                            else:
                                mid += 1
                                act.wait_ge(dx_done, mid)
                            dst = dv[:, g, q, :] if kind == 2 else (dq, dk)[kind][:, g, q, :]
                            on(dst, bank[t % 4][:, 0:HALF if kind == 2 else S], COPY).then_inc(dx_out, 1)
                            t += 1

                    def exp(c):
                        ns = (c % ST + 1) * P * DG
                        act.wait_ge(dt_ready, C * o + c + 1)
                        on(lg_d[:, c % 2, 0:ns], lg_d[:, c % 2, 0:ns], ACT.Exp, bias=small[:, 8 + c % 2:9 + c % 2],
                           accum_out=small[:, 16 + c % 2:17 + c % 2]).then_inc(dt_exp, 1)

                    exp(0)
                    for c in range(C):
                        h, qt = divmod(c, ST)
                        if c + 1 < C:
                            exp(c + 1)
                        act.wait_ge(dt_t, C * o + c + 1)
                        pt = pT_d[:, h % 2, :].rearrange("p (g k q) -> p g k q", g=DG, k=ST)
                        if qt == 0 and OCT * o + h >= 2:
                            act.wait_ge(dt_o, OCT * o + h - 1)
                        if qt == 0:
                            ins = on(pt[:, :, 0, 0:P], bank[2][:, 0:DG * P].rearrange("p (g q) -> p g q", q=P), COPY)
                        else:
                            for g in range(DG):
                                ins = on(pt[:, g, :, P:S], bank[2 + g // 2][:, (g % 2) * S:(g % 2) * S + S]
                                         .rearrange("p (k q) -> p k q", q=P), COPY)
                        ins.then_inc(dt_pt, 1)
                        if qt == 1:
                            b = 64 * (h % 2)
                            act.wait_ge(dt_o, OCT * o + h + 1)
                            on(oT[b:b + 64, 4 * o + h // 2, :], bank[(h // 2) % 2][b:b + 64, 0:S], COPY).then_inc(dt_out, 1)

            for n in subs2:
                i, j = divmod(n, N_SUB)
                r, m = START2[n], M2 + n
                pre2_act(n)
                mod_act(r, m, 0.0)
                turn_act(m)
                if j != 1:
                    ffn_act(r, 2 * DEPTH + 2 * i + j // 2)
                elif i == 0:
                    mla_act(r)
                else:
                    dil_act(r)
                post2_act(n, freed(r, (23, 15, 23, 23, 27, 23)[n]))

        @block.vector
        def _(dve):
            V = nc.vector
            k = Links(dve, dve_link)
            MUL, ADD, SUBT = ALU.mult, ALU.add, ALU.subtract

            def turn_dve(m, blk, n=0):
                dve.wait_ge(mod_cols_done, m + 2)
                src = bank[1][:, 0:16].rearrange("p (c two h) -> p two h c", two=2, h=2)
                V.tensor_copy(mod_cols[:, 0, :].rearrange("p (h c) -> p h c", h=2), src[:, 0])
                ins = V.tensor_scalar(mod_cols[:, 1, :].rearrange("p (h c) -> p h c", h=2), src[:, 1], 1.0, None, ADD)
                if blk:
                    k.link(ins)
                    ins = V.tensor_tensor(mod_cols[:, 1, :], mod_cols[:, 1, :], pre_cols[:, n, :], MUL)
                ins.then_inc(mod_cols_out, 1)
                dve.wait_ge(mod_cols_out, m + 1)
                for q in (1, 3):
                    dve.wait_ge(turned, 4 * m + q + 1)
                    for c in (2 * q, 2 * q + 1):
                        ins = V.tensor_scalar(hT[:, c, :], bank[4 + q][:, (c % 2) * S:(c % 2) * S + S],
                                              mod_cols[:, 1, c:c + 1], mod_cols[:, 0, c:c + 1], MUL, ADD)
                    ins.then_inc(h_dve, 1)

            def ffn_dve(f):
                def tile(t, i=0):
                    dve.wait_ge(silu_done, FT * f + 2 * SLOTS * i + t + 1)
                    V.tensor_tensor(act_t[:, bass.ds(2 * SLOTS * i + t, 1), :], silu[:, t % 2:t % 2 + 1, :],
                                    bank[t % 4][:, S:2 * S].unsqueeze(1), MUL).then_inc(tile_done, 1)

                with dve.Fori(0, IN_UNITS // SLOTS) as i:
                    for t in range(2 * SLOTS):
                        tile(t, i)
                for t in range(IN_UNITS // SLOTS * 2 * SLOTS, FT):
                    tile(t)

            def post1_dve(m, after, res):
                dve.wait_ge(units_done, after)
                dve.wait_ge(gate_out, m + 1)
                for t in range(ST):
                    for h in range(2):
                        V.scalar_tensor_tensor(z[:, t, h * HALF:(h + 1) * HALF], bank[4 + 2 * t + h][:, :], res,
                                               gate[:, h * HALF:(h + 1) * HALF], MUL, MUL).then_inc(y_read, 1)
                dve.wait_ge(y_read, 4 * (m + 2))
                for t in range(ST):
                    k.link(V.scalar_tensor_tensor(z[:, t, :], x[:, t, :], ALPHA, z[:, t, :], MUL, ADD))
                    for h in range(2):
                        ins = V.bn_stats(stat[:, t, h, :], z[:, t, h * HALF:(h + 1) * HALF])
                    k.link(ins)
                    V.memset(carrier[:, :], 0.0)
                    k.link(V.bn_aggr(mv[:, t, :], stat[:, t, :, :]))
                    V.tensor_scalar(ms[:, t:t + 1], mv[:, t, 1:2], LN_EPS, None, ADD).then_inc(var_done, 1)
                for t in range(ST):
                    dve.wait_ge(inv_done, ST * m + t + 1)
                    V.scalar_tensor_tensor(nmr[:, t:t + 1], mv[:, t, 0:1], -1.0, rstd[:, t:t + 1], MUL, MUL).then_inc(nmr_done, 1)
                dve.wait_ge(post_in, 32 * (m + 1))
                for t in range(ST):
                    dve.wait_ge(norm_done, ST * m + t + 1)
                    k.link(V.tensor_tensor(z[:, t, :], z[:, t, :], post_g[:, :], MUL))
                    V.tensor_tensor(x[:, t, :], z[:, t, :], post_b[:, :], ADD).then_inc(rows_ready, 1)

            def mix_dve(round_, l):
                k.link(V.tensor_copy(oml_l[:, :], oml[:, bass.ds(l, 1), :].squeeze(1)))
                dve.wait_ge(px_out, NT * l + 2)
                s0, s1 = sums

                def double(dst, src, w, t0=0):
                    V.tensor_copy(dst[:, t0:2, 0:w], src[:, t0:2, 0:w])
                    k.link(V.tensor_tensor(dst[:, t0:2, w:S], src[:, t0:2, w:S], src[:, t0:2, 0:S - w], ADD))

                def mean(t, b, src):
                    p = slice(b, b + 64)
                    k.link(V.tensor_tensor(src[p, t, :], src[p, t, :], invcnt[p, t, :], MUL))
                    k.link(V.tensor_tensor(src[p, t, :], src[p, t, :], aT[p, t, :], SUBT))
                    return p, t, src

                dve.wait_ge(layer_in, 16 * 7 * (l + 1))
                double(s0, aT, 1)
                double(s1, s0, 2)
                done = [mean(0, 0, s0), mean(0, 64, s1)]
                double(s0, s1, 4, 1)
                double(s1, s0, 8, 1)
                done += [mean(1, 0, s0), mean(1, 64, s1)]
                for p, t, src in done:
                    ins = V.tensor_copy(aT[p, t, :], src[p, t, :])
                ins.then_inc(pool_d, 1)
                dve.wait_ge(px_out, NT * l + 15)
                for n in range(ST * IDX_H):
                    qt, h = divmod(n, IDX_H)
                    ns = (qt + 1) * P
                    dve.wait_ge(ix_relu, 16 * l + n + 1)
                    w = wi[:, qt, h:h + 1]
                    if h == 0:
                        ins = V.tensor_scalar(score[:, 0:ns], relu[:, n % 2, 0:ns], w, None, MUL)
                    else:
                        ins = V.scalar_tensor_tensor(score[:, 0:ns], relu[:, n % 2, 0:ns], w, score[:, 0:ns], MUL, ADD)
                    ins.then_inc(ix_used, 1)
                    dve.wait_ge(ix_used, 16 * l + n + 1)
                    if h == IDX_H - 1:
                        if qt:
                            V.tensor_scalar(score[:, 0:P], score[:, 0:P], IDX_SCALE, None, MUL)
                        k.link(V.scalar_tensor_tensor(score[:, qt * P:ns], score[:, qt * P:ns], IDX_SCALE, causal, MUL, ADD))
                        src = score
                        for r in range(TOP_K // 8):
                            V.memset(carrier[:, :], 0.0)
                            k.link(V.max(small[:, 32:40], src[:, 0:ns]))
                            V.memset(carrier[:, :], 0.0)
                            k.link(V.match_replace(work[:, 0:ns], small[:, 32:40], src[:, 0:ns], PICKED))
                            src = work
                        k.link(V.tensor_scalar(addm[:, qt, 0:ns], work[:, 0:ns], PICKED / 2, MASKED, ALU.is_gt, MUL))

                dve.wait_ge(table_in, 16)

                def logits(c):
                    h, qt = divmod(c, ST)
                    ns = (qt + 1) * P
                    dve.wait_ge(at_s, 8 * l + c + 1)
                    if c >= 2:
                        dve.wait_ge(at_t, 8 * l + c - 1)
                    out_ = lg[:, c % 2, 0:ns]
                    V.scalar_tensor_tensor(out_, bank[4 + c % 2][:, 0:ns], 64 ** -0.5, table1[:, h, S - ns:S], MUL, ADD)\
                     .then_inc(at_read, 1)
                    dve.wait_ge(at_read, 8 * l + c + 1)
                    k.link(V.tensor_tensor(out_, out_, addm[:, qt, 0:ns], ADD))
                    k.link(V.reduce_max(small[:, c % 2:c % 2 + 1], out_, axis=AXX))
                    V.tensor_scalar(small[:, 8 + c % 2:9 + c % 2], small[:, c % 2:c % 2 + 1], -1.0, None, MUL).then_inc(at_ready, 1)

                def probs(c):
                    ns = (c % ST + 1) * P
                    dve.wait_ge(at_exp, 8 * l + c + 1)
                    k.link(V.reciprocal(small[:, 24 + c % 2:25 + c % 2], small[:, 16 + c % 2:17 + c % 2]))
                    V.tensor_scalar(lg[:, c % 2, 0:ns], lg[:, c % 2, 0:ns], small[:, 24 + c % 2:25 + c % 2], None, MUL)\
                     .then_inc(at_p, 1)

                logits(0)
                for c in range(AH * ST):
                    if c + 1 < AH * ST:
                        logits(c + 1)
                    probs(c)
                dve.wait_ge(px_out, NT * l + 29)
                for h in range(HH):
                    ins = V.tensor_scalar(key[:, h, :], key[:, h, :], oml_l[:, h:h + 1], None, MUL)
                k.link(ins)
                k.link(V.tensor_scalar(ff[:, :, :], key[:, :, :], KEY_MAX, -1.0, ALU.min, MUL))
                V.tensor_scalar(ff[:, :, :], ff[:, :, :], 1.0, None, ADD).then_inc(h_f, 1)
                dve.wait_ge(h_f, l + 1)
                dve.wait_ge(at_o, AH * (l + 1))
                dve.wait_ge(pool_done, l + 1)

                def blocks(t, lo, hi):
                    return t[:, :, :].rearrange("p h (b s) -> p (h b) s", s=SUB)[:, :, lo:hi]

                def band(dt):
                    g = (gb0, gb1)[dt % 2]
                    if dt >= 2:
                        dve.wait_ge(band_mm, 2 * (SUB * l + dt - 1))
                    if dt == 0:
                        V.tensor_copy(qb[:, :, :], hq[:, :, :])
                        ins = V.tensor_tensor(g[:, :, :], hq[:, :, :], key[:, :, :], MUL)
                    else:
                        k.link(V.tensor_tensor(blocks(qb, dt, SUB), blocks(qb, dt, SUB), blocks(ff, 1, SUB - dt + 1), MUL))
                        ins = V.tensor_tensor(blocks(g, dt, SUB), blocks(qb, dt, SUB), blocks(key, 0, SUB - dt), MUL)
                    ins.then_inc(band_g, 1)

                band(0)
                dve.wait_ge(vt_out, l + 1)
                for dt in range(SUB):
                    if dt + 1 < SUB:
                        dve.wait_ge(band_g, SUB * l + dt + 1)
                        band(dt + 1)
                    w = SUB - dt
                    for q in range(2):
                        dve.wait_ge(band_mm, 2 * (SUB * l + dt) + q + 1)
                        n = 2 * S // SUB
                        gs = bank[2 * (dt % 2) + q][:, 0:n * w].rearrange("p (b s) -> p b s", s=w)
                        dst = ob if dt == 0 else tm0
                        V.tensor_tensor(blocks(dst, 0, w)[:, q * n:(q + 1) * n], gs,
                                        blocks(vt, 0, w)[:, q * n:(q + 1) * n], MUL).then_inc(band_read, 1)
                    dve.wait_ge(band_read, 2 * (SUB * l + dt + 1))
                    if dt:
                        k.link(V.tensor_tensor(blocks(ob, dt, SUB), blocks(ob, dt, SUB), blocks(tm0, 0, w), ADD))

                dve.wait_ge(h_ln, l + 1)
                for h in range(HH):
                    V.tensor_tensor_scan(decay[:, h, :], cst("reset64"), aa[:, h, :], 0.0, MUL, ADD)
                    ins = V.tensor_tensor_scan(qd[:, h, :], cst("reset8"), aa[:, h, :], 0.0, MUL, ADD)
                k.link(ins)
                for kr in (kr0, kr1):
                    V.memset(kr[:, :, :], 0.0)
                V.memset(scoreT[:, :, :], 0.0)
                a_hc = decay[:, :, :].rearrange("p h (c s) -> p (h c) s", s=CHUNK)
                ins = V.tensor_copy(refs[:, :, 1:NSB + 1], a_hc[:, :, SUB - 1::SUB])
                ins.then_inc(h_scan, 1)
                dve.wait_ge(h_scan, l + 1)

                def kr_view(i):
                    return (kr0, kr1)[i % 2][:, :, :].rearrange("p h (c s) -> p (h c) s", s=CHUNK)[:, :, 0:SUB * i]

                def arg(i):
                    if i >= 3:
                        dve.wait_ge(kr_used, (NSB - 1) * l + i - 2)
                    V.tensor_tensor(kr_view(i), refs[:, :, i:i + 1].to_broadcast([P, HC, SUB * i]), a_hc[:, :, 0:SUB * i], SUBT)\
                     .then_inc(kr_arg, 1)

                arg(1)
                dve.wait_ge(h_ea, l + 1)
                V.tensor_tensor(qa[:, :, :], qa[:, :, :], hq[:, :, :], MUL)
                k.link(V.tensor_tensor(qd[:, :, :], qd[:, :, :], hq[:, :, :], MUL))
                key_hc = key[:, :, :].rearrange("p h (c s) -> p (h c) s", s=CHUNK)
                for i in range(1, NSB + 1):
                    if i < NSB:
                        arg(i + 1)
                    dve.wait_ge(kr_exp, NSB * l + i)
                    V.tensor_tensor(kr_view(i), kr_view(i), key_hc[:, :, 0:SUB * i], MUL).then_inc(kr_ready, 1)
                for c in range(NCH - 1):
                    dve.wait_ge(ds_done, (NCH - 1) * l + c + 1)
                    b = bank[(5, 0, 1)[c]]
                    if c == 0:
                        ins = V.tensor_copy(states[:, 0, :, :], b[:, :].rearrange("p (h v) -> p h v", h=HH))
                    else:
                        for h in range(HH):
                            ins = V.scalar_tensor_tensor(states[:, c, h, :], states[:, c - 1, h, :],
                                                         eal[:, h * NCH + c:h * NCH + c + 1], b[:, h * P:(h + 1) * P], MUL, ADD)
                    ins.then_inc(st_ready, 1)
                    dve.wait_ge(st_ready, (NCH - 1) * l + c + 1)
                dve.wait_ge(ho_done, l + 1)
                for q in range(2):
                    ins = V.tensor_tensor(ob[:, 2 * q:2 * q + 2, :], ob[:, 2 * q:2 * q + 2, :],
                                          bank[6 + q][:, :].rearrange("p (h s) -> p h s", h=2), ADD)
                ins.then_inc(ho_sum, 1)
                dve.wait_ge(ho_ss, l + 1)
                V.tensor_scalar(ms[:, 0:8], bank[2][:, 0:8], 1.0 / P, RMS_EPS, MUL, ADD).then_inc(ho_ms, 1)
                dve.wait_ge(ho_inv, l + 1)
                for h in range(HH):
                    for t in range(ST):
                        ins = V.tensor_scalar(tm1[:, h, t * P:(t + 1) * P], ident, rs[:, h * ST + t:h * ST + t + 1], None, MUL)
                ins.then_inc(ho_diag, 1)
                dve.wait_ge(ho_rep, l + 1)
                dve.wait_ge(ho_sum, l + 1)
                for q in range(2):
                    ins = V.tensor_tensor(ob[:, 2 * q:2 * q + 2, :], ob[:, 2 * q:2 * q + 2, :],
                                          bank[q][:, :].rearrange("p (h s) -> p h s", h=2), MUL)
                k.link(ins)
                for h in range(HH):
                    ins = V.scalar_tensor_tensor(y[:, 4 + h, :], ob[:, h, :], layer_cols[:, 2 + h:3 + h], sg[:, h, :], MUL, MUL)
                ins.then_inc(yc_out, 1)
                dve.wait_ge(gates_out, l + 1)
                for t in range(DC):
                    if t % 4 == 3:
                        dve.wait_ge(units_done, freed(round_, 20 + t // 4))
                    else:
                        dve.wait_ge(br_done, 6 * l + t - t // 4 + 1)
                    b = 2 * (t % 2)
                    V.tensor_tensor(tm0[:, 0, :], gates[:, t, :], bank[b][:, 0:S], MUL)
                    V.tensor_tensor(tm0[:, 1, :], gates[:, DC + t, :], bank[b][:, S:2 * S], MUL)
                    k.link(V.tensor_tensor(tm0[:, 2, :], gates[:, 2 * DC + t, :], bank[b + 1][:, 0:S], MUL))
                    k.link(V.tensor_tensor(tm0[:, 0, :], tm0[:, 0, :], tm0[:, 1, :], ADD))
                    V.tensor_tensor(hT[:, t, :], tm0[:, 0, :], tm0[:, 2, :], ADD).then_inc(merged, 1)
                    dve.wait_ge(merged, DC * l + t + 1)

            dve.wait_ge(start_in, 16 * START_DMAS)
            dve.wait_ge(zeroed, 1)
            mx, e0, e1 = lb_tmp[:, 0, :], lb_tmp[:, 1, :], lb_tmp[:, 2, :]
            k.link(V.tensor_tensor(mx, lb_cols[:, 0, :], lb_cols[:, 1, :], ALU.max))
            V.tensor_tensor(e0, lb_cols[:, 0, :], mx, SUBT)
            V.tensor_tensor(e1, lb_cols[:, 1, :], mx, SUBT).then_inc(lb_arg, 1)
            dve.wait_ge(lb_exp, 1)
            k.link(V.tensor_tensor(mx, e0, e1, ADD))
            k.link(V.reciprocal(mx, mx))
            k.link(V.tensor_tensor(e1, e1, mx, MUL))
            k.link(V.tensor_scalar(oml[:, 1, :], e1, -1.0, 1.0, MUL, ADD))
            V.memset(oml[:, 0, :], 1.0)
            dve.wait_ge(start_act, 1)
            V.tensor_copy(cond_row[:, :, :, 0:1], cond[:, :, :].unsqueeze(3))
            V.tensor_copy(cond_all[:, :, :], cond[:, 0, :].unsqueeze(2).to_broadcast([P, DC, P])).then_inc(start_dve, 1)
            dve.wait_ge(x_in, 16)
            for t in range(ST):
                V.tensor_copy(x[:, t, :], z[:, t, :]).then_inc(rows_ready, 1)
            with k.loop(layers, "dve1") as l:
                for j in subs:
                    r, m = l * LAYER1 + START1[j], sub1(l, j)
                    turn_dve(m, 0)
                    if j == 1:
                        mix_dve(r, l)
                        post1_dve(m, freed(r, 23), 1.0)
                    else:
                        ffn_dve(2 * l + j // 2)
                        post1_dve(m, freed(r, 23), 0.5)

            V1 = ST * M2

            def pre2_dve(n):
                for t in range(ST):
                    dve.wait_ge(sq_done, 6 * n + t + 1)
                    V.tensor_scalar(ms[:, t:t + 1], sq[:, t, 0:1], 1.0 / D, RMS_EPS, MUL, ADD).then_inc(var_done, 1)

            def post2_dve(n, m, res):
                for t in range(ST):
                    dve.wait_ge(sq_done, 6 * n + 4 + 2 * t)
                    k.link(V.tensor_tensor(ms[:, t:t + 1], sq[:, t, 0:1], sq[:, t, 1:2], ADD))
                    V.tensor_scalar(ms[:, t:t + 1], ms[:, t:t + 1], 1.0 / D, RMS_EPS, MUL, ADD).then_inc(var_done, 1)
                dve.wait_ge(gate2_out, n + 1)
                for t in range(ST):
                    dve.wait_ge(inv_done, V1 + 4 * n + 2 + t + 1)
                    k.link(V.tensor_scalar(nmr[:, t:t + 1], rstd[:, t:t + 1], res, None, MUL))
                    for h in range(2):
                        V.scalar_tensor_tensor(z[:, t, h * HALF:(h + 1) * HALF], bank[4 + 2 * t + h][:, :], nmr[:, t:t + 1],
                                               gate[:, h * HALF:(h + 1) * HALF], MUL, MUL).then_inc(y_read, 1)
                    dve.wait_ge(y_read, 4 * (m + 1) + 2 * t + 2)
                    V.tensor_tensor(x[:, t, :], x[:, t, :], z[:, t, :], ADD).then_inc(rows_ready, 1)

            def mla_dve():
                V.memset(mask2[:, 0:P], 0.0)
                k.link(V.tensor_copy(mask2[:, P:S], causal))
                dve.wait_ge(ml_ss, 1)
                V.tensor_scalar(ms[:, 0:2], bank[4][:, 0:2], 1.0 / Q_LORA, RMS_EPS, MUL, ADD)
                V.tensor_scalar(ms[:, 2:4], bank[4][:, 2:4], 1.0 / KV_LORA, RMS_EPS, MUL, ADD).then_inc(ml_ms, 1)
                dve.wait_ge(ml_inv, 1)
                for g in range(4):
                    ins = V.tensor_scalar(inv_diag[:, g // 2, (g % 2) * P:(g % 2 + 1) * P], ident, rs[:, g:g + 1], None, MUL)
                ins.then_inc(ml_diag, 1)
                dve.wait_ge(ml_rep, 1)
                for c in range(5):
                    t, g = (cq[:, c, :], 0) if c < 3 else (ck[:, c - 3, :], 1)
                    ins = V.scalar_tensor_tensor(t, t, mla_cols[:, c:c + 1], bank[5][:, g * S:(g + 1) * S], MUL, MUL)
                ins.then_inc(ml_norm, 1)
                dve.wait_ge(ml_const, 16)
                for t in range(5):
                    dve.wait_ge(rot_done, t + 1)
                    v = kr if t == 4 else qr[:, t, :]
                    V.tensor_tensor(rot, bank[t % 4][:, 0:S], sin_t, MUL)
                    k.link(V.tensor_tensor(v, v, cos_t, MUL))
                    V.tensor_tensor(v, v, rot, ADD).then_inc(rot_out, 1)
                    dve.wait_ge(rot_out, t + 1)

                def logits(c):
                    ns = (c % ST + 1) * P
                    dve.wait_ge(mt_s, c + 1)
                    if c >= 2:
                        dve.wait_ge(mt_t, c - 1)
                    V.scalar_tensor_tensor(lg_m[:, c % 2, 0:ns], bank[4 + c % 2][:, 0:ns], (NOPE + ROPE) ** -0.5,
                                           mask2[:, S - ns:S], MUL, ADD).then_inc(mt_read, 1)
                    dve.wait_ge(mt_read, c + 1)
                    k.link(V.reduce_max(small[:, c % 2:c % 2 + 1], lg_m[:, c % 2, 0:ns], axis=AXX))
                    V.tensor_scalar(small[:, 8 + c % 2:9 + c % 2], small[:, c % 2:c % 2 + 1], -1.0, None, MUL).then_inc(mt_ready, 1)

                logits(0)
                for c in range(MH * ST):
                    ns = (c % ST + 1) * P
                    if c + 1 < MH * ST:
                        logits(c + 1)
                    dve.wait_ge(mt_exp, c + 1)
                    k.link(V.reciprocal(small[:, 24 + c % 2:25 + c % 2], small[:, 16 + c % 2:17 + c % 2]))
                    V.tensor_scalar(lg_m[:, c % 2, 0:ns], lg_m[:, c % 2, 0:ns], small[:, 24 + c % 2:25 + c % 2], None, MUL)\
                     .then_inc(mt_p, 1)

            def dil_dve():
                C = OCT * ST

                def logits(n):
                    c = n % C
                    h, qt = divmod(c, ST)
                    ns = (qt + 1) * P
                    dve.wait_ge(dt_s, n + 1)
                    if n >= 2:
                        dve.wait_ge(dt_t, n - 1)
                    if qt == 0:
                        dve.wait_ge(tabs_in[h % 2], 16 * (n // ST // 2 + 1))
                    lgv = lg_d[:, c % 2, 0:DG * ns].rearrange("p (g s) -> p g s", g=DG)
                    tb = tabs[:, h % 2, :, S - ns:S]
                    b = 4 + 2 * (c % 2)
                    if qt == 0:
                        ins = V.scalar_tensor_tensor(lgv, bank[b][:, 0:DG * P].rearrange("p (g s) -> p g s", g=DG), 64 ** -0.5, tb, MUL, ADD)
                    else:
                        V.scalar_tensor_tensor(lgv[:, 0:2, :], bank[b][:, :].rearrange("p (g s) -> p g s", g=2), 64 ** -0.5,
                                               tb[:, 0:2, :], MUL, ADD)
                        ins = V.scalar_tensor_tensor(lgv[:, 2, :], bank[b + 1][:, 0:S], 64 ** -0.5, tb[:, 2, :], MUL, ADD)
                    ins.then_inc(dt_read, 1)
                    dve.wait_ge(dt_read, n + 1)
                    ins = V.reduce_max(small[:, c % 2:c % 2 + 1], lg_d[:, c % 2, 0:DG * ns], axis=AXX)
                    k.link(ins)
                    ins = V.tensor_scalar(small[:, 8 + c % 2:9 + c % 2], small[:, c % 2:c % 2 + 1], -1.0, None, MUL)
                    ins.then_inc(dt_ready, 1)

                logits(0)
                for n in range(2 * C):
                    c = n % C
                    ns = (c % ST + 1) * P * DG
                    if n + 1 < 2 * C and (n + 1) % C:
                        logits(n + 1)
                    dve.wait_ge(dt_exp, n + 1)
                    k.link(V.reciprocal(small[:, 24 + c % 2:25 + c % 2], small[:, 16 + c % 2:17 + c % 2]))
                    V.tensor_scalar(lg_d[:, c % 2, 0:ns], lg_d[:, c % 2, 0:ns], small[:, 24 + c % 2:25 + c % 2], None, MUL)\
                     .then_inc(dt_p, 1)
                    if n + 1 == C:
                        logits(C)

            if subs2:
                dve.wait_ge(units_done, freed(START2[0] - FFN_ROUNDS, MOD_UNITS - 1))
                V.tensor_copy(cond_all[:, :, :], cond[:, 1, :].unsqueeze(2).to_broadcast([P, DC, P])).then_inc(start_dve, 1)
            for n in subs2:
                i, j = divmod(n, N_SUB)
                m = M2 + n
                pre2_dve(n)
                turn_dve(m, 1, n)
                if j != 1:
                    ffn_dve(2 * DEPTH + 2 * i + j // 2)
                elif i == 0:
                    mla_dve()
                else:
                    dil_dve()
                post2_dve(n, m, (0.5, 1.0, 0.5)[j])

        @block.gpsimd
        def _(pool):
            G = nc.gpsimd

            def rows_in(m, bias, j, *vectors):
                pool.wait_ge(bias_used, MOD_UNITS * (m + 1))
                pool.dma_start(bias_rows[0:MOD_UNITS, :], bias[j * 3 * D:(j + 1) * 3 * D].rearrange("(u n) -> u n", n=HALF))\
                    .then_inc(bias_in, 16)
                pool.wait_ge(rows_ready, ST * (m + 1))
                for dst, src in vectors:
                    pool.dma_start(dst, src.unsqueeze(0).to_broadcast([P, D])).then_inc(post_in, 16)

            def invert(done, at, out_, n=1):
                pool.wait_ge(var_done, at)
                G.tensor_tensor(out_, ms[:, 0:n], neg_half[:, 0:n], ALU.pow).then_inc(done, 1)

            def post1_pool(m):
                for t in range(ST):
                    pool.wait_ge(var_done, ST * m + t + 1)
                    G.tensor_tensor(rstd[:, t:t + 1], ms[:, t:t + 1], neg_half[:, 0:1], ALU.pow).then_inc(inv_done, 1)

            pk = Links(pool, pool_link)
            pk.link(G.memset(cond_row[:, :, :, :], 0.0))
            pk.link(G.memset(pool_bd[:, :, :], 0.0))
            pk.link(G.memset(bias_rows[:, :], 0.0))
            pk.link(G.memset(neg_half[:, :], -0.5))
            pk.link(G.memset(rb1[32:33, :], MASKED))
            pk.link(G.memset(rb2[32:33, :], MASKED))
            G.memset(sq[:, :, :], 0.0).then_inc(units_done, SLOTS)
            pool.wait_ge(units_done, SLOTS)
            for s, first in ((tile_done, 4), (y_read, 4), (mod_cols_done, 1), (bias_used, MOD_UNITS)):
                G.memset(nmr[:, :], 0.0).then_inc(s, first)
                pool.wait_ge(s, first)
            G.memset(lb_tmp[:, :, :], 0.0).then_inc(zeroed, 1)
            pool.wait_ge(zeroed, 1)

            small_loads = [(z[:, :, :], a["x"][0].rearrange("(t p) d -> p t d", p=P), x_in)]
            for dst, src, s in small_loads:
                pool.dma_start(dst, src).then_inc(s, 16)
            pool.dma_start(const[:, :], a["const"][:, 0:KEPT_COLS]).then_inc(const_in, 16)
            loads = [(c_cols[:, 0, :], a["c"][0].rearrange("(kc p) -> p kc", p=P)),
                     (c_cols[:, 1, :], a["c_2"][0].rearrange("(kc p) -> p kc", p=P)),
                     (pick, a["pick"]),
                     (rb1[0:32, :], a["rel_bias"]),
                     (rb2[0:32, :], a["rel_bias_2"])]
            for l in range(DEPTH):
                loads.append((lb_cols[:, l, :], a["hgrn_lb"][l].rearrange("(h p) -> p h", p=P)))
            for i in range(DEPTH * N_SUB):
                loads.append((pre_cols[:, i, :], a["norm_pre_2"][i // N_SUB, i % N_SUB].rearrange("(c p) -> p c", p=P)))
            loads.append((mla_cols[:, 0:3], a["mla_q_norm_2"][0].rearrange("(c p) -> p c", p=P)))
            loads.append((mla_cols[:, 3:5], a["mla_kv_norm_2"][0].rearrange("(c p) -> p c", p=P)))
            assert len(loads) == START_DMAS
            for dst, src in loads:
                pool.dma_start(dst, src, allow_slow_non_contiguous=True).then_inc(start_in, 16)
            pool.wait_ge(start_act, 2)
            for row, n, g in ((0, AH, 0), (AH, DH, 1), (AH + DH, DH, 2), (AH + 2 * DH, DH, 3)):
                pool.dma_start(bias_tab[row:row + n], tab[0:n, g, :].unsqueeze(1).to_broadcast([n, P, TAB])).then_inc(tab_out, 16)
            pool.wait_ge(tab_out, 64)
            pool.dma_start(table1[:, :, :], table_src(0, AH)).then_inc(table_in, 16)
            with pool.Fori(0, layers) as l:
                for j in subs:
                    r, m = l * LAYER1 + START1[j], sub1(l, j)
                    rows_in(m, a["b_ada"][l], j, (post_g[:, :], a["ln_g"][l, j]), (post_b[:, :], a["ln_b"][l, j]))
                    if j == 1:
                        pool.dma_start(invcnt, a["const"][:, CONST["invcnt"][0]:CONST["invcnt"][1]]
                                       .rearrange("p (t s) -> p t s", t=ST)).then_inc(layer_in, 16)
                        for g in range(POOL_GROUPS):
                            b = 64 * (g % 2)
                            pool.dma_start(pool_bd[b:b + 64, g // 2, b:b + 64], a["pool_w"][l, g]).then_inc(layer_in, 16)
                        pool.dma_start(layer_cols[:, 0:2], a["pool_scale"][l].rearrange("(c p) -> p c", p=P),
                                       allow_slow_non_contiguous=True).then_inc(layer_in, 16)
                        pool.dma_start(layer_cols[:, 2:6], a["hgrn_norm_g"][l].rearrange("(c p) -> p c", p=P),
                                       allow_slow_non_contiguous=True).then_inc(layer_in, 16)
                        pool.wait_ge(ho_ms, l + 1)
                        G.tensor_tensor(rs[:, 0:8], ms[:, 0:8], neg_half[:, 0:8], ALU.pow).then_inc(ho_inv, 1)
                    post1_pool(m)

            V1, POST1 = ST * M2, 32 * M2
            for n in subs2:
                i, j = divmod(n, N_SUB)
                r, m = START2[n], M2 + n
                rows_in(m, a["b_mod_2"][i], j, (post_g[:, :], a["norm_post_2"][i, j]))
                if n == 1:
                    pool.dma_start(mla_const, a["const"][:, CONST["swap"][0]:]).then_inc(ml_const, 16)
                for t in range(ST):
                    pool.wait_ge(var_done, V1 + 4 * n + t + 1)
                    G.tensor_tensor(rstd[:, t:t + 1], ms[:, t:t + 1], neg_half[:, 0:1], ALU.pow).then_inc(inv_done, 1)
                if n == 4:
                    for h in range(DH):
                        if h >= 2:
                            pool.wait_ge(dt_read, ST * (h - 1))
                        else:
                            pool.wait_ge(h_act, 2 * m + 2)
                        src = bass.AP(bias_tab.tensor, (AH + h) * (P * TAB) + P - 1,
                                      [[TAB - 1, P], [DH * P * TAB, DG], [1, S]])
                        pool.dma_start(tabs[:, h % 2, :, :], src).then_inc(tabs_in[h % 2], 16)
                if n == 1:
                    pool.wait_ge(ml_ms, 1)
                    G.tensor_tensor(rs[:, 0:4], ms[:, 0:4], neg_half[:, 0:4], ALU.pow).then_inc(ml_inv, 1)
                pool.wait_ge(gate_out, m + 1)
                pool.wait_ge(post_in, POST1 + 16 * (n + 1))
                G.tensor_tensor(gate[:, :], gate[:, :], post_g[:, :], ALU.mult).then_inc(gate2_out, 1)
                for t in range(ST):
                    pool.wait_ge(var_done, V1 + 4 * n + 2 + t + 1)
                    G.tensor_tensor(rstd[:, t:t + 1], ms[:, t:t + 1], neg_half[:, 0:1], ALU.pow).then_inc(inv_done, 1)

    return nc


_INS = ["x", "c", "w_ada", "b_ada", "ln_g", "ln_b", "ffn_w_in", "ffn_w_out", "mix_w_in", "pool_w", "pool_scale",
        "rel_bias", "hgrn_lb", "hgrn_norm_g", "w_branch", "w_out", "c_2", "norm_pre_2", "norm_post_2", "w_mod_2",
        "b_mod_2", "ffn_w_gate_2", "ffn_w_up_2", "ffn_w_down_2", "mla_w_in_2", "mla_q_norm_2", "mla_w_q_up_2",
        "mla_kv_norm_2", "mla_w_kv_up_2", "mla_w_o_2", "dil_w_in_2", "dil_w_o_2", "rel_bias_2"]


def kernel(**inputs):
    from concourse import bacc
    from concourse.bass_utils import run_bass_kernel_spmd

    nc = bacc.Bacc("TRN2", target_bir_lowering=False, num_devices=1)
    arrays = {f"in_{name}": np.ascontiguousarray(inputs[name]) for name in _INS}
    arrays["in_const"], arrays["in_pick"] = constants(), picks()
    args = {name[3:]: nc.dram_tensor(name, v.shape, F32, kind="ExternalInput").ap() for name, v in arrays.items()}
    out = nc.dram_tensor("out_0", (1, S, D), F32, kind="ExternalOutput").ap()
    build(nc, args, out)
    result = run_bass_kernel_spmd(nc, [arrays], core_ids=[0])
    return result.results[0]["out_0"]
```

```python
from contextlib import ExitStack

import numpy as np

import concourse.bass as bass
from concourse import mybir

F32 = mybir.dt.float32
F32R = mybir.dt.float32r
ALU = mybir.AluOpType
ACT = mybir.ActivationFunctionType
AXX = mybir.AxisListType.X

P = 128
S = 256
ST = S // P
D = 1024
DC = D // P
DEPTH = 2
N_SUB = 3
F = 2816
FT = F // P
HALF = 512
ALPHA = (2 * DEPTH) ** 0.25
LN_EPS = 1e-5
RMS_EPS = 1e-6
MASKED = -1e30

SLOTS = 4
SLOT = 4096
FULL = 80
MOD_UNITS = 6
IN_COLS = 256
IN_UNITS = F // IN_COLS
OUT_KC = (4, 3, 3, 3, 3, 3, 3)
FFN_UNITS = IN_UNITS + len(OUT_KC)
FFN_ROUNDS = (MOD_UNITS + IN_UNITS + len(OUT_KC)) // SLOTS

POOL_GROUPS = 4
POOL_WIDTH = 256
POOL_WINDOWS = (2, 4, 8, 16)
AH = 4
IDX_H = 8
TOP_K = min(256, S // 4)
IDX_SCALE = 64 ** -0.5 * IDX_H ** -0.5
PICKED = -3e38
HH = 4
KEY_MAX = 1.0 - 1e-6
CHUNK = 64
NCH = S // CHUNK
SUB = 8
NSB = CHUNK // SUB
HC = HH * NCH
MIX_UNIT_COLS = (0, 512, 1024, 1536, 1608, 3144, 2632, 2120) + tuple(3656 + HALF * u for u in range(6))
MIX_ROUNDS = (MOD_UNITS + len(MIX_UNIT_COLS) + 4) // SLOTS

MH = 16
NOPE, ROPE, VH = 64, 32, 64
Q_LORA, KV_LORA = 384, 256
MLA_ROUNDS = (MOD_UNITS + 2 + 3 + 1 + 4) // SLOTS
DG = 3
DILATION = (1, 4, 16)
DSPAN = 128
DH = 16
OCT = 8
DIL_ROUNDS = (MOD_UNITS + 2 * 9 + 4) // SLOTS
TAB = 384
TABLES = AH + DG * DH

CONST = {}
CONST_COLS = 0
for _name, _cols in (("ident", P), ("ones", P), ("sel4", 4), ("selb", MOD_UNITS * P), ("causal", P),
                     ("reset64", S), ("reset8", S), ("invcnt", ST * S), ("swap", P), ("cos", S), ("sin", S)):
    if _name == "invcnt":
        KEPT_COLS = CONST_COLS
    CONST[_name] = (CONST_COLS, CONST_COLS + _cols)
    CONST_COLS += _cols


def buckets(dist, max_dist):
    d = np.maximum(dist, 1).astype(np.float32)
    large = 16 + (np.log(d / np.float32(16)) / np.float32(np.log(max_dist / 16)) * np.float32(16)).astype(np.int32)
    return np.where(dist < 16, dist, np.minimum(large, 31))


def constants():
    c = np.zeros((P, CONST_COLS), np.float32)

    def part(name, *shape):
        lo, hi = CONST[name]
        v = c[:, lo:hi]
        return v.reshape(P, *shape) if shape else v

    part("ident")[:] = np.eye(P)
    part("ones")[:] = 1.0
    for r in range(4):
        part("sel4")[32 * r, r] = 1.0
    selb = part("selb", MOD_UNITS, P)
    for r in range(4):
        selb[r, r, 0] = 1.0
    for r in range(4, 6):
        selb[r, r, :] = 1.0
    part("causal")[:] = np.where(np.arange(P)[None, :] <= np.arange(P)[:, None], 0.0, MASKED)
    part("reset64")[:] = (np.arange(S) % CHUNK != 0)
    part("reset8")[:] = (np.arange(S) % SUB != 0)
    inv = part("invcnt", ST, S)
    for g, w in enumerate(POOL_WINDOWS):
        inv[64 * (g % 2):64 * (g % 2) + 64, g // 2] = 1.0 / np.minimum(np.arange(1, S + 1), w)
    swap = part("swap")
    for h in range(4):
        for i in range(16):
            swap[32 * h + 16 + i, 32 * h + i] = -1.0
            swap[32 * h + i, 32 * h + 16 + i] = 1.0
    freqs = np.float32(10000.0) ** (-np.arange(16, dtype=np.float32) / np.float32(16))
    ang = np.arange(S, dtype=np.float32)[None, :] * freqs[:, None]
    part("cos")[:] = np.tile(np.cos(ang), (8, 1))
    part("sin")[:] = np.tile(np.sin(ang), (8, 1))
    return c


def picks():
    e = np.zeros((33, 1 + DG, TAB), np.float32)
    dist = S - 1 - np.arange(TAB)
    for g in range(1 + DG):
        dil = 1 if g == 0 else DILATION[g - 1]
        seen = dist >= 0
        if g:
            seen &= (dist % dil == 0) & (dist // dil <= DSPAN)
        b = buckets(np.maximum(dist, 0), 128 if g == 0 else 2048)
        e[np.where(seen, b, 32), g, np.arange(TAB)] = 1.0
    return e


class Links:

    def __init__(self, eng, sem):
        self.eng, self.sem, self.base, self.n = eng, sem, 0, 0

    def inc(self, ins):
        ins.then_inc(self.sem, 1)
        self.n += 1

    def wait(self):
        self.eng.wait_ge(self.sem, self.base + self.n)

    def link(self, ins):
        self.inc(ins)
        self.wait()

    def loop(self, count, name):
        return _LinkLoop(self, count, name)


class _LinkLoop:
    def __init__(self, links, count, name):
        self.links, self.count, self.name, self.per = links, count, name, LINKS[name]

    def __enter__(self):
        k = self.links
        self.kept = (k.base, k.n)
        self.fori = k.eng.Fori(0, self.count)
        i = self.fori.__enter__()
        k.base = k.base + k.n + i * self.per
        k.n = 0
        return i

    def __exit__(self, *error):
        k = self.links
        assert error[0] or k.n == self.per, f"the loop {self.name} makes {k.n} links a round, not {self.per}"
        out = self.fori.__exit__(*error)
        k.base, k.n = self.kept[0], self.kept[1] + self.count * self.per
        return out


ARENA = 21504
START_DMAS = 15
LINKS = {"dve1": 224, "ffn": 4 * SLOTS}


def build(nc, a, out):
    ctx = ExitStack()
    with ctx:
        def sb(name, shape):
            return ctx.enter_context(nc.sbuf_tensor(name, shape, F32))

        def sem(name):
            return ctx.enter_context(nc.semaphore(name))

        def sb_twice(name, shape):
            at = -(-nc.sbuf_base // 32) * 32
            return sb(name, shape), nc.alloc_sbuf_tensor_at(name + "_r", shape, F32R, offset=at)

        ring, ring_r = zip(*(sb_twice(f"ring{s}", [P, SLOT]) for s in range(SLOTS)))
        const = sb("const", [P, KEPT_COLS])
        x = sb("x", [P, ST, D])
        z, z_r = sb_twice("z", [P, ST, D])
        hT, h_lo = sb_twice("hT", [P, DC, S])
        gate = sb("gate", [P, D])
        post_g = sb("post_g", [P, D])
        post_b = sb("post_b", [P, D])
        mod_rows = sb("mod_rows", [P, HALF])
        mod_cols = sb("mod_cols", [P, 2, DC])
        bias_rows = sb("bias_rows", [P, HALF])
        c_cols = sb("c_cols", [P, 2, DC])
        cond = sb("cond", [P, 2, DC])
        cond_row = sb("cond_row", [P, 2, DC, 32])
        cond_all = sb("cond_all", [P, DC, P])
        stat = sb("stat", [P, ST, 2, 6])
        mv = sb("mv", [P, ST, 2])
        rstd = sb("rstd", [P, ST])
        nmr = sb("nmr", [P, ST])
        sq = sb("sq", [P, ST, 2])
        pre_cols = sb("pre_cols", [P, DEPTH * N_SUB, DC])
        table1 = sb("table1", [P, AH, S])
        pool_bd = sb("pool_bd", [P, 2, P])
        layer_cols = sb("layer_cols", [P, 6])
        lb_cols = sb("lb_cols", [P, DEPTH, HH])
        oml = sb("oml", [P, DEPTH, HH])
        oml_l = sb("oml_l", [P, HH])
        lb_tmp = sb("lb_tmp", [P, 3, HH])
        eal = sb("eal", [P, HC])
        small = sb("small", [P, 64])
        mla_cols = sb("mla_cols", [P, 5])
        arena, arena_r = sb_twice("arena", [P, ARENA])

        def view(at, *shape, parts=P, of=arena):
            n = int(np.prod(shape))
            assert at + n <= ARENA
            v = of[0:parts, at:at + n]
            if len(shape) == 2:
                v = v.rearrange("p (a b) -> p a b", a=shape[0])
            if len(shape) == 3:
                v = v.rearrange("p (a b c) -> p a b c", a=shape[0], b=shape[1])
            return v

        act_hi = view(0, FT, S, of=arena_r)
        act_lo = view(ARENA - FT * S, FT, S, of=arena_r)
        silu = view(FT * S, 2, S)
        h_hi = view(FT * S + 2 * S, DC, S, of=arena_r)
        W_HI0 = FT * S + 2 * S + DC * S
        w_hi = [view(W_HI0 + b * SLOT // 2, SLOT // 2, of=arena_r) for b in range(3)]
        w_hi.append(z_r[:, :, :].rearrange("p t d -> p (t d)"))
        assert W_HI0 + 3 * SLOT // 2 <= ARENA - FT * S
        pick = view(0, 1 + DG, TAB, parts=33)
        rb1 = view(1536, AH, parts=33)
        rb2 = view(1600, DG * DH, parts=33)
        tab = view(ARENA - (1 + DG) * TAB, 1 + DG, TAB, parts=DH)
        gates = view(0, 3 * DC, S)
        K0 = 3 * DC * S
        W = HH * S
        hq, sg, key, ff, aa, _, vt, ob = (view(K0 + n * W, HH, S) for n in range(8))
        vrows = view(K0 + 5 * W, ST, HH * P)
        y = z[:, :, :].rearrange("p t (c s) -> p (t c) s", s=S)
        T0 = K0 + 8 * W
        qT, kT = view(T0, 2, S), view(T0 + 512, 2, S)
        v_rows = view(T0 + 1024, ST, AH * 64)
        qiT = view(T0 + 1536, 4, S)
        kiT = view(T0 + 2560, S)
        wi = view(T0 + 2816, ST, IDX_H)
        aT = view(T0 + 2832, 2, S)
        T1 = T0 + 3344
        addm = view(T1, ST, S)
        score, work = view(T1 + 512, S), view(T1 + 768, S)
        relu = view(T1 + 1024, 2, S)
        lg = view(T1 + 1536, 3, S)
        pT = view(T1 + 2304, 2, ST * S)
        sums = [view(K0 + 7 * W, 2, S), view(K0 + 7 * W + 512, 2, S)]
        qb, gb0, gb1, tm0, tm1 = (view(T0 + n * W, HH, S) for n in range(5))
        qa, qd, kr0, kr1 = (view(T0 + n * W, HH, S) for n in range(4))
        kd_rows = view(T0 + 4 * W, ST, HH * P)
        states = view(T0 + 5 * W, NCH - 1, HH, P)
        scoreT = aa
        refs = view(T0 + 4 * W, HC, NSB + 1)
        decay = ff

        cq, ck, kr = view(0, 3, S), view(768, 2, S), view(1280, S)
        lat_sq = view(1536, 5, S)
        inv_diag = view(2816, 2, S)
        rot = view(3328, S)
        mla_const = view(3584, P + 2 * S)
        swap, cos_t, sin_t = mla_const[:, 0:P], mla_const[:, P:P + S], mla_const[:, P + S:]
        mask2 = view(4224, S)
        qn, qr = view(4480, MH // 2, S), view(6528, MH // 4, S)
        kn = view(7552, MH // 2, S)
        v_mla = view(9600, ST, MH * VH)
        pT_m, lg_m = view(12160, 2, ST * S), view(13184, 3, S)
        oT = view(15360, DC, S)
        dq, dk = view(0, DG, OCT // 2, S), view(3072, DG, OCT // 2, S)
        dv = view(6144, DG, ST, OCT * 64)
        tabs = view(9216, 2, DG, S)
        lg_d = view(17408, 3, DG * S)
        hd_hi = z_r[:, :, :].rearrange("p t (c s) -> p (t c) s", s=S)
        wd_hi = [view(at, DC, S, of=arena_r) for at in (10752, 12800, 17408, 19456)]
        pT_d = view(12288, 2, DG * ST * S)

        def cst(name, parts=P):
            lo, hi = CONST[name]
            return const[0:parts, lo:hi]

        ident, ones, sel4, causal = cst("ident"), cst("ones"), cst("sel4"), cst("causal")
        selb = cst("selb").rearrange("r (u m) -> r u m", u=MOD_UNITS)
        invcnt = aa[:, 0:2, :]
        carrier = sb("carrier", [P, 1])
        neg_half = sb("neg_half", [P, 8])
        ms = sb("ms", [P, 8])
        rs = sb("rs", [P, 8])

        bank = [ctx.enter_context(nc.psum_tensor(f"bank{b}", [P, HALF], F32)) for b in range(8)]

        bias_tab = nc.dram_tensor("bias_tab", (TABLES, P, TAB), F32, kind="Internal").ap()

        def table_src(row, n):
            return bass.AP(bias_tab.tensor, row * (P * TAB) + P - 1, [[TAB - 1, P], [P * TAB, n], [1, S]])

        ring_full = [sem(f"ring_full{s}") for s in range(SLOTS)]
        units_done = sem("units_done")
        const_in, x_in, start_in = sem("const_in"), sem("x_in"), sem("start_in")
        start_dve, start_act, start_pe = sem("start_dve"), sem("start_act"), sem("start_pe")
        lb_arg, lb_exp = sem("lb_arg"), sem("lb_exp")
        zeroed = sem("zeroed")
        tab_out, table_in = sem("tab_out"), sem("table_in")
        layer_in = sem("layer_in")
        bias_in, bias_used = sem("bias_in"), sem("bias_used")
        mod_rows_out = sem("mod_rows_out")
        mod_cols_done = sem("mod_cols_done")
        mod_cols_out = sem("mod_cols_out")
        gate_out = sem("gate_out")
        post_in = sem("post_in")
        rows_ready = sem("rows_ready")
        y_read = sem("y_read")
        turned = sem("turned")
        h_act, h_dve = sem("h_act"), sem("h_dve")
        w_hi_out, w_lo_out = sem("w_hi_out"), sem("w_lo_out")
        in_done = sem("in_done")
        silu_done = sem("silu_done")
        tile_done = sem("tile_done")
        var_done, inv_done = sem("var_done"), sem("inv_done")
        nmr_done, norm_done = sem("nmr_done"), sem("norm_done")
        sq_done = sem("sq_done")
        out_done = sem("out_done")
        dve_link, act_link, pool_link = sem("dve_link"), sem("act_link"), sem("pool_link")
        px_done, px_out = sem("px_done"), sem("px_out")
        pool_d, pool_done = sem("pool_d"), sem("pool_done")
        ya_out = sem("ya_out")
        ix_done, ix_relu, ix_used = sem("ix_done"), sem("ix_relu"), sem("ix_used")
        at_s, at_read, at_ready, at_exp = sem("at_s"), sem("at_read"), sem("at_ready"), sem("at_exp")
        at_p, at_t, at_pt, at_o, at_out = sem("at_p"), sem("at_t"), sem("at_pt"), sem("at_o"), sem("at_out")
        h_f, h_ln, h_scan, h_ea = sem("h_f"), sem("h_ln"), sem("h_scan"), sem("h_ea")
        vt_done, vt_out = sem("vt_done"), sem("vt_out")
        band_g, band_mm, band_read = sem("band_g"), sem("band_mm"), sem("band_read")
        kr_arg, kr_exp, kr_ready, kr_used = sem("kr_arg"), sem("kr_exp"), sem("kr_ready"), sem("kr_used")
        kd_done, kd_out = sem("kd_done"), sem("kd_out")
        sc_out, ds_done, st_ready, ho_done = sem("sc_out"), sem("ds_done"), sem("st_ready"), sem("ho_done")
        ho_sum, ho_sq, ho_ss = sem("ho_sum"), sem("ho_sq"), sem("ho_ss")
        ho_ms, ho_inv, ho_diag, ho_rep, yc_out = sem("ho_ms"), sem("ho_inv"), sem("ho_diag"), sem("ho_rep"), sem("yc_out")
        gates_out, br_done, merged = sem("gates_out"), sem("br_done"), sem("merged")

        normed = sem("normed")
        gate2_out = sem("gate2_out")
        ml_done, ml_out = sem("ml_done"), sem("ml_out")
        ml_sq, ml_ss, ml_ms, ml_inv = sem("ml_sq"), sem("ml_ss"), sem("ml_ms"), sem("ml_inv")
        ml_diag, ml_rep, ml_norm = sem("ml_diag"), sem("ml_rep"), sem("ml_norm")
        ml_const, rot_done, rot_out = sem("ml_const"), sem("rot_done"), sem("rot_out")
        mt_s, mt_read, mt_ready, mt_exp = sem("mt_s"), sem("mt_read"), sem("mt_ready"), sem("mt_exp")
        mt_p, mt_t, mt_pt, mt_o, mt_out = sem("mt_p"), sem("mt_t"), sem("mt_pt"), sem("mt_o"), sem("mt_out")
        hd_hi_out, hd_lo_out = sem("hd_hi_out"), sem("hd_lo_out")
        wd_hi_out, wd_lo_out = sem("wd_hi_out"), sem("wd_lo_out")
        dx_done, dx_out = sem("dx_done"), sem("dx_out")
        tabs_in = [sem("tabs_in0"), sem("tabs_in1")]
        dt_s, dt_read, dt_ready, dt_exp = sem("dt_s"), sem("dt_read"), sem("dt_ready"), sem("dt_exp")
        dt_p, dt_t, dt_pt, dt_o, dt_out = sem("dt_p"), sem("dt_t"), sem("dt_pt"), sem("dt_o"), sem("dt_out")

        block = ctx.enter_context(nc.Block())
        layers = DEPTH
        subs = range(N_SUB)

        START1 = (0, FFN_ROUNDS, FFN_ROUNDS + MIX_ROUNDS)
        LAYER1 = 2 * FFN_ROUNDS + MIX_ROUNDS

        START2 = [DEPTH * LAYER1]
        for rounds in (FFN_ROUNDS, MLA_ROUNDS, FFN_ROUNDS, FFN_ROUNDS, DIL_ROUNDS):
            START2.append(START2[-1] + rounds)
        M2 = DEPTH * N_SUB
        subs2 = range(DEPTH * N_SUB)

        def freed(round_, unit):
            return SLOTS + SLOTS * round_ + unit + 1

        TILES = []
        for u, kinds in enumerate((["c"] * 4, ["c", "c", "r256", "r256"], ["c"] * 4, ["c", "r8", "r8"], ["c"] * 4,
                                   ["c"] * 4, ["r512", "r512"], ["c"] * 4) + (["c"] * 4,) * 6):
            for k, kind in enumerate(kinds):
                rows = kind[0] == "r"
                n = int(kind[1:]) if rows else P
                c0 = (0 if n == HALF else (256 if n == 256 else P)) if rows else k * P
                TILES.append((MOD_UNITS + u, rows, c0, n, k - (2 if n == 256 else 1 if n == 8 else 0) if rows else 0,
                              k == len(kinds) - 1))
        MID = sum(not t[5] for t in TILES)
        NT = len(TILES)
        PROJ = NT - 3 * DC
        GATES_IX, GATES_SEL, GATES_AT = PROJ, PROJ + 4, PROJ + 9
        GATES_HG = GATES_AT + AH * ST
        assert NT - GATES_HG == NSB - 1
        IX_PAUSE = 11

        def tile_bank(i):
            return i % 4 if i < PROJ else 2 + (i - PROJ) % 2 if i < GATES_HG else (2, 3, 0, 1, 6, 7, 5)[i - GATES_HG]

        MID_AT = [sum(not t[5] for t in TILES[:i + 1]) for i in range(NT)]

        def cols_of(slot):
            return slot[:, :].rearrange("p (kc n) -> p kc n", n=HALF)

        def half(slot, b, h, n=None):
            hi = w_hi[2 * b + h]
            if n is None:
                return *(r[slot][:, :].rearrange("p (r n) -> p r n", n=IN_COLS)[:, :, h * P:(h + 1) * P]
                         for r in (ring, ring_r)), hi.rearrange("p (r n) -> p r n", n=P)
            w = n * D // 2
            return ring[slot][:, h * w:(h + 1) * w], ring_r[slot][:, h * w:(h + 1) * w], hi[:, 0:w]

        def ffn_half(u, h):
            return half((MOD_UNITS + u) % SLOTS, u % 2, h, None if u < IN_UNITS else OUT_KC[u - IN_UNITS])

        def dil_half(u, h):
            s, c = (MOD_UNITS + u) % SLOTS, slice(h * S, (h + 1) * S)
            return (cols_of(ring[s])[:, :, c], cols_of(ring_r[s])[:, :, c], wd_hi[2 * (u % 2) + h])

        def halves(f, u, h):
            return 2 * FFN_UNITS * f + 2 * u + h + 1

        def kcn(w):
            return w.rearrange("(kc p) n -> p kc n", p=P)

        def cols(slot, kc, n):
            return ring[slot][:, 0:kc * n].rearrange("p (kc n) -> p kc n", kc=kc)

        def sub1(l, j):
            return l * N_SUB + j

        @block.sync
        def _(sp):
            def load(round_, slot, *moves):
                sp.wait_ge(units_done, SLOTS * round_ + slot + 1)
                for i, (dst, src) in enumerate(moves):
                    sp.dma_start(dst, src).then_inc(ring_full[slot], FULL - 16 * (len(moves) - 1) if i == 0 else 16)

            def load_mod(round_, m, w, bias, j):
                sp.wait_ge(bias_used, MOD_UNITS * (m + 1))
                sp.dma_start(bias_rows[0:MOD_UNITS, :], bias[j * 3 * D:(j + 1) * 3 * D].rearrange("(u n) -> u n", n=HALF))\
                  .then_inc(bias_in, 16)
                for u in range(MOD_UNITS):
                    at = (j * MOD_UNITS + u) * HALF
                    if u == 2:
                        sp.wait_ge(start_in, 16 * START_DMAS)
                    load(round_ + u // SLOTS, u % SLOTS, (cols(u % SLOTS, DC, HALF), kcn(w)[:, :, at:at + HALF]))

            def load_ffn(round_, w_gate, w_up, w_out):
                def unit(u, i=0):
                    r, s = divmod(MOD_UNITS + u, SLOTS)
                    at = (i * SLOTS + u) * IN_COLS
                    v = ring[s][:, :].rearrange("p (two kc n) -> p two kc n", two=2, kc=DC)
                    load(round_ + i + r, s,
                         (v[:, 0], kcn(w_gate)[:, :, bass.ds(at, IN_COLS)]),
                         (v[:, 1], kcn(w_up)[:, :, bass.ds(at, IN_COLS)]))

                with sp.Fori(0, IN_UNITS // SLOTS) as i:
                    for u in range(SLOTS):
                        unit(u, i)
                for u in range(IN_UNITS // SLOTS * SLOTS, IN_UNITS):
                    unit(u)
                kc = 0
                for u, n in enumerate(OUT_KC):
                    r, s = divmod(MOD_UNITS + IN_UNITS + u, SLOTS)
                    load(round_ + r, s, (cols(s, n, D), kcn(w_out)[:, kc:kc + n, :]))
                    kc += n

            def load_mix(round_, w, w_branch, w_out):
                for u, at in enumerate(MIX_UNIT_COLS):
                    r, s = divmod(MOD_UNITS + u, SLOTS)
                    if u == 3:
                        v = cols(s, DC, P + IDX_H)
                        load(round_ + r, s, (v[:, :, 0:64], kcn(w)[:, :, at:at + 64]),
                             (v[:, :, 64:P + IDX_H], kcn(w)[:, :, at:at + 64 + IDX_H]))
                    else:
                        load(round_ + r, s, (cols(s, DC, HALF), kcn(w)[:, :, at:at + HALF]))
                for h in range(2):
                    load(round_ + 5, h, (cols(h, DC, HALF), kcn(w_branch)[:, :, h * HALF:(h + 1) * HALF]))
                for h in range(2):
                    load(round_ + 5, 2 + h, (cols(2 + h, 4, D), kcn(w_out)[:, 4 * h:4 * h + 4, :]))

            sp.wait_ge(zeroed, 1)
            with sp.Fori(0, layers) as l:
                for j in subs:
                    r = l * LAYER1 + START1[j]
                    load_mod(r, sub1(l, j), a["w_ada"][l], a["b_ada"][l], j)
                    if j == 1:
                        load_mix(r, a["mix_w_in"][l], a["w_branch"][l], a["w_out"][l])
                    else:
                        w_in = a["ffn_w_in"][l, j // 2]
                        load_ffn(r, w_in[:, 0:F], w_in[:, F:2 * F], a["ffn_w_out"][l, j // 2])
            for n in subs2:
                i, j = divmod(n, N_SUB)
                r = START2[n]
                load_mod(r, M2 + n, a["w_mod_2"][i], a["b_mod_2"][i], j)
                if j != 1:
                    load_ffn(r, a["ffn_w_gate_2"][i, j // 2], a["ffn_w_up_2"][i, j // 2], a["ffn_w_down_2"][i, j // 2])
                elif i == 0:
                    w = kcn(a["mla_w_in_2"][0])
                    load(r + 1, 2, (cols(2, DC, Q_LORA), w[:, :, 0:Q_LORA]))
                    v = cols(3, DC, KV_LORA + P)
                    load(r + 1, 3, (v[:, :, 0:KV_LORA], w[:, :, Q_LORA:Q_LORA + KV_LORA]),
                         *((v[:, :, KV_LORA + 32 * g:KV_LORA + 32 * (g + 1)], w[:, :, Q_LORA + KV_LORA:]) for g in range(4)))
                    for q in range(3):
                        w = a["mla_w_q_up_2"][0][q * P:(q + 1) * P].rearrange("p (h e) -> p h e", h=MH)
                        load(r + 2, q, (ring[q][:, 0:MH * NOPE].rearrange("p (h e) -> p h e", h=MH), w[:, :, 0:NOPE]),
                             (ring[q][:, MH * NOPE:MH * (NOPE + ROPE)].rearrange("p (h e) -> p h e", h=MH), w[:, :, NOPE:]))
                    moves = []
                    for kc in range(2):
                        w = a["mla_w_kv_up_2"][0][kc * P:(kc + 1) * P].rearrange("p (h two e) -> p two h e", h=MH, two=2)
                        for g in range(2):
                            moves.append((cols(3, 4, MH * NOPE)[:, 2 * kc + g, :].rearrange("p (h e) -> p h e", h=MH), w[:, g]))
                    load(r + 2, 3, *moves)
                    for q in range(4):
                        load(r + 3, q, (cols(q, 2, D), kcn(a["mla_w_o_2"][0])[:, 2 * q:2 * q + 2, :]))
                else:
                    for u in range(2 * 3 * DG):
                        rr, s = divmod(MOD_UNITS + u, SLOTS)
                        o, gt = divmod(u, 3 * DG)
                        at = gt * D + o * OCT * 64
                        load(r + rr, s, (cols(s, DC, HALF), kcn(a["dil_w_in_2"][0])[:, :, at:at + HALF]))
                    for q in range(4):
                        load(r + 6, q, (cols(q, 2, D), kcn(a["dil_w_o_2"][0])[:, 2 * q:2 * q + 2, :]))
            sp.wait_ge(rows_ready, ST * (layers * len(subs) + len(subs2) + 1))
            sp.dma_start(out[0].rearrange("(t p) d -> p t d", p=P), x[:, :, :]).then_inc(out_done, 16)
            sp.wait_ge(out_done, 16)

        @block.tensor
        def _(pe):
            mm = nc.tensor.matmul

            def arrived(round_, unit):
                r, s = divmod(unit, SLOTS)
                pe.wait_ge(ring_full[s], (round_ + r + 1) * FULL)
                return s

            def mod_pe(round_, m, blk):
                pe.wait_ge(bias_in, 16 * (m + 1))
                for u in range(MOD_UNITS):
                    w = cols(arrived(round_, u), DC, HALF)
                    if u < 4:
                        o, lhs = bank[0][32 * u:32 * u + 32, :], cond_row[:, blk]
                    else:
                        o, lhs = bank[u - 2][:, :], cond_all
                    mm(o, selb[:, u, 0:32 if u < 4 else P], bias_rows[:, :], start=True, stop=False).then_inc(bias_used, 1)
                    for kc in range(DC):
                        ins = mm(o, lhs[:, kc, :], w[:, kc, :], start=False, stop=kc == DC - 1)
                    ins.then_inc(units_done, 1)
                pe.wait_ge(mod_rows_out, m + 1)
                for c in range(4):
                    ins = mm(bank[1][:, 4 * c:4 * c + 4], mod_rows[:, c * P:(c + 1) * P], sel4, start=True, stop=True)
                ins.then_inc(mod_cols_done, 1)

            def turn_pe(m, src, ready, base):
                for t in range(ST):
                    pe.wait_ge(ready, base + t + 1)
                    if t == 0:
                        pe.wait_ge(y_read, 4 * (m + 1))
                    for c in range(DC):
                        ins = nc.tensor.transpose(bank[4 + c // 2][:, (c % 2) * S + t * P:(c % 2) * S + (t + 1) * P],
                                                  src[:, t, c * P:(c + 1) * P], ident)
                        if t == ST - 1 and c % 2:
                            ins.then_inc(turned, 1)

            def ffn_pe(round_, m, f):
                def unit(u, i=0):
                    if u == 0:
                        pe.wait_ge(h_act, 2 * m + 2)
                        pe.wait_ge(h_dve, 2 * m + 2)
                    for q in range(2):
                        pe.wait_ge(w_lo_out, halves(f, u, q) + 2 * SLOTS * i)
                        _, lo, hi = ffn_half(u, q)
                        t = 2 * u + q
                        pe.wait_ge(tile_done, FT * f + 2 * SLOTS * i + t + 1)
                        for g in range(2):
                            o = bank[t % 4][:, g * S:(g + 1) * S]
                            for kc in range(DC):
                                r = g * DC + kc
                                mm(o, hi[:, r, :], h_hi[:, kc, :], start=kc == 0, stop=False)
                                mm(o, hi[:, r, :], h_lo[:, kc, :], start=False, stop=False)
                                ins = mm(o, lo[:, r, :], h_hi[:, kc, :], start=False, stop=kc == DC - 1)
                        ins.then_inc(in_done if q == 0 else units_done, 1)

                with pe.Fori(0, IN_UNITS // SLOTS) as i:
                    for u in range(SLOTS):
                        unit(u, i)
                for u in range(IN_UNITS // SLOTS * SLOTS, IN_UNITS):
                    unit(u)
                k0 = 0
                for u, n in enumerate(OUT_KC, IN_UNITS):
                    pe.wait_ge(tile_done, 4 + FT * f + k0 + n)
                    for q in range(2):
                        pe.wait_ge(w_lo_out, halves(f, u, q))
                        _, lo, hi = (v.rearrange("p (r n) -> p r n", n=HALF) for v in ffn_half(u, q))
                        for r in range(n):
                            kc, h = divmod(q * n + r, 2)
                            kc += k0
                            for t in range(ST):
                                a_hi, a_lo = act_hi[:, kc, t * P:(t + 1) * P], act_lo[:, kc, t * P:(t + 1) * P]
                                o = bank[4 + 2 * t + h][:, :]
                                mm(o, a_hi, hi[:, r, :], start=kc == 0, stop=False)
                                mm(o, a_hi, lo[:, r, :], start=False, stop=False)
                                ins = mm(o, a_lo, hi[:, r, :], start=False, stop=kc == FT - 1)
                    ins.then_inc(units_done, 1)
                    k0 += n

            def mix_pe(round_, m, l):
                pe.wait_ge(h_act, 2 * m + 2)
                pe.wait_ge(h_dve, 2 * m + 2)

                def tiles(i0, i1):
                    for i in range(i0, i1):
                        u, rows, c0, n, tt, last = TILES[i]
                        w = cols(arrived(round_, u), DC, P + IDX_H if u == MOD_UNITS + 3 else HALF)
                        if 4 <= i < GATES_HG:
                            pe.wait_ge(px_out, NT * l + (i - 3 if i < PROJ else i - 1))
                        o = bank[tile_bank(i)]
                        for kc in range(DC):
                            if rows:
                                ins = mm(o[:, 0:n], hT[:, kc, tt * P:(tt + 1) * P], w[:, kc, c0:c0 + n],
                                         start=kc == 0, stop=kc == DC - 1)
                            else:
                                ins = mm(o[:, 0:S], w[:, kc, c0:c0 + P], hT[:, kc, :],
                                         start=kc == 0, stop=kc == DC - 1)
                        ins.then_inc(units_done if last else px_done, 1)

                tiles(0, PROJ)
                pe.wait_ge(px_out, NT * l + PROJ)
                pe.wait_ge(layer_in, 16 * 7 * (l + 1))
                pe.wait_ge(pool_d, l + 1)
                for t in range(2):
                    ins = mm(bank[4][:, t * S:(t + 1) * S], pool_bd[:, t, :], aT[:, t, :], start=True, stop=True)
                ins.then_inc(pool_done, 1)
                for n in range(ST * IDX_H):
                    qt, h = divmod(n, IDX_H)
                    ns, b = (qt + 1) * P, 64 * (h % 2)
                    if n == IX_PAUSE:
                        tiles(GATES_IX, GATES_SEL)
                    if n >= 2:
                        pe.wait_ge(ix_relu, 16 * l + n - 1)
                    mm(bank[n % 2][:, 0:ns], qiT[b:b + 64, h // 2, qt * P:(qt + 1) * P], kiT[b:b + 64, 0:ns],
                       start=True, stop=True).then_inc(ix_done, 1)

                def scores(c):
                    h, qt = divmod(c, ST)
                    ns, b = (qt + 1) * P, 64 * (h % 2)
                    if c >= 2:
                        pe.wait_ge(at_read, 8 * l + c - 1)
                    elif c == 0:
                        pe.wait_ge(ya_out, l + 1)
                    mm(bank[4 + c % 2][:, 0:ns], qT[b:b + 64, h // 2, qt * P:(qt + 1) * P], kT[b:b + 64, h // 2, 0:ns],
                       start=True, stop=True).then_inc(at_s, 1)

                def output(h):
                    b = 64 * (h % 2)
                    pe.wait_ge(at_pt, 8 * l + ST * (h + 1))
                    if h == 0:
                        pe.wait_ge(ix_relu, 16 * (l + 1))
                    pt = pT[:, h % 2, :].rearrange("p (k q) -> p k q", k=ST)
                    o = bank[h // 2][b:b + 64, :]
                    mm(o[:, 0:S], v_rows[:, 0, h * 64:(h + 1) * 64], pt[:, 0, :], start=True, stop=False)
                    mm(o[:, P:S], v_rows[:, 1, h * 64:(h + 1) * 64], pt[:, 1, P:S], start=False, stop=True).then_inc(at_o, 1)

                scores(0)
                scores(1)
                tiles(GATES_SEL, GATES_AT)
                for c in range(AH * ST):
                    h, qt = divmod(c, ST)
                    if c + 2 < AH * ST:
                        scores(c + 2)
                    tiles(GATES_AT + c, GATES_AT + c + 1)
                    pe.wait_ge(at_p, 8 * l + c + 1)
                    if c >= 2:
                        pe.wait_ge(at_pt, 8 * l + c - 1)
                    for k in range(qt + 1):
                        ins = nc.tensor.transpose(bank[6 + c % 2][:, k * P:(k + 1) * P], lg[:, c % 3, k * P:(k + 1) * P], ident)
                    ins.then_inc(at_t, 1)
                    if qt == 0 and h:
                        output(h - 1)
                output(AH - 1)

                pe.wait_ge(at_pt, 8 * (l + 1))
                pe.wait_ge(at_read, 8 * (l + 1))
                for h in range(HH):
                    for t in range(ST):
                        ins = nc.tensor.transpose(bank[4 + h // 2][:, (h % 2) * S + t * P:(h % 2) * S + (t + 1) * P],
                                                  vrows[:, t, h * P:(h + 1) * P], ident)
                ins.then_inc(vt_done, 1)
                for dt in range(SUB):
                    g = (gb0, gb1)[dt % 2]
                    pe.wait_ge(band_g, SUB * l + dt + 1)
                    if dt >= 2:
                        pe.wait_ge(band_read, 2 * (SUB * l + dt - 1))
                    elif dt == 0:
                        pe.wait_ge(at_out, AH * (l + 1))
                        pe.wait_ge(px_out, NT * l + GATES_HG)
                    nblk, w = 2 * S // SUB, SUB - dt
                    for q in range(2):
                        gv = g[:, 2 * q:2 * q + 2, :].rearrange("p h (b s) -> p (h b) s", s=SUB)[:, :, dt:SUB]
                        ov = bank[2 * (dt % 2) + q][:, 0:nblk * w].rearrange("p (b s) -> p b s", s=w)
                        mm(ov, ones, gv, start=True, stop=True).then_inc(band_mm, 1)
                pe.wait_ge(vt_out, l + 1)
                pe.wait_ge(band_read, 2 * SUB * (l + 1))
                for i in range(1, NSB):
                    kr = (kr0, kr1)[i % 2]
                    pe.wait_ge(kr_ready, NSB * l + i)
                    for hc in range(HC):
                        h, c = divmod(hc, NCH)
                        b = CHUNK * (c % 2)
                        at = (h * 2 + c // 2) * CHUNK + SUB * i
                        ins = mm(bank[4][b:b + CHUNK, at:at + SUB], kr[:, h, c * CHUNK:(c + 1) * CHUNK],
                                 qd[:, h, c * CHUNK + SUB * i:c * CHUNK + SUB * (i + 1)], start=True, stop=True)
                    ins.then_inc(kr_used, 1)
                    tiles(GATES_HG + i - 1, GATES_HG + i)
                pe.wait_ge(kr_ready, NSB * (l + 1))
                pe.wait_ge(px_out, NT * (l + 1))
                for t in range(ST):
                    for h in range(HH):
                        ins = nc.tensor.transpose(bank[2 + t][:, h * P:(h + 1) * P], kr0[:, h, t * P:(t + 1) * P], ident)
                ins.then_inc(kd_done, 1)
                pe.wait_ge(kd_out, l + 1)
                for c in range(NCH - 1):
                    b = CHUNK * (c % 2)
                    for h in range(HH):
                        ins = mm(bank[(5, 0, 1)[c]][:, h * P:(h + 1) * P], kd_rows[b:b + CHUNK, c // 2, h * P:(h + 1) * P],
                                 vrows[b:b + CHUNK, c // 2, h * P:(h + 1) * P], start=True, stop=True)
                    ins.then_inc(ds_done, 1)
                pe.wait_ge(sc_out, l + 1)
                for t in range(ST):
                    for h in range(HH):
                        o = bank[6 + h // 2][:, (h % 2) * S:(h % 2) * S + S]
                        mm(o[:, t * P:(t + 1) * P], vrows[:, t, h * P:(h + 1) * P], scoreT[:, h, t * P:(t + 1) * P],
                           start=True, stop=False)
                        for c in ((1,), (2, 3))[t]:
                            if h == 0:
                                pe.wait_ge(st_ready, (NCH - 1) * l + c)
                            ins = mm(o[:, c * CHUNK:(c + 1) * CHUNK], states[:, c - 1, h, :], qa[:, h, c * CHUNK:(c + 1) * CHUNK],
                                     start=False, stop=c != 2)
                ins.then_inc(ho_done, 1)
                pe.wait_ge(ho_sq, l + 1)
                for h in range(HH):
                    for t in range(ST):
                        ins = mm(bank[2][:, h * ST + t:h * ST + t + 1], tm0[:, h, t * P:(t + 1) * P], ones[:, 0:1],
                                 start=True, stop=True)
                ins.then_inc(ho_ss, 1)
                pe.wait_ge(ho_diag, l + 1)
                for q in range(2):
                    ins = mm(bank[q][:, :], ones, tm1[:, 2 * q:2 * q + 2, :], start=True, stop=True)
                ins.then_inc(ho_rep, 1)
                pe.wait_ge(yc_out, l + 1)
                pe.wait_ge(at_out, AH * (l + 1))
                for u in range(2):
                    w = cols(arrived(round_, 20 + u), DC, HALF)
                    for q in range(4):
                        t = 4 * u + q
                        if t >= 2:
                            pe.wait_ge(merged, DC * l + t - 1)
                        for g, (k0, k1) in enumerate(((0, 2), (2, 4), (4, 8))):
                            o = bank[2 * (t % 2) + g // 2][:, (g % 2) * S:(g % 2) * S + S]
                            for kc in range(k0, k1):
                                ins = mm(o, w[:, kc, q * P:(q + 1) * P], y[:, kc, :], start=kc == k0, stop=kc == k1 - 1)
                        ins.then_inc(units_done if q == 3 else br_done, 1)
                out_pe(round_, 22, hT, lambda k: pe.wait_ge(merged, DC * l + k))

            def out_pe(round_, unit0, src, ready, kcs=4):
                for u in range(DC // kcs):
                    w = cols(arrived(round_, unit0 + u), kcs, D)
                    ready(kcs * (u + 1))
                    for kc in range(kcs):
                        for t in range(ST):
                            for h in range(2):
                                ins = mm(bank[4 + 2 * t + h][:, :], src[:, kcs * u + kc, t * P:(t + 1) * P],
                                         w[:, kc, h * HALF:(h + 1) * HALF], start=u + kc == 0, stop=kcs * u + kc == DC - 1)
                    ins.then_inc(units_done, 1)

            def mla_pe(round_, m):
                pe.wait_ge(h_act, 2 * m + 2)
                pe.wait_ge(h_dve, 2 * m + 2)
                w6, w7 = cols(arrived(round_, 6), DC, Q_LORA), cols(arrived(round_, 7), DC, KV_LORA + P)
                for t in range(6):
                    if t >= 4:
                        pe.wait_ge(ml_out, t - 3)
                    for kc in range(DC):
                        if t < 3:
                            lhs = w6[:, kc, t * P:(t + 1) * P]
                        else:
                            lhs = w7[:, kc, (t - 3) * P:(t - 2) * P]
                        ins = mm(bank[t % 4][:, 0:S], lhs, hT[:, kc, :], start=kc == 0, stop=kc == DC - 1)
                    ins.then_inc(units_done if t in (2, 5) else ml_done, 1)
                pe.wait_ge(ml_sq, 1)
                for g, (c0, c1) in enumerate(((0, 3), (3, 5))):
                    for t in range(ST):
                        for c in range(c0, c1):
                            ins = mm(bank[4][:, 2 * g + t:2 * g + t + 1], lat_sq[:, c, t * P:(t + 1) * P], ones[:, 0:1],
                                     start=c == c0, stop=c == c1 - 1)
                ins.then_inc(ml_ss, 1)
                pe.wait_ge(ml_diag, 1)
                mm(bank[5][:, :], ones, inv_diag, start=True, stop=True).then_inc(ml_rep, 1)
                pe.wait_ge(ml_norm, 1)
                wq = [ring[arrived(round_, 8 + q)] for q in range(3)]
                wkv = cols(arrived(round_, 11), 4, MH * NOPE)
                for t in range(24):
                    pe.wait_ge(ml_out, t + 3)
                    n = 3 if t < 12 else 2
                    for kc in range(n):
                        o = bank[(6 + t) % 4][:, 0:S]
                        if t < 12:
                            lhs, rhs = wq[kc][:, t * P:(t + 1) * P], cq[:, kc, :]
                        elif t < 20:
                            lhs, rhs = wkv[:, 2 * kc, (t - 12) * P:(t - 11) * P], ck[:, kc, :]
                        else:
                            tt, g = divmod(t - 20, 2)
                            o = bank[(6 + t) % 4][:, :]
                            lhs, rhs = ck[:, kc, tt * P:(tt + 1) * P], wkv[:, 2 * kc + 1, g * HALF:(g + 1) * HALF]
                        ins = mm(o, lhs, rhs, start=kc == 0, stop=kc == n - 1)
                    if t == 11:
                        ins.then_inc(units_done, 3)
                    elif t == 23:
                        ins.then_inc(units_done, 1)
                    else:
                        ins.then_inc(ml_done, 1)
                pe.wait_ge(ml_const, 16)
                pe.wait_ge(ml_out, 30)
                for t in range(5):
                    if t >= 4:
                        pe.wait_ge(rot_out, t - 3)
                    mm(bank[t % 4][:, 0:S], swap, kr if t == 4 else qr[:, t, :], start=True, stop=True).then_inc(rot_done, 1)
                pe.wait_ge(rot_out, 5)

                def scores(c):
                    h, qt = divmod(c, ST)
                    ns = (qt + 1) * P
                    if c >= 2:
                        pe.wait_ge(mt_read, c - 1)
                    b = 64 * (h % 2)
                    mm(bank[4 + c % 2][:, 0:ns], qn[b:b + 64, h // 2, qt * P:(qt + 1) * P], kn[b:b + 64, h // 2, 0:ns],
                       start=True, stop=False)
                    b = 32 * (h % 4)
                    mm(bank[4 + c % 2][:, 0:ns], qr[b:b + 32, h // 4, qt * P:(qt + 1) * P], kr[b:b + 32, 0:ns],
                       start=False, stop=True).then_inc(mt_s, 1)

                def output(h):
                    b = 64 * (h % 2)
                    pe.wait_ge(mt_pt, ST * (h + 1))
                    if h >= 4:
                        pe.wait_ge(mt_out, h - 3)
                    pt = pT_m[:, h % 2, :].rearrange("p (k q) -> p k q", k=ST)
                    o = bank[(h // 2) % 2][b:b + 64, :]
                    mm(o[:, 0:S], v_mla[:, 0, h * 64:(h + 1) * 64], pt[:, 0, :], start=True, stop=False)
                    mm(o[:, P:S], v_mla[:, 1, h * 64:(h + 1) * 64], pt[:, 1, P:S], start=False, stop=True).then_inc(mt_o, 1)

                scores(0)
                scores(1)
                for c in range(MH * ST):
                    h, qt = divmod(c, ST)
                    if c + 2 < MH * ST:
                        scores(c + 2)
                    pe.wait_ge(mt_p, c + 1)
                    if c >= 2:
                        pe.wait_ge(mt_pt, c - 1)
                    for kk in range(qt + 1):
                        ins = nc.tensor.transpose(bank[6 + c % 2][:, kk * P:(kk + 1) * P], lg_m[:, c % 3, kk * P:(kk + 1) * P], ident)
                    ins.then_inc(mt_t, 1)
                    if qt == 0 and h:
                        output(h - 1)
                output(MH - 1)
                pe.wait_ge(mt_pt, MH * ST)
                out_pe(round_, 12, oT, lambda kc: pe.wait_ge(mt_out, 2 * kc), 2)

            def dil_pe(round_, m):
                pe.wait_ge(hd_lo_out, 1)
                for o in range(2):
                    t = 0
                    for u in range(3 * DG):
                        tiles = 2 if u % 3 == 2 else 4
                        for q in range(4):
                            _, w_lo, hi = dil_half(3 * DG * o + u, q // 2)
                            if q % 2 == 0:
                                pe.wait_ge(wd_lo_out, 2 * (3 * DG * o + u) + q // 2 + 1)
                            at = t + q % tiles
                            if 30 * o + at >= 4 and q < tiles:
                                pe.wait_ge(dx_out, 30 * o + at - 3)
                            for kc in range(DC):
                                if tiles == 2:
                                    o_, c = bank[at % 4][:, q // 2 * S:(q // 2 + 1) * S], slice(q % 2 * P, (q % 2 + 1) * P)
                                    for i, (l_, r_) in enumerate(((hd_hi, hi), (h_lo, hi), (hd_hi, w_lo))):
                                        ins = mm(o_, l_[:, kc, c], r_[:, kc, :], start=kc + i == 0, stop=kc == DC - 1 and i == 2)
                                else:
                                    o_, c = bank[at % 4][:, 0:S], slice(q % 2 * P, (q % 2 + 1) * P)
                                    for i, (l_, r_) in enumerate(((hi, hd_hi), (hi, h_lo), (w_lo, hd_hi))):
                                        ins = mm(o_, l_[:, kc, c], r_[:, kc, :], start=kc + i == 0, stop=kc == DC - 1 and i == 2)
                            if q == 3:
                                ins.then_inc(units_done, 1)
                            elif q >= 4 - tiles:
                                ins.then_inc(dx_done, 1)
                        t += tiles
                    pe.wait_ge(dx_out, 30 * (o + 1))
                    C = OCT * ST

                    def scores(c):
                        h, qt = divmod(c, ST)
                        ns, b = (qt + 1) * P, 64 * (h % 2)
                        if C * o + c >= 2:
                            pe.wait_ge(dt_read, C * o + c - 1)
                        for g in range(DG):
                            at = g * ns
                            ins = mm(bank[4 + 2 * (c % 2) + at // HALF][:, at % HALF:at % HALF + ns],
                                     dq[b:b + 64, g, h // 2, qt * P:(qt + 1) * P], dk[b:b + 64, g, h // 2, 0:ns],
                                     start=True, stop=True)
                        ins.then_inc(dt_s, 1)

                    def output(h):
                        b = 64 * (h % 2)
                        pe.wait_ge(dt_pt, C * o + ST * (h + 1))
                        if OCT * o + h >= 2:
                            pe.wait_ge(dt_out, OCT * o + h - 1)
                        pt = pT_d[:, h % 2, :].rearrange("p (g k q) -> p g k q", g=DG, k=ST)
                        ob_ = bank[0][b:b + 64, :]
                        for g in range(DG):
                            mm(ob_[:, 0:S], dv[:, g, 0, h * 64:(h + 1) * 64], pt[:, g, 0, :], start=g == 0, stop=False)
                            ins = mm(ob_[:, P:S], dv[:, g, 1, h * 64:(h + 1) * 64], pt[:, g, 1, P:S], start=False, stop=g == DG - 1)
                        ins.then_inc(dt_o, 1)

                    scores(0)
                    scores(1)
                    for c in range(C):
                        h, qt = divmod(c, ST)
                        if c + 2 < C:
                            scores(c + 2)
                        pe.wait_ge(dt_p, C * o + c + 1)
                        if C * o + c >= 2:
                            pe.wait_ge(dt_pt, C * o + c - 1)
                        for kk in range(DG * (qt + 1)):
                            ins = nc.tensor.transpose(bank[1 + qt + kk // 4][:, kk % 4 * P:(kk % 4 + 1) * P],
                                                      lg_d[:, (C * o + c) % 3, kk * P:(kk + 1) * P], ident)
                        ins.then_inc(dt_t, 1)
                        if qt == 0 and h:
                            output(h - 1)
                    output(OCT - 1)
                    pe.wait_ge(dt_pt, C * (o + 1))
                    pe.wait_ge(dt_out, OCT * (o + 1))
                out_pe(round_, 24, oT, lambda kc: None, 2)

            pe.wait_ge(const_in, 16)
            pe.wait_ge(start_in, 16 * START_DMAS)
            pe.wait_ge(zeroed, 1)
            mm(bank[0][0:AH, 0:TAB], rb1, pick[:, 0, :], start=True, stop=True)
            for g in range(DG):
                ins = mm(bank[1 + g][0:DH, 0:TAB], rb2[:, g * DH:(g + 1) * DH], pick[:, 1 + g, :], start=True, stop=True)
            ins.then_inc(start_pe, 1)
            pe.wait_ge(start_dve, 1)
            pe.wait_ge(start_act, 2)
            with pe.Fori(0, layers) as l:
                for j in subs:
                    r, m = l * LAYER1 + START1[j], sub1(l, j)
                    mod_pe(r, m, 0)
                    turn_pe(m, x, rows_ready, ST * m)
                    if j == 1:
                        mix_pe(r, m, l)
                    else:
                        ffn_pe(r, m, 2 * l + j // 2)
            for n in subs2:
                i, j = divmod(n, N_SUB)
                r, m = START2[n], M2 + n
                if n == 0:
                    pe.wait_ge(start_dve, 2)
                mod_pe(r, m, 1)
                turn_pe(m, z, normed, ST * n)
                if j != 1:
                    ffn_pe(r, m, 2 * DEPTH + 2 * i + j // 2)
                elif i == 0:
                    mla_pe(r, m)
                else:
                    dil_pe(r, m)

        @block.scalar
        def _(act):
            on = nc.scalar.activation
            IDENT, COPY = ACT.Identity, ACT.Copy
            links = Links(act, act_link)

            def mod_act(round_, m, one):
                act.wait_ge(units_done, freed(round_, 3))
                act.wait_ge(mod_cols_done, m + 1)
                on(mod_rows[:, :], bank[0][:, :], COPY).then_inc(mod_rows_out, 1)
                act.wait_ge(units_done, freed(round_, 5))
                act.wait_ge(y_read, 4 * (m + 1))
                for h in range(2):
                    ins = on(gate[:, h * HALF:(h + 1) * HALF], bank[2 + h][:, :], COPY, bias=one)
                ins.then_inc(gate_out, 1)

            def turn_act(m, split):
                act.wait_ge(mod_cols_out, m + 1)
                for k in (0, 2):
                    act.wait_ge(turned, 4 * m + k + 1)
                    for c in (2 * k, 2 * k + 1):
                        for dst in (hT, h_hi) if split else (hT,):
                            ins = on(dst[:, c, :], bank[4 + k][:, (c % 2) * S:(c % 2) * S + S], IDENT,
                                     bias=mod_cols[:, 0, c:c + 1], scale=mod_cols[:, 1, c:c + 1])
                    ins.then_inc(h_act, 1)

            def post1_act(m):
                for t in range(ST):
                    act.wait_ge(nmr_done, ST * m + t + 1)
                    on(z[:, t, :], z[:, t, :], IDENT, bias=nmr[:, t:t + 1], scale=rstd[:, t:t + 1]).then_inc(norm_done, 1)

            def split_act(round_, u, i=0):
                r, s = divmod(MOD_UNITS + u, SLOTS)
                act.wait_ge(ring_full[s], (round_ + i + r + 1) * FULL)
                for h in range(2):
                    src, _, hi = ffn_half(u, h)
                    on(hi, src, COPY).then_inc(w_hi_out, 1)

            def ffn_act(round_, m, f):
                act.wait_ge(turned, 4 * (m + 1))
                split_act(round_, 1)

                def unit(u, i=0):
                    for q in range(2):
                        t = 2 * u + q
                        if q == 0:
                            act.wait_ge(in_done, IN_UNITS * f + SLOTS * i + u + 1)
                        else:
                            act.wait_ge(units_done, freed(round_ + i, MOD_UNITS + u))
                        act.wait_ge(tile_done, 4 + FT * f + 2 * SLOTS * i + t - 1)
                        on(silu[:, t % 2, :], bank[t % 4][:, 0:S], ACT.Silu).then_inc(silu_done, 1)
                    split_act(round_, u + 2, i)

                with act.Fori(0, IN_UNITS // SLOTS) as i:
                    for u in range(SLOTS):
                        unit(u, i)
                for u in range(IN_UNITS // SLOTS * SLOTS, IN_UNITS):
                    unit(u)
                for u in range(IN_UNITS, FFN_UNITS - 2):
                    act.wait_ge(units_done, freed(round_, MOD_UNITS + u))
                    split_act(round_, u + 2)

            def mix_act(round_, l):
                act.wait_ge(tab_out, 64)
                dests = ([(aT[:, i, :], COPY, 1.0) for i in range(2)] + [(qT[:, i, :], COPY, 1.0) for i in range(2)]
                         + [(kT[:, i, :], COPY, 1.0) for i in range(2)] + [(v_rows[:, i, :], COPY, 1.0) for i in range(2)]
                         + [(qiT[:, i, :], COPY, 1.0) for i in range(4)] + [(kiT, COPY, 1.0)]
                         + [(wi[:, i, :], COPY, 1.0) for i in range(2)] + [(hq[:, i, :], ACT.Silu, 1.0) for i in range(4)]
                         + [(sg[:, i, :], ACT.Silu, 1.0) for i in range(4)] + [(vrows[:, i, :], COPY, 1.0) for i in range(2)]
                         + [(key[:, i, :], ACT.Sigmoid, -1.0) for i in range(4)]
                         + [(gates[:, i, :], COPY, 1.0) for i in range(24)])

                def tiles(i0, i1):
                    for i in range(i0, i1):
                        u, rows, c0, n, tt, last = TILES[i]
                        if last:
                            act.wait_ge(units_done, freed(round_, u))
                        else:
                            act.wait_ge(px_done, MID * l + MID_AT[i])
                        dst, func, scale = dests[i]
                        on(dst, bank[tile_bank(i)][:, 0:n if rows else S], func, scale=scale).then_inc(px_out, 1)

                tiles(0, PROJ)
                act.wait_ge(pool_done, l + 1)
                for t in range(2):
                    ins = on(y[:, t, :], bank[4][:, t * S:(t + 1) * S], COPY, scale=layer_cols[:, t:t + 1])
                ins.then_inc(ya_out, 1)
                for n in range(ST * IDX_H):
                    ns = (n // IDX_H + 1) * P
                    if n == IX_PAUSE:
                        tiles(GATES_IX, GATES_SEL)
                    act.wait_ge(ix_done, 16 * l + n + 1)
                    if n >= 2:
                        act.wait_ge(ix_used, 16 * l + n - 1)
                    on(relu[:, n % 2, 0:ns], bank[n % 2][:, 0:ns], ACT.Relu).then_inc(ix_relu, 1)

                def exp(c):
                    ns = (c % ST + 1) * P
                    act.wait_ge(at_ready, 8 * l + c + 1)
                    on(lg[:, c % 3, 0:ns], lg[:, c % 3, 0:ns], ACT.Exp, bias=small[:, 8 + c % 3:9 + c % 3],
                       accum_out=small[:, 16 + c % 3:17 + c % 3]).then_inc(at_exp, 1)

                def output(h):
                    b = 64 * (h % 2)
                    act.wait_ge(at_o, AH * l + h + 1)
                    on(y[b:b + 64, 2 + h // 2, :], bank[h // 2][b:b + 64, 0:S], COPY).then_inc(at_out, 1)

                tiles(GATES_SEL, GATES_AT)
                exp(0)
                exp(1)
                for c in range(AH * ST):
                    h, qt = divmod(c, ST)
                    tiles(GATES_AT + c, GATES_AT + c + 1)
                    act.wait_ge(at_t, 8 * l + c + 1)
                    pt = pT[:, h % 2, :].rearrange("p (k q) -> p k q", k=ST)
                    if qt == 0 and h >= 2:
                        act.wait_ge(at_o, AH * l + h - 1)
                    on(pt[:, 0:qt + 1, qt * P:(qt + 1) * P],
                       bank[6 + c % 2][:, 0:(qt + 1) * P].rearrange("p (k q) -> p k q", q=P), COPY).then_inc(at_pt, 1)
                    if c + 2 < AH * ST:
                        exp(c + 2)
                    if qt == 0 and h:
                        output(h - 1)
                output(AH - 1)
                act.wait_ge(vt_done, l + 1)
                for h in range(HH):
                    ins = on(vt[:, h, :], bank[4 + h // 2][:, (h % 2) * S:(h % 2) * S + S], COPY)
                ins.then_inc(vt_out, 1)
                act.wait_ge(h_f, l + 1)
                on(aa[:, :, :], ff[:, :, :], ACT.Ln).then_inc(h_ln, 1)
                act.wait_ge(h_scan, l + 1)
                on(qa[:, :, :], decay[:, :, :], ACT.Exp)
                on(eal[:, :], refs[:, :, NSB], ACT.Exp)
                on(qd[:, :, :], qd[:, :, :], ACT.Exp).then_inc(h_ea, 1)
                for i in range(1, NSB + 1):
                    act.wait_ge(kr_arg, NSB * l + i)
                    kr = (kr0, kr1)[i % 2][:, :, :].rearrange("p h (c s) -> p (h c) s", s=CHUNK)[:, :, 0:SUB * i]
                    on(kr, kr, ACT.Exp).then_inc(kr_exp, 1)
                tiles(GATES_HG, NT)
                act.wait_ge(kd_done, l + 1)
                for t in range(ST):
                    ins = on(kd_rows[:, t, :], bank[2 + t][:, :], COPY)
                ins.then_inc(kd_out, 1)
                act.wait_ge(kr_used, (NSB - 1) * (l + 1))
                for b in (0, CHUNK):
                    src = bank[4][b:b + CHUNK, :].rearrange("p (h t q) -> p h t q", h=HH, t=ST)
                    dst = scoreT[b:b + CHUNK, :, :].rearrange("p h (t c q) -> p h t c q", t=ST, c=2)[:, :, :, b // CHUNK, :]
                    ins = on(dst[:, :, :, SUB:], src[:, :, :, SUB:], COPY)
                ins.then_inc(sc_out, 1)
                act.wait_ge(ho_sum, l + 1)
                on(tm0[:, :, :], ob[:, :, :], ACT.Square).then_inc(ho_sq, 1)
                on(gates[:, :, :], gates[:, :, :], ACT.Sigmoid).then_inc(gates_out, 1)

            act.wait_ge(start_in, 16 * START_DMAS)
            on(cond[:, :, :], c_cols[:, :, :], ACT.Silu).then_inc(start_act, 1)
            act.wait_ge(lb_arg, 1)
            on(lb_tmp[:, 1:3, :], lb_tmp[:, 1:3, :], ACT.Exp).then_inc(lb_exp, 1)
            act.wait_ge(start_pe, 1)
            on(tab[0:AH, 0, :], bank[0][0:AH, 0:TAB], COPY)
            for g in range(DG):
                ins = on(tab[:, 1 + g, :], bank[1 + g][0:DH, 0:TAB], COPY)
            ins.then_inc(start_act, 1)
            with act.Fori(0, layers) as l:
                for j in subs:
                    r, m = l * LAYER1 + START1[j], sub1(l, j)
                    mod_act(r, m, 1.0)
                    if j != 1:
                        split_act(r, 0)
                    turn_act(m, j != 1)
                    if j == 1:
                        mix_act(r, l)
                    else:
                        ffn_act(r, m, 2 * l + j // 2)
                    post1_act(m)

            V1 = ST * M2

            def pre2_act(n):
                for t in range(ST):
                    act.wait_ge(rows_ready, ST * (M2 + n) + t + 1)
                    on(z[:, t, :], x[:, t, :], ACT.Square, accum_out=sq[:, t, 0:1]).then_inc(sq_done, 1)
                for t in range(ST):
                    act.wait_ge(inv_done, V1 + 4 * n + t + 1)
                    act.wait_ge(sq_done, 6 * n + 2)
                    on(z[:, t, :], x[:, t, :], COPY, scale=rstd[:, t:t + 1]).then_inc(normed, 1)

            def post2_act(n, after):
                act.wait_ge(units_done, after)
                for t in range(ST):
                    for h in range(2):
                        on(z[:, t, h * HALF:(h + 1) * HALF], bank[4 + 2 * t + h][:, :], ACT.Square,
                           accum_out=sq[:, t, h:h + 1]).then_inc(sq_done, 1)

            def mla_act(round_):
                dests = ([cq[:, i, :] for i in range(3)] + [ck[:, i, :] for i in range(2)] + [kr]
                         + [qn[:, i, :] for i in range(8)] + [qr[:, i, :] for i in range(4)] + [kn[:, i, :] for i in range(8)]
                         + [v_mla[:, i // 2, (i % 2) * HALF:(i % 2 + 1) * HALF] for i in range(4)])
                mid = 0
                for t, dst in enumerate(dests):
                    if t in (2, 5, 17, 29):
                        act.wait_ge(units_done, freed(round_, {2: 6, 5: 7, 17: 10, 29: 11}[t]))
                    else:
                        mid += 1
                        act.wait_ge(ml_done, mid)
                    on(dst, bank[t % 4][:, 0:HALF if t >= 26 else S], COPY).then_inc(ml_out, 1)
                    if t == 5:
                        act.wait_ge(ml_out, 6)
                        on(lat_sq[:, 0:3, :], cq, ACT.Square)
                        on(lat_sq[:, 3:5, :], ck, ACT.Square).then_inc(ml_sq, 1)

                def exp(c):
                    ns = (c % ST + 1) * P
                    act.wait_ge(mt_ready, c + 1)
                    on(lg_m[:, c % 3, 0:ns], lg_m[:, c % 3, 0:ns], ACT.Exp, bias=small[:, 8 + c % 3:9 + c % 3],
                       accum_out=small[:, 16 + c % 3:17 + c % 3]).then_inc(mt_exp, 1)

                def output(h):
                    b = 64 * (h % 2)
                    act.wait_ge(mt_o, h + 1)
                    on(oT[b:b + 64, h // 2, :], bank[(h // 2) % 2][b:b + 64, 0:S], COPY).then_inc(mt_out, 1)

                exp(0)
                exp(1)
                for c in range(MH * ST):
                    h, qt = divmod(c, ST)
                    act.wait_ge(mt_t, c + 1)
                    pt = pT_m[:, h % 2, :].rearrange("p (k q) -> p k q", k=ST)
                    if qt == 0 and h >= 2:
                        act.wait_ge(mt_o, h - 1)
                    on(pt[:, 0:qt + 1, qt * P:(qt + 1) * P],
                       bank[6 + c % 2][:, 0:(qt + 1) * P].rearrange("p (k q) -> p k q", q=P), COPY).then_inc(mt_pt, 1)
                    if c + 2 < MH * ST:
                        exp(c + 2)
                    if qt == 0 and h:
                        output(h - 1)
                output(MH - 1)

            def dil_act(round_, m):
                act.wait_ge(turned, 4 * (m + 1))
                act.wait_ge(h_dve, 2 * m + 2)
                act.wait_ge(h_act, 2 * m + 2)
                on(hd_hi, hT[:, :, :], COPY).then_inc(hd_hi_out, 1)

                def split(u):
                    r, s = divmod(MOD_UNITS + u, SLOTS)
                    act.wait_ge(ring_full[s], (round_ + r + 1) * FULL)
                    for h in range(2):
                        w, _, hi = dil_half(u, h)
                        on(hi, w, COPY).then_inc(wd_hi_out, 1)

                mid = 0
                C = OCT * ST
                for o in range(2):
                    t = 0
                    split(3 * DG * o)
                    split(3 * DG * o + 1)
                    for u in range(3 * DG):
                        g, kind = divmod(u, 3)
                        tiles = 2 if kind == 2 else 4
                        for q in range(tiles):
                            if q == tiles - 1:
                                act.wait_ge(units_done, freed(round_, MOD_UNITS + 9 * o + u))
                            else:
                                mid += 1
                                act.wait_ge(dx_done, mid)
                            dst = dv[:, g, q, :] if kind == 2 else (dq, dk)[kind][:, g, q, :]
                            on(dst, bank[t % 4][:, 0:HALF if kind == 2 else S], COPY).then_inc(dx_out, 1)
                            t += 1
                        if u + 2 < 3 * DG:
                            split(3 * DG * o + u + 2)

                    def exp(c):
                        ns = (c % ST + 1) * P * DG
                        act.wait_ge(dt_ready, C * o + c + 1)
                        b = (C * o + c) % 3
                        on(lg_d[:, b, 0:ns], lg_d[:, b, 0:ns], ACT.Exp, bias=small[:, 8 + b:9 + b],
                           accum_out=small[:, 16 + b:17 + b]).then_inc(dt_exp, 1)

                    def output(h):
                        b = 64 * (h % 2)
                        act.wait_ge(dt_o, OCT * o + h + 1)
                        on(oT[b:b + 64, 4 * o + h // 2, :], bank[0][b:b + 64, 0:S], COPY).then_inc(dt_out, 1)

                    exp(0)
                    exp(1)
                    for c in range(C):
                        h, qt = divmod(c, ST)
                        act.wait_ge(dt_t, C * o + c + 1)
                        pt = pT_d[:, h % 2, :].rearrange("p (g k q) -> p g k q", g=DG, k=ST)
                        if qt == 0 and OCT * o + h >= 2:
                            act.wait_ge(dt_o, OCT * o + h - 1)
                        if qt == 0:
                            ins = on(pt[:, :, 0, 0:P], bank[1][:, 0:DG * P].rearrange("p (g q) -> p g q", q=P), COPY)
                        else:
                            for g in range(DG):
                                ins = on(pt[:, g, :, P:S], bank[2 + g // 2][:, (g % 2) * S:(g % 2) * S + S]
                                         .rearrange("p (k q) -> p k q", q=P), COPY)
                        ins.then_inc(dt_pt, 1)
                        if c + 2 < C:
                            exp(c + 2)
                        if qt == 0 and h:
                            output(h - 1)
                    output(OCT - 1)

            for n in subs2:
                i, j = divmod(n, N_SUB)
                r, m = START2[n], M2 + n
                pre2_act(n)
                mod_act(r, m, 0.0)
                if j != 1:
                    split_act(r, 0)
                turn_act(m, j != 1)
                if j != 1:
                    ffn_act(r, m, 2 * DEPTH + 2 * i + j // 2)
                elif i == 0:
                    mla_act(r)
                else:
                    dil_act(r, m)
                post2_act(n, freed(r, (23, 15, 23, 23, 27, 23)[n]))

        @block.vector
        def _(dve):
            V = nc.vector
            k = Links(dve, dve_link)
            MUL, ADD, SUBT = ALU.mult, ALU.add, ALU.subtract

            def split_dve(f, u, i=0):
                for h in range(2):
                    w, lo, hi = ffn_half(u, h)
                    dve.wait_ge(w_hi_out, halves(f, u, h) + 2 * SLOTS * i)
                    V.tensor_tensor(lo, w, hi.bitcast(F32), SUBT).then_inc(w_lo_out, 1)

            def turn_dve(m, blk, n=0, f=None):
                dve.wait_ge(mod_cols_done, m + 2)
                src = bank[1][:, 0:16].rearrange("p (c two h) -> p two h c", two=2, h=2)
                V.tensor_copy(mod_cols[:, 0, :].rearrange("p (h c) -> p h c", h=2), src[:, 0])
                ins = V.tensor_scalar(mod_cols[:, 1, :].rearrange("p (h c) -> p h c", h=2), src[:, 1], 1.0, None, ADD)
                if blk:
                    k.link(ins)
                    ins = V.tensor_tensor(mod_cols[:, 1, :], mod_cols[:, 1, :], pre_cols[:, n, :], MUL)
                ins.then_inc(mod_cols_out, 1)
                if f is not None:
                    split_dve(f, 0)
                dve.wait_ge(mod_cols_out, m + 1)
                for q in (1, 3):
                    dve.wait_ge(turned, 4 * m + q + 1)
                    for c in (2 * q, 2 * q + 1):
                        for dst in (hT,) if f is None else (hT, h_hi):
                            ins = V.tensor_scalar(dst[:, c, :], bank[4 + q][:, (c % 2) * S:(c % 2) * S + S],
                                                  mod_cols[:, 1, c:c + 1], mod_cols[:, 0, c:c + 1], MUL, ADD)
                    if f is None:
                        ins.then_inc(h_dve, 1)
                        continue
                    k.link(ins)
                    dve.wait_ge(h_act, 2 * m + q // 2 + 1)
                    c = slice(2 * q - 2, 2 * q + 2)
                    V.tensor_tensor(h_lo[:, c, :], hT[:, c, :], h_hi[:, c, :].bitcast(F32), SUBT).then_inc(h_dve, 1)

            def ffn_dve(f):
                split_dve(f, 1)

                def unit(u, i=0):
                    for t in (2 * u, 2 * u + 1):
                        at = bass.ds(2 * SLOTS * i + t, 1)
                        p = silu[:, t % 2:t % 2 + 1, :]
                        dve.wait_ge(silu_done, FT * f + 2 * SLOTS * i + t + 1)
                        k.link(V.tensor_tensor(p, p, bank[t % 4][:, S:2 * S].unsqueeze(1), MUL))
                        k.link(V.tensor_scalar(act_hi[:, at, :], p, 1.0, None, MUL))
                        V.tensor_tensor(act_lo[:, at, :], p, act_hi[:, at, :].bitcast(F32), SUBT).then_inc(tile_done, 1)
                    split_dve(f, u + 2, i)

                with k.loop(IN_UNITS // SLOTS, "ffn") as i:
                    for u in range(SLOTS):
                        unit(u, i)
                dve.wait_ge(tab_out, 64)
                for u in range(IN_UNITS // SLOTS * SLOTS, IN_UNITS):
                    unit(u)
                for u in range(IN_UNITS, FFN_UNITS - 2):
                    split_dve(f, u + 2)

            def post1_dve(m, after, res):
                dve.wait_ge(units_done, after)
                dve.wait_ge(gate_out, m + 1)
                for t in range(ST):
                    for h in range(2):
                        V.scalar_tensor_tensor(z[:, t, h * HALF:(h + 1) * HALF], bank[4 + 2 * t + h][:, :], res,
                                               gate[:, h * HALF:(h + 1) * HALF], MUL, MUL).then_inc(y_read, 1)
                dve.wait_ge(y_read, 4 * (m + 2))
                for t in range(ST):
                    k.link(V.scalar_tensor_tensor(z[:, t, :], x[:, t, :], ALPHA, z[:, t, :], MUL, ADD))
                    for h in range(2):
                        ins = V.bn_stats(stat[:, t, h, :], z[:, t, h * HALF:(h + 1) * HALF])
                    k.link(ins)
                    V.memset(carrier[:, :], 0.0)
                    k.link(V.bn_aggr(mv[:, t, :], stat[:, t, :, :]))
                    V.tensor_scalar(ms[:, t:t + 1], mv[:, t, 1:2], LN_EPS, None, ADD).then_inc(var_done, 1)
                for t in range(ST):
                    dve.wait_ge(inv_done, ST * m + t + 1)
                    V.scalar_tensor_tensor(nmr[:, t:t + 1], mv[:, t, 0:1], -1.0, rstd[:, t:t + 1], MUL, MUL).then_inc(nmr_done, 1)
                dve.wait_ge(post_in, 32 * (m + 1))
                for t in range(ST):
                    dve.wait_ge(norm_done, ST * m + t + 1)
                    k.link(V.tensor_tensor(z[:, t, :], z[:, t, :], post_g[:, :], MUL))
                    V.tensor_tensor(x[:, t, :], z[:, t, :], post_b[:, :], ADD).then_inc(rows_ready, 1)

            def mix_dve(round_, l):
                k.link(V.tensor_copy(oml_l[:, :], oml[:, bass.ds(l, 1), :].squeeze(1)))
                dve.wait_ge(px_out, NT * l + 2)
                s0, s1 = sums

                def double(dst, src, w, t0=0):
                    V.tensor_copy(dst[:, t0:2, 0:w], src[:, t0:2, 0:w])
                    k.link(V.tensor_tensor(dst[:, t0:2, w:S], src[:, t0:2, w:S], src[:, t0:2, 0:S - w], ADD))

                def mean(t, b, src):
                    p = slice(b, b + 64)
                    k.link(V.tensor_tensor(src[p, t, :], src[p, t, :], invcnt[p, t, :], MUL))
                    k.link(V.tensor_tensor(src[p, t, :], src[p, t, :], aT[p, t, :], SUBT))
                    return p, t, src

                dve.wait_ge(layer_in, 16 * 7 * (l + 1))
                double(s0, aT, 1)
                double(s1, s0, 2)
                done = [mean(0, 0, s0), mean(0, 64, s1)]
                double(s0, s1, 4, 1)
                double(s1, s0, 8, 1)
                done += [mean(1, 0, s0), mean(1, 64, s1)]
                for p, t, src in done:
                    ins = V.tensor_copy(aT[p, t, :], src[p, t, :])
                ins.then_inc(pool_d, 1)
                dve.wait_ge(px_out, NT * l + 15)
                for n in range(ST * IDX_H):
                    qt, h = divmod(n, IDX_H)
                    ns = (qt + 1) * P
                    dve.wait_ge(ix_relu, 16 * l + n + 1)
                    w = wi[:, qt, h:h + 1]
                    if h == 0:
                        ins = V.tensor_scalar(score[:, 0:ns], relu[:, n % 2, 0:ns], w, None, MUL)
                    else:
                        ins = V.scalar_tensor_tensor(score[:, 0:ns], relu[:, n % 2, 0:ns], w, score[:, 0:ns], MUL, ADD)
                    ins.then_inc(ix_used, 1)
                    dve.wait_ge(ix_used, 16 * l + n + 1)
                    if h == IDX_H - 1:
                        if qt:
                            V.tensor_scalar(score[:, 0:P], score[:, 0:P], IDX_SCALE, None, MUL)
                        k.link(V.scalar_tensor_tensor(score[:, qt * P:ns], score[:, qt * P:ns], IDX_SCALE, causal, MUL, ADD))
                        src = score
                        for r in range(TOP_K // 8):
                            V.memset(carrier[:, :], 0.0)
                            k.link(V.max(small[:, 32:40], src[:, 0:ns]))
                            V.memset(carrier[:, :], 0.0)
                            k.link(V.match_replace(work[:, 0:ns], small[:, 32:40], src[:, 0:ns], PICKED))
                            src = work
                        k.link(V.tensor_scalar(addm[:, qt, 0:ns], work[:, 0:ns], PICKED / 2, MASKED, ALU.is_gt, MUL))

                dve.wait_ge(table_in, 16)

                def logits(c):
                    h, qt = divmod(c, ST)
                    ns = (qt + 1) * P
                    dve.wait_ge(at_s, 8 * l + c + 1)
                    if c >= 3:
                        dve.wait_ge(at_t, 8 * l + c - 2)
                    out_ = lg[:, c % 3, 0:ns]
                    V.scalar_tensor_tensor(out_, bank[4 + c % 2][:, 0:ns], 64 ** -0.5, table1[:, h, S - ns:S], MUL, ADD)\
                     .then_inc(at_read, 1)
                    dve.wait_ge(at_read, 8 * l + c + 1)
                    k.link(V.tensor_tensor(out_, out_, addm[:, qt, 0:ns], ADD))
                    k.link(V.reduce_max(small[:, c % 3:c % 3 + 1], out_, axis=AXX))
                    V.tensor_scalar(small[:, 8 + c % 3:9 + c % 3], small[:, c % 3:c % 3 + 1], -1.0, None, MUL).then_inc(at_ready, 1)

                def probs(c):
                    ns = (c % ST + 1) * P
                    dve.wait_ge(at_exp, 8 * l + c + 1)
                    k.link(V.reciprocal(small[:, 24 + c % 3:25 + c % 3], small[:, 16 + c % 3:17 + c % 3]))
                    V.tensor_scalar(lg[:, c % 3, 0:ns], lg[:, c % 3, 0:ns], small[:, 24 + c % 3:25 + c % 3], None, MUL)\
                     .then_inc(at_p, 1)

                logits(0)
                logits(1)
                for c in range(AH * ST):
                    probs(c)
                    if c + 2 < AH * ST:
                        logits(c + 2)
                dve.wait_ge(px_out, NT * l + 29)
                for h in range(HH):
                    ins = V.tensor_scalar(key[:, h, :], key[:, h, :], oml_l[:, h:h + 1], None, MUL)
                k.link(ins)
                k.link(V.tensor_scalar(ff[:, :, :], key[:, :, :], KEY_MAX, -1.0, ALU.min, MUL))
                V.tensor_scalar(ff[:, :, :], ff[:, :, :], 1.0, None, ADD).then_inc(h_f, 1)
                dve.wait_ge(h_f, l + 1)
                dve.wait_ge(at_o, AH * (l + 1))
                dve.wait_ge(pool_done, l + 1)

                def blocks(t, lo, hi):
                    return t[:, :, :].rearrange("p h (b s) -> p (h b) s", s=SUB)[:, :, lo:hi]

                def band(dt):
                    g = (gb0, gb1)[dt % 2]
                    if dt >= 2:
                        dve.wait_ge(band_mm, 2 * (SUB * l + dt - 1))
                    if dt == 0:
                        V.tensor_copy(qb[:, :, :], hq[:, :, :])
                        ins = V.tensor_tensor(g[:, :, :], hq[:, :, :], key[:, :, :], MUL)
                    else:
                        k.link(V.tensor_tensor(blocks(qb, dt, SUB), blocks(qb, dt, SUB), blocks(ff, 1, SUB - dt + 1), MUL))
                        ins = V.tensor_tensor(blocks(g, dt, SUB), blocks(qb, dt, SUB), blocks(key, 0, SUB - dt), MUL)
                    ins.then_inc(band_g, 1)

                band(0)
                dve.wait_ge(vt_out, l + 1)
                for dt in range(SUB):
                    if dt + 1 < SUB:
                        dve.wait_ge(band_g, SUB * l + dt + 1)
                        band(dt + 1)
                    w = SUB - dt
                    for q in range(2):
                        dve.wait_ge(band_mm, 2 * (SUB * l + dt) + q + 1)
                        n = 2 * S // SUB
                        gs = bank[2 * (dt % 2) + q][:, 0:n * w].rearrange("p (b s) -> p b s", s=w)
                        dst = ob if dt == 0 else tm0
                        V.tensor_tensor(blocks(dst, 0, w)[:, q * n:(q + 1) * n], gs,
                                        blocks(vt, 0, w)[:, q * n:(q + 1) * n], MUL).then_inc(band_read, 1)
                    dve.wait_ge(band_read, 2 * (SUB * l + dt + 1))
                    if dt:
                        k.link(V.tensor_tensor(blocks(ob, dt, SUB), blocks(ob, dt, SUB), blocks(tm0, 0, w), ADD))

                dve.wait_ge(h_ln, l + 1)
                for h in range(HH):
                    V.tensor_tensor_scan(decay[:, h, :], cst("reset64"), aa[:, h, :], 0.0, MUL, ADD)
                    ins = V.tensor_tensor_scan(qd[:, h, :], cst("reset8"), aa[:, h, :], 0.0, MUL, ADD)
                k.link(ins)
                for kr in (kr0, kr1):
                    V.memset(kr[:, :, :], 0.0)
                V.memset(scoreT[:, :, :], 0.0)
                a_hc = decay[:, :, :].rearrange("p h (c s) -> p (h c) s", s=CHUNK)
                ins = V.tensor_copy(refs[:, :, 1:NSB + 1], a_hc[:, :, SUB - 1::SUB])
                ins.then_inc(h_scan, 1)
                dve.wait_ge(h_scan, l + 1)

                def kr_view(i):
                    return (kr0, kr1)[i % 2][:, :, :].rearrange("p h (c s) -> p (h c) s", s=CHUNK)[:, :, 0:SUB * i]

                def arg(i):
                    if i >= 3:
                        dve.wait_ge(kr_used, (NSB - 1) * l + i - 2)
                    V.tensor_tensor(kr_view(i), refs[:, :, i:i + 1].to_broadcast([P, HC, SUB * i]), a_hc[:, :, 0:SUB * i], SUBT)\
                     .then_inc(kr_arg, 1)

                arg(1)
                dve.wait_ge(h_ea, l + 1)
                V.tensor_tensor(qa[:, :, :], qa[:, :, :], hq[:, :, :], MUL)
                k.link(V.tensor_tensor(qd[:, :, :], qd[:, :, :], hq[:, :, :], MUL))
                key_hc = key[:, :, :].rearrange("p h (c s) -> p (h c) s", s=CHUNK)
                for i in range(1, NSB + 1):
                    if i < NSB:
                        arg(i + 1)
                    dve.wait_ge(kr_exp, NSB * l + i)
                    V.tensor_tensor(kr_view(i), kr_view(i), key_hc[:, :, 0:SUB * i], MUL).then_inc(kr_ready, 1)
                for c in range(NCH - 1):
                    dve.wait_ge(ds_done, (NCH - 1) * l + c + 1)
                    b = bank[(5, 0, 1)[c]]
                    if c == 0:
                        ins = V.tensor_copy(states[:, 0, :, :], b[:, :].rearrange("p (h v) -> p h v", h=HH))
                    else:
                        for h in range(HH):
                            ins = V.scalar_tensor_tensor(states[:, c, h, :], states[:, c - 1, h, :],
                                                         eal[:, h * NCH + c:h * NCH + c + 1], b[:, h * P:(h + 1) * P], MUL, ADD)
                    ins.then_inc(st_ready, 1)
                    dve.wait_ge(st_ready, (NCH - 1) * l + c + 1)
                dve.wait_ge(ho_done, l + 1)
                for q in range(2):
                    ins = V.tensor_tensor(ob[:, 2 * q:2 * q + 2, :], ob[:, 2 * q:2 * q + 2, :],
                                          bank[6 + q][:, :].rearrange("p (h s) -> p h s", h=2), ADD)
                ins.then_inc(ho_sum, 1)
                dve.wait_ge(ho_ss, l + 1)
                V.tensor_scalar(ms[:, 0:8], bank[2][:, 0:8], 1.0 / P, RMS_EPS, MUL, ADD).then_inc(ho_ms, 1)
                dve.wait_ge(ho_inv, l + 1)
                for h in range(HH):
                    for t in range(ST):
                        ins = V.tensor_scalar(tm1[:, h, t * P:(t + 1) * P], ident, rs[:, h * ST + t:h * ST + t + 1], None, MUL)
                ins.then_inc(ho_diag, 1)
                dve.wait_ge(ho_rep, l + 1)
                dve.wait_ge(ho_sum, l + 1)
                for q in range(2):
                    ins = V.tensor_tensor(ob[:, 2 * q:2 * q + 2, :], ob[:, 2 * q:2 * q + 2, :],
                                          bank[q][:, :].rearrange("p (h s) -> p h s", h=2), MUL)
                k.link(ins)
                for h in range(HH):
                    ins = V.scalar_tensor_tensor(y[:, 4 + h, :], ob[:, h, :], layer_cols[:, 2 + h:3 + h], sg[:, h, :], MUL, MUL)
                ins.then_inc(yc_out, 1)
                dve.wait_ge(gates_out, l + 1)
                for t in range(DC):
                    if t % 4 == 3:
                        dve.wait_ge(units_done, freed(round_, 20 + t // 4))
                    else:
                        dve.wait_ge(br_done, 6 * l + t - t // 4 + 1)
                    b = 2 * (t % 2)
                    V.tensor_tensor(tm0[:, 0, :], gates[:, t, :], bank[b][:, 0:S], MUL)
                    V.tensor_tensor(tm0[:, 1, :], gates[:, DC + t, :], bank[b][:, S:2 * S], MUL)
                    k.link(V.tensor_tensor(tm0[:, 2, :], gates[:, 2 * DC + t, :], bank[b + 1][:, 0:S], MUL))
                    k.link(V.tensor_tensor(tm0[:, 0, :], tm0[:, 0, :], tm0[:, 1, :], ADD))
                    V.tensor_tensor(hT[:, t, :], tm0[:, 0, :], tm0[:, 2, :], ADD).then_inc(merged, 1)
                    dve.wait_ge(merged, DC * l + t + 1)

            dve.wait_ge(start_in, 16 * START_DMAS)
            dve.wait_ge(zeroed, 1)
            mx, e0, e1 = lb_tmp[:, 0, :], lb_tmp[:, 1, :], lb_tmp[:, 2, :]
            k.link(V.tensor_tensor(mx, lb_cols[:, 0, :], lb_cols[:, 1, :], ALU.max))
            V.tensor_tensor(e0, lb_cols[:, 0, :], mx, SUBT)
            V.tensor_tensor(e1, lb_cols[:, 1, :], mx, SUBT).then_inc(lb_arg, 1)
            dve.wait_ge(lb_exp, 1)
            k.link(V.tensor_tensor(mx, e0, e1, ADD))
            k.link(V.reciprocal(mx, mx))
            k.link(V.tensor_tensor(e1, e1, mx, MUL))
            k.link(V.tensor_scalar(oml[:, 1, :], e1, -1.0, 1.0, MUL, ADD))
            V.memset(oml[:, 0, :], 1.0)
            dve.wait_ge(start_act, 1)
            V.tensor_copy(cond_row[:, :, :, 0:1], cond[:, :, :].unsqueeze(3))
            V.tensor_copy(cond_all[:, :, :], cond[:, 0, :].unsqueeze(2).to_broadcast([P, DC, P])).then_inc(start_dve, 1)
            dve.wait_ge(x_in, 16)
            for t in range(ST):
                V.tensor_copy(x[:, t, :], z[:, t, :]).then_inc(rows_ready, 1)
            with k.loop(layers, "dve1") as l:
                for j in subs:
                    r, m = l * LAYER1 + START1[j], sub1(l, j)
                    turn_dve(m, 0, f=None if j == 1 else 2 * l + j // 2)
                    if j == 1:
                        mix_dve(r, l)
                        post1_dve(m, freed(r, 23), 1.0)
                    else:
                        ffn_dve(2 * l + j // 2)
                        post1_dve(m, freed(r, 23), 0.5)

            V1 = ST * M2

            def pre2_dve(n):
                for t in range(ST):
                    dve.wait_ge(sq_done, 6 * n + t + 1)
                    V.tensor_scalar(ms[:, t:t + 1], sq[:, t, 0:1], 1.0 / D, RMS_EPS, MUL, ADD).then_inc(var_done, 1)

            def post2_dve(n, m, res):
                for t in range(ST):
                    dve.wait_ge(sq_done, 6 * n + 4 + 2 * t)
                    k.link(V.tensor_tensor(ms[:, t:t + 1], sq[:, t, 0:1], sq[:, t, 1:2], ADD))
                    V.tensor_scalar(ms[:, t:t + 1], ms[:, t:t + 1], 1.0 / D, RMS_EPS, MUL, ADD).then_inc(var_done, 1)
                dve.wait_ge(gate2_out, n + 1)
                for t in range(ST):
                    dve.wait_ge(inv_done, V1 + 4 * n + 2 + t + 1)
                    k.link(V.tensor_scalar(nmr[:, t:t + 1], rstd[:, t:t + 1], res, None, MUL))
                    for h in range(2):
                        V.scalar_tensor_tensor(z[:, t, h * HALF:(h + 1) * HALF], bank[4 + 2 * t + h][:, :], nmr[:, t:t + 1],
                                               gate[:, h * HALF:(h + 1) * HALF], MUL, MUL).then_inc(y_read, 1)
                    dve.wait_ge(y_read, 4 * (m + 1) + 2 * t + 2)
                    V.tensor_tensor(x[:, t, :], x[:, t, :], z[:, t, :], ADD).then_inc(rows_ready, 1)

            def mla_dve():
                V.memset(mask2[:, 0:P], 0.0)
                k.link(V.tensor_copy(mask2[:, P:S], causal))
                dve.wait_ge(ml_ss, 1)
                V.tensor_scalar(ms[:, 0:2], bank[4][:, 0:2], 1.0 / Q_LORA, RMS_EPS, MUL, ADD)
                V.tensor_scalar(ms[:, 2:4], bank[4][:, 2:4], 1.0 / KV_LORA, RMS_EPS, MUL, ADD).then_inc(ml_ms, 1)
                dve.wait_ge(ml_inv, 1)
                for g in range(4):
                    ins = V.tensor_scalar(inv_diag[:, g // 2, (g % 2) * P:(g % 2 + 1) * P], ident, rs[:, g:g + 1], None, MUL)
                ins.then_inc(ml_diag, 1)
                dve.wait_ge(ml_rep, 1)
                for c in range(5):
                    t, g = (cq[:, c, :], 0) if c < 3 else (ck[:, c - 3, :], 1)
                    ins = V.scalar_tensor_tensor(t, t, mla_cols[:, c:c + 1], bank[5][:, g * S:(g + 1) * S], MUL, MUL)
                ins.then_inc(ml_norm, 1)
                dve.wait_ge(ml_const, 16)
                for t in range(5):
                    dve.wait_ge(rot_done, t + 1)
                    v = kr if t == 4 else qr[:, t, :]
                    V.tensor_tensor(rot, bank[t % 4][:, 0:S], sin_t, MUL)
                    k.link(V.tensor_tensor(v, v, cos_t, MUL))
                    V.tensor_tensor(v, v, rot, ADD).then_inc(rot_out, 1)
                    dve.wait_ge(rot_out, t + 1)

                def logits(c):
                    ns = (c % ST + 1) * P
                    dve.wait_ge(mt_s, c + 1)
                    if c >= 3:
                        dve.wait_ge(mt_t, c - 2)
                    V.scalar_tensor_tensor(lg_m[:, c % 3, 0:ns], bank[4 + c % 2][:, 0:ns], (NOPE + ROPE) ** -0.5,
                                           mask2[:, S - ns:S], MUL, ADD).then_inc(mt_read, 1)
                    dve.wait_ge(mt_read, c + 1)
                    k.link(V.reduce_max(small[:, c % 3:c % 3 + 1], lg_m[:, c % 3, 0:ns], axis=AXX))
                    V.tensor_scalar(small[:, 8 + c % 3:9 + c % 3], small[:, c % 3:c % 3 + 1], -1.0, None, MUL).then_inc(mt_ready, 1)

                logits(0)
                logits(1)
                for c in range(MH * ST):
                    ns = (c % ST + 1) * P
                    dve.wait_ge(mt_exp, c + 1)
                    k.link(V.reciprocal(small[:, 24 + c % 3:25 + c % 3], small[:, 16 + c % 3:17 + c % 3]))
                    V.tensor_scalar(lg_m[:, c % 3, 0:ns], lg_m[:, c % 3, 0:ns], small[:, 24 + c % 3:25 + c % 3], None, MUL)\
                     .then_inc(mt_p, 1)
                    if c + 2 < MH * ST:
                        logits(c + 2)

            def dil_dve():
                C = OCT * ST

                def split(o):
                    for u in range(3 * DG * o, 3 * DG * (o + 1)):
                        for h in range(2):
                            w, lo, hi = dil_half(u, h)
                            dve.wait_ge(wd_hi_out, 2 * u + h + 1)
                            V.tensor_tensor(lo, w, hi.bitcast(F32), SUBT).then_inc(wd_lo_out, 1)

                dve.wait_ge(hd_hi_out, 1)
                V.tensor_tensor(h_lo[:, :, :], hT[:, :, :], hd_hi.bitcast(F32), SUBT).then_inc(hd_lo_out, 1)

                def logits(n):
                    c = n % C
                    h, qt = divmod(c, ST)
                    ns = (qt + 1) * P
                    dve.wait_ge(dt_s, n + 1)
                    if n >= 3:
                        dve.wait_ge(dt_t, n - 2)
                    if qt == 0:
                        dve.wait_ge(tabs_in[h % 2], 16 * (n // ST // 2 + 1))
                    lgv = lg_d[:, n % 3, 0:DG * ns].rearrange("p (g s) -> p g s", g=DG)
                    tb = tabs[:, h % 2, :, S - ns:S]
                    b = 4 + 2 * (c % 2)
                    if qt == 0:
                        ins = V.scalar_tensor_tensor(lgv, bank[b][:, 0:DG * P].rearrange("p (g s) -> p g s", g=DG), 64 ** -0.5, tb, MUL, ADD)
                    else:
                        V.scalar_tensor_tensor(lgv[:, 0:2, :], bank[b][:, :].rearrange("p (g s) -> p g s", g=2), 64 ** -0.5,
                                               tb[:, 0:2, :], MUL, ADD)
                        ins = V.scalar_tensor_tensor(lgv[:, 2, :], bank[b + 1][:, 0:S], 64 ** -0.5, tb[:, 2, :], MUL, ADD)
                    ins.then_inc(dt_read, 1)
                    dve.wait_ge(dt_read, n + 1)
                    ins = V.reduce_max(small[:, n % 3:n % 3 + 1], lg_d[:, n % 3, 0:DG * ns], axis=AXX)
                    k.link(ins)
                    ins = V.tensor_scalar(small[:, 8 + n % 3:9 + n % 3], small[:, n % 3:n % 3 + 1], -1.0, None, MUL)
                    ins.then_inc(dt_ready, 1)

                for n in range(2 * C):
                    c = n % C
                    ns = (c % ST + 1) * P * DG
                    if c == 0:
                        split(n // C)
                        logits(n)
                        logits(n + 1)
                    dve.wait_ge(dt_exp, n + 1)
                    k.link(V.reciprocal(small[:, 24 + n % 3:25 + n % 3], small[:, 16 + n % 3:17 + n % 3]))
                    V.tensor_scalar(lg_d[:, n % 3, 0:ns], lg_d[:, n % 3, 0:ns], small[:, 24 + n % 3:25 + n % 3], None, MUL)\
                     .then_inc(dt_p, 1)
                    if c + 2 < C:
                        logits(n + 2)

            dve.wait_ge(units_done, freed(START2[0] - FFN_ROUNDS, MOD_UNITS - 1))
            V.tensor_copy(cond_all[:, :, :], cond[:, 1, :].unsqueeze(2).to_broadcast([P, DC, P])).then_inc(start_dve, 1)
            for n in subs2:
                i, j = divmod(n, N_SUB)
                m = M2 + n
                pre2_dve(n)
                turn_dve(m, 1, n, None if j == 1 else 2 * DEPTH + 2 * i + j // 2)
                if j != 1:
                    ffn_dve(2 * DEPTH + 2 * i + j // 2)
                elif i == 0:
                    mla_dve()
                else:
                    dil_dve()
                post2_dve(n, m, (0.5, 1.0, 0.5)[j])

        @block.gpsimd
        def _(pool):
            G = nc.gpsimd

            def rows_in(m, *vectors):
                pool.wait_ge(rows_ready, ST * (m + 1))
                for dst, src in vectors:
                    pool.dma_start(dst, src.unsqueeze(0).to_broadcast([P, D])).then_inc(post_in, 16)

            def invert(done, at, out_, n=1):
                pool.wait_ge(var_done, at)
                G.tensor_tensor(out_, ms[:, 0:n], neg_half[:, 0:n], ALU.pow).then_inc(done, 1)

            def post1_pool(m):
                for t in range(ST):
                    pool.wait_ge(var_done, ST * m + t + 1)
                    G.tensor_tensor(rstd[:, t:t + 1], ms[:, t:t + 1], neg_half[:, 0:1], ALU.pow).then_inc(inv_done, 1)

            pk = Links(pool, pool_link)
            pk.link(G.memset(cond_row[:, :, :, :], 0.0))
            pk.link(G.memset(pool_bd[:, :, :], 0.0))
            pk.link(G.memset(bias_rows[:, :], 0.0))
            pk.link(G.memset(neg_half[:, :], -0.5))
            pk.link(G.memset(rb1[32:33, :], MASKED))
            pk.link(G.memset(rb2[32:33, :], MASKED))
            G.memset(sq[:, :, :], 0.0).then_inc(units_done, SLOTS)
            pool.wait_ge(units_done, SLOTS)
            for s, first in ((tile_done, 4), (y_read, 4), (mod_cols_done, 1), (bias_used, MOD_UNITS)):
                G.memset(nmr[:, :], 0.0).then_inc(s, first)
                pool.wait_ge(s, first)
            G.memset(lb_tmp[:, :, :], 0.0).then_inc(zeroed, 1)
            pool.wait_ge(zeroed, 1)

            pool.dma_start(z[:, :, :], a["x"][0].rearrange("(t p) d -> p t d", p=P)).then_inc(x_in, 16)
            pool.dma_start(const[:, :], a["const"][:, 0:KEPT_COLS]).then_inc(const_in, 16)
            loads = [(c_cols[:, 0, :], a["c"][0].rearrange("(kc p) -> p kc", p=P)),
                     (c_cols[:, 1, :], a["c_2"][0].rearrange("(kc p) -> p kc", p=P)),
                     (pick, a["pick"]),
                     (rb1[0:32, :], a["rel_bias"]),
                     (rb2[0:32, :], a["rel_bias_2"])]
            for l in range(DEPTH):
                loads.append((lb_cols[:, l, :], a["hgrn_lb"][l].rearrange("(h p) -> p h", p=P)))
            for i in range(DEPTH * N_SUB):
                loads.append((pre_cols[:, i, :], a["norm_pre_2"][i // N_SUB, i % N_SUB].rearrange("(c p) -> p c", p=P)))
            loads.append((mla_cols[:, 0:3], a["mla_q_norm_2"][0].rearrange("(c p) -> p c", p=P)))
            loads.append((mla_cols[:, 3:5], a["mla_kv_norm_2"][0].rearrange("(c p) -> p c", p=P)))
            assert len(loads) == START_DMAS
            for dst, src in loads:
                pool.dma_start(dst, src, allow_slow_non_contiguous=True).then_inc(start_in, 16)
            pool.wait_ge(start_act, 2)
            for row, n, g in ((0, AH, 0), (AH, DH, 1), (AH + DH, DH, 2), (AH + 2 * DH, DH, 3)):
                pool.dma_start(bias_tab[row:row + n], tab[0:n, g, :].unsqueeze(1).to_broadcast([n, P, TAB])).then_inc(tab_out, 16)
            pool.wait_ge(tab_out, 64)
            pool.dma_start(table1[:, :, :], table_src(0, AH)).then_inc(table_in, 16)
            with pool.Fori(0, layers) as l:
                for j in subs:
                    r, m = l * LAYER1 + START1[j], sub1(l, j)
                    rows_in(m, (post_g[:, :], a["ln_g"][l, j]), (post_b[:, :], a["ln_b"][l, j]))
                    if j == 1:
                        pool.dma_start(invcnt, a["const"][:, CONST["invcnt"][0]:CONST["invcnt"][1]]
                                       .rearrange("p (t s) -> p t s", t=ST)).then_inc(layer_in, 16)
                        for g in range(POOL_GROUPS):
                            b = 64 * (g % 2)
                            pool.dma_start(pool_bd[b:b + 64, g // 2, b:b + 64], a["pool_w"][l, g]).then_inc(layer_in, 16)
                        pool.dma_start(layer_cols[:, 0:2], a["pool_scale"][l].rearrange("(c p) -> p c", p=P),
                                       allow_slow_non_contiguous=True).then_inc(layer_in, 16)
                        pool.dma_start(layer_cols[:, 2:6], a["hgrn_norm_g"][l].rearrange("(c p) -> p c", p=P),
                                       allow_slow_non_contiguous=True).then_inc(layer_in, 16)
                        pool.wait_ge(ho_ms, l + 1)
                        G.tensor_tensor(rs[:, 0:8], ms[:, 0:8], neg_half[:, 0:8], ALU.pow).then_inc(ho_inv, 1)
                    post1_pool(m)

            V1, POST1 = ST * M2, 32 * M2
            for n in subs2:
                i, j = divmod(n, N_SUB)
                r, m = START2[n], M2 + n
                rows_in(m, (post_g[:, :], a["norm_post_2"][i, j]))
                if n == 1:
                    pool.dma_start(mla_const, a["const"][:, CONST["swap"][0]:]).then_inc(ml_const, 16)
                for t in range(ST):
                    pool.wait_ge(var_done, V1 + 4 * n + t + 1)
                    G.tensor_tensor(rstd[:, t:t + 1], ms[:, t:t + 1], neg_half[:, 0:1], ALU.pow).then_inc(inv_done, 1)
                if n == 4:
                    for h in range(DH):
                        if h >= 2:
                            pool.wait_ge(dt_read, ST * (h - 1))
                        else:
                            pool.wait_ge(h_act, 2 * m + 2)
                        src = bass.AP(bias_tab.tensor, (AH + h) * (P * TAB) + P - 1,
                                      [[TAB - 1, P], [DH * P * TAB, DG], [1, S]])
                        pool.dma_start(tabs[:, h % 2, :, :], src).then_inc(tabs_in[h % 2], 16)
                if n == 1:
                    pool.wait_ge(ml_ms, 1)
                    G.tensor_tensor(rs[:, 0:4], ms[:, 0:4], neg_half[:, 0:4], ALU.pow).then_inc(ml_inv, 1)
                pool.wait_ge(gate_out, m + 1)
                pool.wait_ge(post_in, POST1 + 16 * (n + 1))
                G.tensor_tensor(gate[:, :], gate[:, :], post_g[:, :], ALU.mult).then_inc(gate2_out, 1)
                for t in range(ST):
                    pool.wait_ge(var_done, V1 + 4 * n + 2 + t + 1)
                    G.tensor_tensor(rstd[:, t:t + 1], ms[:, t:t + 1], neg_half[:, 0:1], ALU.pow).then_inc(inv_done, 1)

    return nc


_INS = ["x", "c", "w_ada", "b_ada", "ln_g", "ln_b", "ffn_w_in", "ffn_w_out", "mix_w_in", "pool_w", "pool_scale",
        "rel_bias", "hgrn_lb", "hgrn_norm_g", "w_branch", "w_out", "c_2", "norm_pre_2", "norm_post_2", "w_mod_2",
        "b_mod_2", "ffn_w_gate_2", "ffn_w_up_2", "ffn_w_down_2", "mla_w_in_2", "mla_q_norm_2", "mla_w_q_up_2",
        "mla_kv_norm_2", "mla_w_kv_up_2", "mla_w_o_2", "dil_w_in_2", "dil_w_o_2", "rel_bias_2"]


def kernel(**inputs):
    from concourse import bacc
    from concourse.bass_utils import run_bass_kernel_spmd

    nc = bacc.Bacc("TRN2", target_bir_lowering=False, num_devices=1)
    arrays = {f"in_{name}": np.ascontiguousarray(inputs[name]) for name in _INS}
    arrays["in_const"], arrays["in_pick"] = constants(), picks()
    args = {name[3:]: nc.dram_tensor(name, v.shape, F32, kind="ExternalInput").ap() for name, v in arrays.items()}
    out = nc.dram_tensor("out_0", (1, S, D), F32, kind="ExternalOutput").ap()
    build(nc, args, out)
    result = run_bass_kernel_spmd(nc, [arrays], core_ids=[0])
    return result.results[0]["out_0"]
```
